# Optimizing a Trainium2 kernel written in Bass

```python
import jax
import jax.numpy as jnp
from jax import lax
import numpy as np

D_MODEL = 1024
BATCH = 1
SEQ = 128
DEPTH = 1
DEC_BATCH = 1
DEC_SEQ = 512
PAST_LEN = 128

GRID_W = 64
D_MIX = D_MODEL
C_CONV = D_MIX // 2
CONV_K = 31
N_HEADS = 4
D_NOPE = 128
D_ROPE = 64
D_V = 128
D_ATT = N_HEADS * D_V
Q_LORA = 384
KV_LORA = 256
IN_COLS = 2 * C_CONV + Q_LORA + KV_LORA + D_ROPE
SPLITS = (2 * C_CONV, 2 * C_CONV + Q_LORA, 2 * C_CONV + Q_LORA + KV_LORA)
N_GROUPS = 4
E_PER_GROUP = 8
N_EXPERTS = N_GROUPS * E_PER_GROUP
TOP_K = 2
D_EXPERT = 256
ROPE_BASE = 10000.0
EPS = 1e-6
Q_BLOCK = 128
ATT_SCALE = (D_NOPE + D_ROPE) ** -0.5

kernel_name = "hymba_conformer_mla_hiermoe_diffusion_step"

def _rmsnorm(x, g):
    xf = x.astype(jnp.float32)
    y = xf * lax.rsqrt(jnp.mean(xf * xf, axis=-1, keepdims=True) + EPS)
    return (y * g.astype(jnp.float32)).astype(x.dtype)

def _layernorm(x, g, b):
    xf = x.astype(jnp.float32)
    mu = jnp.mean(xf, axis=-1, keepdims=True)
    var = jnp.mean(jnp.square(xf - mu), axis=-1, keepdims=True)
    y = (xf - mu) * lax.rsqrt(var + EPS)
    return (y * g.astype(jnp.float32) + b.astype(jnp.float32)).astype(x.dtype)

def _adaln(cvec, w_ada, b_ada):
    m = jax.nn.silu(cvec) @ w_ada + b_ada
    return tuple(t[:, None, :] for t in jnp.split(m, 6, axis=-1))

def _modulate(x, g, shift, scale):
    return _rmsnorm(x, g) * (1.0 + scale) + shift

def _axial_tables(rows):
    row = jnp.repeat(jnp.arange(rows, dtype=jnp.float32), GRID_W)
    col = jnp.tile(jnp.arange(GRID_W, dtype=jnp.float32), rows)
    n_freq = D_ROPE // 4
    freqs = ROPE_BASE ** (-jnp.arange(n_freq, dtype=jnp.float32) / n_freq)
    ang_r = (row[:, None] * freqs)[:, None, :]
    ang_c = (col[:, None] * freqs)[:, None, :]
    return (jnp.cos(ang_r), jnp.sin(ang_r), jnp.cos(ang_c), jnp.sin(ang_c))

def _rot_half(x, cos, sin):
    x1, x2 = jnp.split(x, 2, axis=-1)
    cos = cos.astype(x.dtype)
    sin = sin.astype(x.dtype)
    return jnp.concatenate([x1 * cos - x2 * sin, x2 * cos + x1 * sin], axis=-1)

def _rope2d(x, tabs):
    cos_r, sin_r, cos_c, sin_c = tabs
    xr, xc = jnp.split(x, 2, axis=-1)
    return jnp.concatenate([_rot_half(xr, cos_r, sin_r), _rot_half(xc, cos_c, sin_c)], axis=-1)

def _conformer_conv(u, w_dw, b_dw, ln_g, ln_b):
    a, g = jnp.split(u, 2, axis=-1)
    h = a * jax.nn.sigmoid(g)
    h = lax.conv_general_dilated(
        h, w_dw[:, None, :].astype(h.dtype), window_strides=(1,),
        padding=[(CONV_K // 2, CONV_K // 2)],
        dimension_numbers=("NWC", "WIO", "NWC"), feature_group_count=C_CONV)
    h = h + b_dw
    return jax.nn.silu(_layernorm(h, ln_g, ln_b))

def _mla_queries(u_q, q_norm_g, w_uq):
    b, t, _ = u_q.shape
    q = (_rmsnorm(u_q, q_norm_g) @ w_uq).reshape(b, t, N_HEADS, D_NOPE + D_ROPE)
    return q[..., :D_NOPE], q[..., D_NOPE:]

def _mla_decompress(ckv, w_ukv):
    b, s, _ = ckv.shape
    kv = (ckv @ w_ukv).reshape(b, s, N_HEADS, D_NOPE + D_V)
    return kv[..., :D_NOPE], kv[..., D_NOPE:]

def _mla_attend(q_nope, q_rope, k_nope, k_rope, v):
    b, t = q_nope.shape[0], q_nope.shape[1]
    nb = t // Q_BLOCK
    qn = q_nope.reshape(b, nb, Q_BLOCK, N_HEADS, D_NOPE).transpose(1, 0, 2, 3, 4)
    qr = q_rope.reshape(b, nb, Q_BLOCK, N_HEADS, D_ROPE).transpose(1, 0, 2, 3, 4)

    def block(args):
        qn_b, qr_b = args
        s = (jnp.einsum('bqhd,bkhd->bhqk', qn_b, k_nope)
             + jnp.einsum('bqhr,bkr->bhqk', qr_b, k_rope))
        p = jax.nn.softmax(s.astype(jnp.float32) * ATT_SCALE, axis=-1).astype(v.dtype)
        return jnp.einsum('bhqk,bkhd->bqhd', p, v)

    o = lax.map(block, (qn, qr))
    return o.transpose(1, 0, 2, 3, 4).reshape(b, t, D_ATT)

def _token_mix(h, w_in, w_dw, b_dw, ln_g, ln_b, q_norm_g, kv_norm_g, w_uq, w_ukv, w_out,
               tabs, ctx_ckv, ctx_krope):
    u = h @ w_in
    u_conv, u_q, u_kv, u_kr = jnp.split(u, SPLITS, axis=-1)
    conv_out = _conformer_conv(u_conv, w_dw, b_dw, ln_g, ln_b)
    q_nope, q_rope = _mla_queries(u_q, q_norm_g, w_uq)
    ckv = _rmsnorm(u_kv, kv_norm_g)
    k_rope = u_kr
    if tabs is None:
        ckv_keys, kr_keys = ckv, k_rope
    else:
        q_rope = _rope2d(q_rope, tabs)
        k_rope = _rope2d(k_rope[:, :, None, :], tabs)[:, :, 0]
        ckv_keys = jnp.concatenate([ctx_ckv.astype(ckv.dtype), ckv], axis=1)
        kr_keys = jnp.concatenate([ctx_krope.astype(k_rope.dtype), k_rope], axis=1)
    k_nope, v = _mla_decompress(ckv_keys, w_ukv)
    att = _mla_attend(q_nope, q_rope, k_nope, kr_keys, v)
    out = jnp.concatenate([conv_out, att], axis=-1) @ w_out
    return out, ckv, k_rope

def _hier_moe(h, w_rg, b_rg, w_re, b_re, w_gate, w_up, w_down):
    b, t, d = h.shape
    xt = h.reshape(-1, d)
    g_prob = jax.nn.softmax((xt @ w_rg).astype(jnp.float32) + b_rg.astype(jnp.float32), axis=-1)
    g_top, g_idx = lax.top_k(g_prob, 1)
    e_logits = ((xt @ w_re).astype(jnp.float32) + b_re.astype(jnp.float32)).reshape(-1, N_GROUPS, E_PER_GROUP)
    e_sel = jnp.take_along_axis(e_logits, g_idx[:, :, None], axis=1)[:, 0]
    e_top, e_idx = lax.top_k(jax.nn.softmax(e_sel, axis=-1), TOP_K)
    e_w = e_top / jnp.sum(e_top, axis=-1, keepdims=True) * g_top
    expert_id = g_idx * E_PER_GROUP + e_idx
    gates = jnp.sum(jax.nn.one_hot(expert_id, N_EXPERTS, dtype=jnp.float32) * e_w[..., None], axis=1)
    gates = gates.astype(xt.dtype)
    out = jnp.zeros_like(xt)
    for e in range(N_EXPERTS):
        he = jax.nn.silu(xt @ w_gate[e]) * (xt @ w_up[e])
        out = out + gates[:, e:e + 1] * (he @ w_down[e])
    return out.reshape(b, t, d)

def setup_inputs(seed: int = 0) -> dict:
    key = jax.random.key(seed)
    ks = jax.random.split(key, 32)
    f = jnp.float32
    L, D = DEPTH, D_MODEL

    def nrm(k, shape, scale):
        return jax.random.normal(k, shape, f) * scale

    return {
        "x_prompt": nrm(ks[0], (BATCH, SEQ, D), 1.0),
        "x_sample": nrm(ks[1], (DEC_BATCH, DEC_SEQ, D), 1.0),
        "cache_ckv": nrm(ks[2], (DEC_BATCH, L, PAST_LEN, KV_LORA), 1.0),
        "cache_krope": nrm(ks[3], (DEC_BATCH, L, PAST_LEN, D_ROPE), 1.0),
        "c": nrm(ks[4], (DEC_BATCH, D), 1.0),
        "c_ctx": nrm(ks[5], (D,), 1.0),
        "w_ada": nrm(ks[6], (L, D, 6 * D), 0.5 * D ** -0.5),
        "b_ada": nrm(ks[7], (L, 6 * D), 0.02),
        "g_pre1": 1.0 + nrm(ks[8], (L, D), 0.05),
        "g_post1": 1.0 + nrm(ks[9], (L, D), 0.05),
        "g_pre2": 1.0 + nrm(ks[10], (L, D), 0.05),
        "g_post2": 1.0 + nrm(ks[11], (L, D), 0.05),
        "w_in": nrm(ks[12], (L, D, IN_COLS), D ** -0.5),
        "w_dw": nrm(ks[13], (L, CONV_K, C_CONV), CONV_K ** -0.5),
        "b_dw": nrm(ks[14], (L, C_CONV), 0.02),
        "conv_ln_g": 1.0 + nrm(ks[15], (L, C_CONV), 0.05),
        "conv_ln_b": nrm(ks[16], (L, C_CONV), 0.02),
        "q_norm_g": 1.0 + nrm(ks[17], (L, Q_LORA), 0.05),
        "kv_norm_g": 1.0 + nrm(ks[18], (L, KV_LORA), 0.05),
        "w_uq": nrm(ks[19], (L, Q_LORA, N_HEADS * (D_NOPE + D_ROPE)), Q_LORA ** -0.5),
        "w_ukv": nrm(ks[20], (L, KV_LORA, N_HEADS * (D_NOPE + D_V)), KV_LORA ** -0.5),
        "w_out": nrm(ks[21], (L, D_MIX, D), D_MIX ** -0.5),
        "w_rg": nrm(ks[22], (L, D, N_GROUPS), D ** -0.5),
        "b_rg": nrm(ks[23], (L, N_GROUPS), 0.01),
        "w_re": nrm(ks[24], (L, D, N_EXPERTS), D ** -0.5),
        "b_re": nrm(ks[25], (L, N_EXPERTS), 0.01),
        "w_gate": nrm(ks[26], (L, N_EXPERTS, D, D_EXPERT), D ** -0.5),
        "w_up": nrm(ks[27], (L, N_EXPERTS, D, D_EXPERT), D ** -0.5),
        "w_down": nrm(ks[28], (L, N_EXPERTS, D_EXPERT, D), D_EXPERT ** -0.5),
    }

def reference(x_prompt, x_sample, cache_ckv, cache_krope, c, c_ctx, w_ada, b_ada,
              g_pre1, g_post1, g_pre2, g_post2, w_in, w_dw, b_dw, conv_ln_g, conv_ln_b,
              q_norm_g, kv_norm_g, w_uq, w_ukv, w_out, w_rg, b_rg, w_re, b_re,
              w_gate, w_up, w_down):
    rows = x_sample.shape[1] // GRID_W
    tabs = _axial_tables(rows)
    xp, xs = x_prompt, x_sample
    new_ckv, new_krope = [], []
    for l in range(DEPTH):
        mix_w = (w_in[l], w_dw[l], b_dw[l], conv_ln_g[l], conv_ln_b[l], q_norm_g[l],
                 kv_norm_g[l], w_uq[l], w_ukv[l], w_out[l])
        moe_w = (w_rg[l], b_rg[l], w_re[l], b_re[l], w_gate[l], w_up[l], w_down[l])

        sh1, sc1, gt1, sh2, sc2, gt2 = _adaln(c_ctx[None, :], w_ada[l], b_ada[l])
        h = _modulate(xp, g_pre1[l], sh1, sc1)
        out, ckv, krope = _token_mix(h, *mix_w, None, None, None)
        xp = xp + gt1 * _rmsnorm(out, g_post1[l])
        h = _modulate(xp, g_pre2[l], sh2, sc2)
        xp = xp + gt2 * _rmsnorm(_hier_moe(h, *moe_w), g_post2[l])
        new_ckv.append(ckv)
        new_krope.append(krope)

        sh1, sc1, gt1, sh2, sc2, gt2 = _adaln(c, w_ada[l], b_ada[l])
        h = _modulate(xs, g_pre1[l], sh1, sc1)
        out, _, _ = _token_mix(h, *mix_w, tabs, cache_ckv[:, l], cache_krope[:, l])
        xs = xs + gt1 * _rmsnorm(out, g_post1[l])
        h = _modulate(xs, g_pre2[l], sh2, sc2)
        xs = xs + gt2 * _rmsnorm(_hier_moe(h, *moe_w), g_post2[l])

    state_ckv = jnp.stack(new_ckv, axis=1)
    state_krope = jnp.stack(new_krope, axis=1)
    return (xp, xs, state_ckv, state_krope)


_drawn_inputs = setup_inputs


def setup_inputs(seed=0):
    import zlib

    import numpy as np

    out = dict(_drawn_inputs(seed))
    spreads = {}
    factors = {'g_post2': 3.971, 'q_norm_g': 4.838, 'b_re': 3.15}
    for name, (base, spread) in spreads.items():
        noise = np.random.default_rng([zlib.crc32(name.encode()), seed]).standard_normal(out[name].shape)
        drawn = base * np.exp(spread * noise) if base else spread * noise
        out[name] = jnp.asarray(drawn.astype(out[name].dtype))
    for name, factor in factors.items():
        out[name] = (out[name] * factor).astype(out[name].dtype)
    return out
```

```python
from contextlib import ExitStack

import numpy as np

import concourse.bass as bass
from concourse import mybir

F32 = mybir.dt.float32
BF16 = mybir.dt.bfloat16
I32 = mybir.dt.int32
ALU = mybir.AluOpType
ACT = mybir.ActivationFunctionType
AX = mybir.AxisListType

P = 128
D = 1024
KD = D // P
TP, TS, PAST = 128, 512, 128
T = TP + TS
NT = T // P
NKEY = TP + PAST + TS
KT = NKEY // P
C = 512
CM = C // P
TAPS = 31
HALF = TAPS // 2
H, DN, DR, DV = 4, 128, 64, 128
QL, KVL = 384, 256
QM, KM = QL // P, KVL // P
QKR = QL + KVL + DR
SCALE = float(DN + DR) ** -0.5
EPS = 1e-6
G, EG, E = 4, 8, 32
FE = 256
KF = FE // P
ROWS = 64
ROUNDS = T // ROWS
PAIRS = E // 2
MORE = (2 * T - 1) // ROWS
PADW = HALF + TP + HALF + TS + HALF
CONVW = PADW - 2 * HALF
SAMP0 = TP + HALF
CHUNK = 512
NCH = 6 * D // CHUNK
ADA = [(0, 4), (4, 2), (6, 2), (8, 2), (10, 2)]
RING = 3
UNITS = H * NT

C_ID, C_DUP, C_TRI, C_CS, C_RANK, C_IDB, C_YB, C_TOK, C_EPS = 0, 128, 256, 384, 1024, 1060, 1092, 1124, 1129
C_N = 1130


def constants():
    t = np.zeros((P, C_N), np.float32)
    p = np.arange(P)
    t[:, C_ID:C_ID + P] = np.eye(P)
    t[:, C_DUP:C_DUP + P] = (p[:, None] % DR) == (p[None, :] % DR)
    t[:, C_TRI:C_TRI + P] = p[:, None] < p[None, :]
    t[:DR, C_CS:C_CS + TP] = 1.0
    tok = np.arange(TS)
    nf = DR // 4
    freqs = (np.float32(10000.0) ** (-np.arange(nf, dtype=np.float32) / nf)).astype(np.float32)
    for d in range(DR):
        place = (tok // 64 if d < DR // 2 else tok % 64).astype(np.float32)
        ang = (place * freqs[d % nf]).astype(np.float32)
        t[d, C_CS + TP:C_CS + T] = np.cos(ang)
        t[DR + d, C_CS + TP:C_CS + T] = np.sin(ang) * (-1.0 if d % 32 < nf else 1.0)
    t[:, C_RANK:C_RANK + G] = G - np.arange(G)
    t[:, C_RANK + G:C_RANK + G + E] = E - np.arange(E)
    e = np.arange(E)
    t[:, C_IDB:C_IDB + E] = (e % 2) * ROWS * PAIRS + e // 2
    t[:, C_YB:C_YB + E] = (e // 2) * P + (e % 2) * ROWS
    t[:, C_TOK:C_TOK + NT] = np.arange(NT)[None, :] * P + p[:, None]
    t[:, C_EPS] = EPS
    return t


def pe_groups():
    names = ["vt", "ada0"] + [f"tr{k}" for k in range(KD)]
    for m in range(CM):
        names += [f"g{m}", f"a{m}", f"ada{m + 1}"]
    names += ["q0", "q1", "q2", "kv0", "stq", "kv1", "kr", "stkv", "cache", "krdup"]
    for h in range(H):
        names += [f"qn{h}", f"qr{h}"]
    names += ["state"] + [f"k{h}" for h in range(H)] + [f"v{t}" for t in range(KT)]
    for u in range(UNITS + 1):
        if u < UNITS:
            names.append(f"S{u}")
        if u >= 1:
            names.append(f"T{u - 1}")
            if u % NT == 0:
                names.append(f"O{u // NT - 1}")
    names += ["lnm", "lnv"]
    for b in range(NT + 2):
        if b < NT:
            names.append(f"P{b}")
        if b >= 2:
            names += [f"ht{b - 2}", f"rt{b - 2}", f"rl{b - 2}"]
    names.append("pos")
    return names


def hybrid_layer(nc, i, outs):
    y_prompt, y_sample, state_ckv, state_krope = outs
    order = pe_groups()
    place = {name: (n % 4, n // 4) for n, name in enumerate(order)}

    with ExitStack() as ctx:
        def sb(name, shape, dt=F32):
            return ctx.enter_context(nc.sbuf_tensor(name, shape, dt))

        def sem(name):
            return ctx.enter_context(nc.semaphore(name))

        def dram(name, shape, dt=F32):
            return nc.dram_tensor(name, shape, dt, kind="Internal").ap()

        def part(t, at, *shape):
            n = int(np.prod(shape))
            v = t[:, at:at + n]
            if len(shape) == 2:
                return v.rearrange("p (a b) -> p a b", a=shape[0])
            if len(shape) == 3:
                return v.rearrange("p (a b c) -> p a b c", a=shape[0], b=shape[1])
            return v

        ada_d = dram("ada_d", (2, NCH, 4, P))
        h2_d = dram("h2_d", (T, D))
        ids_d = dram("ids_d", (ROUNDS * P * PAIRS, 1), I32)
        y_d = dram("y_d", ((PAIRS + MORE) * P, D))

        x = sb("x", [P, NT, D])
        cst = sb("cst", [P, C_N])
        W = sb("W", [P, 2 * KD * P * 4 + KD * QKR])
        R1 = sb("R1", [P, RING * KD * CHUNK])
        QW = sb("QW", [P, 3 * 768 + 2 * 1024 + 3 * 512])
        HM = sb("HM", [P, KD * T])
        CQ = sb("CQ", [P, 7936])
        ones = sb("ones", [P, P])
        onesb = sb("onesb", [P, P], BF16)
        trib = sb("trib", [P, P], BF16)
        cT = sb("cT", [P, 2, KD])
        csT = sb("csT", [P, KD, 32])
        wr = sb("wr", [P, KD, G + E])
        rbias = sb("rbias", [G + E, 1])
        modT = sb("modT", [P, 2, 2, KD])
        stat = sb("stat", [P, 8, NT])
        vecT = sb("vecT", [P, 17])
        wdw = sb("wdw", [P, CM * TAPS])
        amax = sb("amax", [P, 3, UNITS])
        asum = sb("asum", [P, 2, UNITS])
        wsel = sb("wsel", [P, 2, NT])
        slot_i = sb("slot_i", [P, 2, 2, NT], I32)
        tok_i = sb("tok_i", [P, NT], I32)
        ids = sb("ids", [P, ROUNDS, PAIRS], I32)
        idx = sb("idx", [P, 4], I32)
        extra = sb("extra", [1, PAIRS], I32)
        first = sb("first", [1, PAIRS], I32)
        more_i = sb("more_i", [P, PAIRS], I32)
        idx_r = sb("idx_r", [P, 2 * NT], I32)

        x_rg = sb("x_rg", [P, KD, G])[:]
        x_re = sb("x_re", [P, KD, E])[:]

        ident = cst[:, C_ID:C_ID + P]
        dup = cst[:, C_DUP:C_DUP + P]
        CS = cst[:, C_CS:C_CS + T]
        eps = cst[:, C_EPS:C_EPS + 1]

        wC = part(W, 0, KD, 2 * C)
        wQ = part(W, KD * 2 * C, KD, QKR)
        acc = part(W, 0, CM, CONVW)
        o = CM * CONVW
        sq = part(W, o, 5, T)
        rB = part(W, o + 5 * T, 2, T)
        wkr = part(W, o + 7 * T, KD, P)
        assert o + 7 * T + KD * P <= KD * 2 * C
        wo = part(W, o, KD, D)
        ring = part(R1, 0, RING, KD, CHUNK)
        qn = part(R1, 0, H, T)
        qr = part(R1, 2560, H, T)
        kn = part(R1, 5120, H, NKEY)
        kr = part(R1, 8192, NKEY)
        vv = part(R1, 8960, KT, H * DV)
        wuq = part(QW, 0, QM, H * (DN + DR))
        wukv = part(QW, 2304, KM, H * (DN + DV))
        wqr = part(QW, 4352, QM * H, P)
        gg1 = part(QW, 0, 2, D)
        a2 = part(QW, 2048, 2, D)
        h2T = part(QW, 4096, KD, P)
        wdrow = HM[0:TAPS, 0:C]
        vrow = HM[0:17, C:C + P]
        hT = part(HM, 0, KD, T)
        mixT = hT
        xn = part(CQ, 0, NT, D)
        rows = part(CQ, NT * D, NCH, P)
        grow = part(CQ, NT * D + NCH * P, 8, P)
        hc = part(CQ, 0, CM, PADW)
        o = CM * PADW
        sg = part(CQ, o, 2, T)
        qa = part(CQ, o, QM, T)
        ck = part(CQ, o + QM * T, KM, NKEY)
        tk = part(CQ, o + QM * T + KM * NKEY, T)
        ckr = part(CQ, o + QM * T + KM * NKEY + T, P)
        cckv = part(CQ, o + QM * T + KM * NKEY + T + P, KVL)
        sto = part(CQ, o + QM * T + KM * NKEY + T + P + KVL, KVL + DR)
        assert o + QM * T + KM * NKEY + T + P + 2 * KVL + DR <= 7936
        pr = part(CQ, o, 2, T)
        pT = part(CQ, o + 2 * T, 5, TS)
        pTp = part(CQ, o + 2 * T + 5 * TS, P)
        lsq = part(CQ, o, CM, T)
        mB = part(CQ, o + CM * T, CONVW)
        sB = part(CQ, o + CM * T + CONVW, CONVW)
        b2 = part(CQ, 0, 2, D)
        po = part(CQ, o, 2, D)
        h2 = part(CQ, o + 2 * D, 2, D)
        lg = CQ[0:G + E, o + 4 * D:o + 4 * D + P]
        assert o + 4 * D + P <= 7936
        L = part(CQ, o + 4 * D + P, NT, G + E)
        rt = part(CQ, o, 12, NT * E)
        rt_e = rt[:, 11, 0:NT * (G + 1)].rearrange("p (t g) -> p t g", g=G + 1)
        maskb = sb("maskb", [P, NT, E], BF16)
        gg2 = part(CQ, 0, 2, D)
        slots = [part(R1, 0, 2, 3, KD * FE), part(W, 0, 2, 3, KD * FE)]
        xg = part(HM, 0, 2, D)
        xT = part(HM, 2048, 2, KD, P)
        he = part(HM, 4096, 2, FE)
        heT = part(HM, 4096 + 2 * FE, 2, KF, P)
        ys = part(QW, 0, 2, D)
        xgX = part(QW, 2048, D)
        xTX = part(QW, 3072, KD, P)
        ysX = part(QW, 4096, D)
        heX = part(QW, 5120, FE)
        heTX = part(QW, 5120 + FE, KF, P)
        yg = part(R1, 0, 4, D)
        yo = part(R1, 4 * D, 2, D)
        yjunk = part(R1, 6 * D, D)

        ps = ctx.enter_context(nc.psum_tensor("ps", [P, 8, 512], F32))

        def pp(name):
            s = place[name][0]
            return ps[:, 2 * s:2 * s + 2, :].rearrange("p a b -> p (a b)")

        filled = [sem(f"filled{s}") for s in range(4)]
        drained = [sem(f"drained{s}") for s in range(4)]
        x_in = [sem(f"x_in{b}") for b in range(NT)]
        cst_in, cvec_in, vec_in, brow_in = sem("cst_in"), sem("cvec_in"), sem("vec_in"), sem("brow_in")
        ada_in = [sem(f"ada_in{s}") for s in range(RING)]
        ada_used = sem("ada_used")
        wc_in, wq_in, wuq_in, wukv_in = sem("wc_in"), sem("wq_in"), sem("wuq_in"), sem("wukv_in")
        cache_in, wr_in, wo_in = sem("cache_in"), sem("wr_in"), sem("wo_in")
        zeroed, cs_ready, wr_ready, small_ready = sem("zeroed"), sem("cs_ready"), sem("wr_ready"), sem("small_ready")
        ss_ready, var_ready, sd_ready, xn_ready = sem("ss_ready"), sem("var_ready"), sem("sd_ready"), sem("xn_ready")
        rows_ready, ada_st, mod_in = sem("rows_ready"), [sem(f"ada_st{n}") for n in range(5)], sem("mod_in")
        hT_act, hT_dve = sem("hT_act"), sem("hT_dve")
        hc_zero, sg_ready = sem("hc_zero"), sem("sg_ready")
        wkr_ready, wqr_ready = sem("wkr_ready"), sem("wqr_ready")
        sq_ready, qn_ready, ckn_ready = sem("sq_ready"), sem("qn_ready"), sem("ckn_ready")
        cachekv_ready, state_out = sem("cachekv_ready"), sem("state_out")
        proj_act, proj_dve = sem("proj_act"), sem("proj_dve")
        max_ready, p_ready = sem("max_ready"), sem("p_ready")
        conv_ready, cen_ready, lsq_ready, lnn_ready, mixc_ready = (
            sem("conv_ready"), sem("cen_ready"), sem("lsq_ready"), sem("lnn_ready"), sem("mixc_ready"))
        gg1_in, a2_in, b2_in, gg2_in = sem("gg1_in"), sem("a2_in"), sem("b2_in"), sem("gg2_in")
        pss, pvar, psd, x1_ready, xss, xvar, xsd, h2m_ready = (
            sem("pss"), sem("pvar"), sem("psd"), sem("x1_ready"), sem("xss"), sem("xvar"), sem("xsd"), sem("h2m_ready"))
        h2_ready = sem("h2_ready")
        h2_st = [sem("h2_st0"), sem("h2_st1")]
        rgmax, rexp, mask_ready, idx_ready, cnt_ready = sem("rgmax"), sem("rexp"), sem("mask_ready"), sem("idx_ready"), sem("cnt_ready")
        ids_zero, ids_st, ids_in, y_zero = sem("ids_zero"), sem("ids_st"), sem("ids_in"), sem("y_zero")
        w_in_s = [[sem(f"w{s}{j}") for j in range(2)] for s in range(2)]
        w_used = sem("w_used")
        xg_in = [sem("xg_in0"), sem("xg_in1")]
        e_tr, e_xT, e_gu, e_silu, e_h, e_ht, e_hT, e_y, e_ys = (sem(n) for n in (
            "e_tr", "e_xT", "e_gu", "e_silu", "e_h", "e_ht", "e_hT", "e_y", "e_ys"))
        y_st = [sem("y_st0"), sem("y_st1")]
        r_dma, r_xg, r_tr, r_xT, r_gu, r_silu, r_h, r_ht, r_hT, r_y, r_ys, r_st = (sem(n) for n in (
            "r_dma", "r_xg", "r_tr", "r_xT", "r_gu", "r_silu", "r_h", "r_ht", "r_hT", "r_y", "r_ys", "r_st"))
        yg_in, f_mix, f_ss, f_var, f_sd, f_out, out_st = ([sem("yg_in0"), sem("yg_in1")], sem("f_mix"), sem("f_ss"),
                                                          sem("f_var"), sem("f_sd"), sem("f_out"), sem("out_st"))

        def begin(pe, name):
            s, use = place[name]
            if use:
                pe.wait_ge(drained[s], use)

        def done(ins, name):
            return ins.then_inc(filled[place[name][0]], 1)

        def landed(eng, name):
            s, use = place[name]
            eng.wait_ge(filled[s], use + 1)

        def free(ins, name):
            return ins.then_inc(drained[place[name][0]], 1)

        def emptied(eng, name):
            s, use = place[name]
            eng.wait_ge(drained[s], use + 1)

        w_in_v = i["w_in"][0].rearrange("(p k) n -> p k n", k=KD)
        ada_v = i["w_ada"][0].rearrange("(p k) (c n) -> c p k n", k=KD, n=CHUNK)
        ada_flat = ada_d.rearrange("v n j c -> v (n j c)")

        def bcast(v, vec):
            return ada_flat[v:v + 1, vec * D:(vec + 1) * D].broadcast_to([P, D])

        block = ctx.enter_context(nc.Block())

        @block.sync
        def _(sp):
            for b in range(NT):
                src = i["x_prompt"][0] if b == 0 else i["x_sample"][0, (b - 1) * P:b * P, :]
                sp.dma_start(x[:, b, :], src).then_inc(x_in[b], 16)

            def ada_chunk(n):
                if n >= RING:
                    sp.wait_ge(ada_used, n - RING + 1)
                sp.dma_start(ring[:, n % RING], ada_v[n]).then_inc(ada_in[n % RING], 16)

            for n in range(4):
                ada_chunk(n)
            sp.dma_start(wC, w_in_v[:, :, 0:2 * C]).then_inc(wc_in, 16)
            sp.dma_start(wQ, w_in_v[:, :, 2 * C:]).then_inc(wq_in, 16)
            for n in range(4, 7):
                ada_chunk(n)
            sp.dma_start(wuq, i["w_uq"][0].rearrange("(k p) n -> p k n", p=P)).then_inc(wuq_in, 16)
            sp.dma_start(wukv, i["w_ukv"][0].rearrange("(k p) n -> p k n", p=P)).then_inc(wukv_in, 16)
            for n in range(7, NCH):
                ada_chunk(n)
            sp.wait_ge(zeroed, 1)
            zero = ids[:].rearrange("p a b -> p (a b)").bitcast(F32)[:, 0:P].unsqueeze(1).broadcast_to([P, D // P, P])
            for n in range(MORE):
                rows_n = y_d[(PAIRS + n) * P:(PAIRS + n + 1) * P, :].rearrange("p (a b) -> p a b", b=P)
                sp.dma_start(rows_n, zero).then_inc(y_zero, 16)
            emptied(sp, "kr")
            landed(sp, "stkv")
            sp.wait_ge(qn_ready, 1)
            sp.wait_ge(ckn_ready, 1)
            sp.dma_start(wo, i["w_out"][0].rearrange("(k p) n -> p k n", p=P)).then_inc(wo_in, 16)
            landed(sp, "v5")
            sp.wait_ge(ada_st[1], 32)
            sp.wait_ge(ada_st[3], 32)
            for v in range(2):
                sp.dma_start(gg1[:, v, :], bcast(v, 2)).then_inc(gg1_in, 16)
                sp.dma_start(a2[:, v, :], bcast(v, 4)).then_inc(a2_in, 16)
            sp.wait_ge(conv_ready, 1)
            sp.wait_ge(ada_st[2], 32)
            for v in range(2):
                sp.dma_start(b2[:, v, :], bcast(v, 3)).then_inc(b2_in, 16)

            for one in (y_st[0], y_st[1], r_st):
                sp.sem_inc(one, 16)

            def load_pair(pair, s):
                for j in range(2):
                    for n, w in enumerate(("w_gate", "w_up")):
                        src = i[w][0][bass.ds(2 * pair + j, 1)].rearrange("e (p k) f -> p (e k f)", k=KD)
                        sp.dma_start(slots[s][:, j, n, :], src).then_inc(w_in_s[s][j], 16)
                    src = i["w_down"][0][bass.ds(2 * pair + j, 1)].rearrange("e (p k) f -> p (e k f)", k=KF)
                    sp.dma_start(slots[s][:, j, 2, :], src).then_inc(w_in_s[s][j], 16)

            landed(sp, f"O{H - 1}")
            sp.wait_ge(ada_used, NCH)
            load_pair(0, 0)
            for b in range(NT):
                sp.wait_ge(h2_ready, b + 1)
                sp.dma_start(h2_d[b * P:(b + 1) * P, :], h2[:, b % 2, :]).then_inc(h2_st[b % 2], 16)
                if b == NT - 1:
                    landed(sp, f"P{NT - 1}")
                    sp.wait_ge(mixc_ready, 1)
                    load_pair(1, 1)
            sp.wait_ge(xvar, NT)
            sp.wait_ge(h2_ready, NT)
            sp.wait_ge(ada_st[4], 32)
            for v in range(2):
                sp.dma_start(gg2[:, v, :], bcast(v, 5)).then_inc(gg2_in, 16)

            y_blocks = y_d.rearrange("(q p) d -> q p d", p=P)
            sp.wait_ge(y_zero, 16 * MORE)

            def store_pair(pair, s):
                sp.wait_ge(e_ys, pair + 2)
                sp.dma_start(y_blocks[bass.ds(pair, 1)].rearrange("q p d -> (q p) d"), ys[:, s, :]).then_inc(y_st[s], 16)
                n = sp.value_load(extra[0:1, bass.ds(pair, 1)], min_val=0, max_val=ROUNDS - 1)
                block0 = sp.value_load(first[0:1, bass.ds(pair, 1)], min_val=0, max_val=MORE)
                with sp.If(n > 0):
                    with sp.Fori(1, ROUNDS) as r:
                        with sp.If(n >= r):
                            sp.wait_ge(r_ys, pair * (ROUNDS - 1) + r + 1)
                            row = nc.s_assert_within(sp.snap(block0 + r + (PAIRS - 1)), 0, PAIRS + MORE - 1)
                            sp.dma_start(y_blocks[bass.ds(row, 1)].rearrange("q p d -> (q p) d"),
                                         ysX).then_inc(r_st, 16)
                            sp.nop()
                        with sp.Else():
                            sp.sem_inc(r_st, 16)
                        sp.nop()
                    sp.nop()
                with sp.Else():
                    sp.sem_inc(r_st, 16 * (ROUNDS - 1))
                sp.nop()

            sp.wait_ge(cnt_ready, 1)
            with sp.Fori(0, PAIRS // 2 - 1) as turn2:
                q = 2 * turn2
                for s in range(2):
                    store_pair(q + s, s)
                    sp.wait_ge(w_used, q + s + 1)
                    load_pair(q + s + 2, s)
            for s in range(2):
                store_pair(PAIRS - 2 + s, s)
            for b in range(NT):
                sp.wait_ge(f_out, b + 1)
                dst = y_prompt[0] if b == 0 else y_sample[0, (b - 1) * P:b * P, :]
                sp.dma_start(dst, x[:, b, :]).then_inc(out_st, 16)
            sp.wait_ge(out_st, 16 * NT)
            sp.wait_ge(state_out, 32)

        @block.gpsimd
        def _(gp):
            gp.memset(ones[:], 1.0)
            gp.memset(onesb[:], 1.0)
            gp.memset(csT[:], 0.0)
            gp.memset(ids[:], 0)
            gp.memset(rows, 0.0)
            gp.memset(grow, 0.0).then_inc(zeroed, 1)
            gp.wait_ge(zeroed, 1)
            gp.dma_start(ids_d.rearrange("(p n) one -> p (n one)", p=P), ids[:].rearrange("p a b -> p (a b)")).then_inc(ids_zero, 16)
            bv = i["b_ada"][0].rearrange("(n j c) -> j n c", j=4, c=P)
            gains = (("g_pre1", 0), ("g_post1", 2), ("g_pre2", 4), ("g_post2", 6))
            for v in range(2):
                gp.dma_start(rows[v:v + 97:32], bv).then_inc(brow_in, 16)
                for name, at in gains:
                    gp.dma_start(grow[v:v + 97:32, at:at + 2], i[name][0].rearrange("(n j c) -> j n c", j=4, c=P)).then_inc(brow_in, 16)
            gp.wait_ge(cst_in, 16)
            gp.tensor_copy(trib[:], cst[:, C_TRI:C_TRI + P])
            gp.tensor_copy(tok_i[:], cst[:, C_TOK:C_TOK + NT]).then_inc(small_ready, 1)

            def put_rows(n):
                gp.wait_ge(rows_ready, n + 1)
                a, c = ADA[n]
                for v in range(2):
                    gp.dma_start(ada_d[v, a:a + c].rearrange("n j c -> j n c"), rows[v:v + 97:32, a:a + c]).then_inc(ada_st[n], 16)

            put_rows(0)
            gp.wait_ge(ada_st[0], 32)
            for v in range(2):
                gp.dma_start(modT[:, v], ada_flat[v, 0:2 * D].rearrange("(a p k) -> p a k", p=P, k=KD)).then_inc(mod_in, 16)
            landed(gp, "tr7")
            for a, n in ((0, HALF), (HALF + TP, HALF), (PADW - HALF, HALF)):
                last = gp.memset(hc[:, :, a:a + n], 0.0)
            last.then_inc(hc_zero, 1)
            gp.wait_ge(wr_in, 64)
            gp.tensor_copy(wr[:, :, 0:G], x_rg)
            gp.tensor_copy(wr[:, :, G:], x_re).then_inc(wr_ready, 1)
            for n in range(1, 3):
                put_rows(n)
            landed(gp, "a3")
            gp.wait_ge(wq_in, 16)
            krw = wQ[:, :, QL + KVL:]
            gp.tensor_copy(wkr[:, :, 0:DR], krw)
            for half in range(2):
                dst = wkr[:, :, DR:].rearrange("p k (b h c) -> p k b h c", b=2, h=2)[:, :, :, half, :]
                src = krw.rearrange("p k (b h c) -> p k b h c", b=2, h=2)[:, :, :, 1 - half, :]
                last = gp.tensor_copy(dst, src)
            last.then_inc(wkr_ready, 1)
            gp.wait_ge(wuq_in, 16)
            qrw = wuq.rearrange("p k (h c) -> p (k h) c", h=H)[:, :, DN:]
            gp.tensor_copy(wqr[:, :, 0:DR], qrw)
            for half in range(2):
                dst = wqr[:, :, DR:].rearrange("p k (b h c) -> p k b h c", b=2, h=2)[:, :, :, half, :]
                src = qrw.rearrange("p k (b h c) -> p k b h c", b=2, h=2)[:, :, :, 1 - half, :]
                last = gp.tensor_copy(dst, src)
            last.then_inc(wqr_ready, 1)
            for n in range(3, 5):
                put_rows(n)
            for n in range(5):
                gp.wait_ge(ada_st[n], 32)
            for n in range(2):
                gp.dma_start(ckr[:, n * DR:(n + 1) * DR], i["cache_krope"][0, 0]).then_inc(cache_in, 16)
            gp.dma_start(cckv, i["cache_ckv"][0, 0]).then_inc(cache_in, 16)
            gp.wait_ge(b2_in, 32)
            for b in range(NT):
                gp.wait_ge(h2m_ready, b + 1)
                gp.tensor_tensor(h2[:, b % 2, :], h2[:, b % 2, :], b2[:, min(b, 1), :], ALU.add).then_inc(h2_ready, 1)
            gp.wait_ge(idx_ready, 1)
            gp.wait_ge(ids_zero, 16)
            for b in range(NT):
                for c in range(2):
                    gp.indirect_dma_start(ids_d, bass.IndirectOffsetOnAxis(slot_i[:, 0, c, b:b + 1], 0),
                                          tok_i[:, b:b + 1], None).then_inc(ids_st, 16)
            gp.wait_ge(y_zero, 16 * MORE)
            gp.wait_ge(ids_st, 16 * 2 * NT)
            gp.dma_start(ids[:], ids_d.rearrange("(r p q) one -> p r (q one)", r=ROUNDS, q=PAIRS)).then_inc(ids_in, 16)
            gp.wait_ge(ids_in, 16)
            gp.wait_ge(h2_st[0], 16 * 3)
            gp.wait_ge(h2_st[1], 16 * 2)
            gp.wait_ge(cnt_ready, 1)

            def gather(pair, s):
                gp.tensor_copy(idx[:, s:s + 1], ids[:, 0, bass.ds(pair, 1)])
                gp.drain()
                gp.indirect_dma_start(xg[:, s, :], None, h2_d, bass.IndirectOffsetOnAxis(idx[:, s:s + 1], 0)).then_inc(xg_in[s], 16)

            def further(pair):
                n = gp.value_load(extra[0:1, bass.ds(pair, 1)], min_val=0, max_val=ROUNDS - 1)
                with gp.If(n > 0):
                    with gp.Fori(1, ROUNDS) as r:
                        with gp.If(n >= r):
                            at = gp.snap(pair * (ROUNDS - 1) + r)
                            gp.wait_ge(r_st, 16 * at)
                            gp.tensor_copy(idx[:, 2:3], ids[:].rearrange("p a b -> p (a b)")[:, bass.ds(r * PAIRS + pair, 1)])
                            gp.drain()
                            gp.indirect_dma_start(xgX, None, h2_d, bass.IndirectOffsetOnAxis(idx[:, 2:3], 0)).then_inc(r_dma, 16)
                            gp.drain().then_inc(r_xg, 1)
                            gp.nop()
                        with gp.Else():
                            gp.sem_inc(r_xg, 1)
                        gp.nop()
                    gp.nop()
                with gp.Else():
                    gp.sem_inc(r_xg, ROUNDS - 1)
                gp.nop()

            landed(gp, f"P{NT - 1}")
            for s in range(2):
                gather(s, s)
            with gp.Fori(0, PAIRS // 2 - 1) as turn2:
                q = 2 * turn2
                for s in range(2):
                    gp.wait_ge(e_tr, q + s + 1)
                    gather(q + s + 2, s)
                    further(q + s)
            for s in range(2):
                further(PAIRS - 2 + s)
            gp.wait_ge(y_st[0], 16 * (PAIRS // 2 + 1))
            gp.wait_ge(y_st[1], 16 * (PAIRS // 2 + 1))
            gp.wait_ge(r_st, 16 * (PAIRS * (ROUNDS - 1) + 1))
            gp.wait_ge(w_used, PAIRS)
            for b in range(NT):
                if b >= 2:
                    gp.wait_ge(f_mix, b - 1)
                for c in range(2):
                    gp.indirect_dma_start(yg[:, 2 * (b % 2) + c, :], None, y_d,
                                          bass.IndirectOffsetOnAxis(slot_i[:, 1, c, b:b + 1], 0)).then_inc(yg_in[b % 2], 16)

        def rms(act, name, n, scale):
            landed(act, name)
            act.activation(rB[:, n, TP:], pp(name)[:, 0:TS], ACT.Sqrt, bias=eps, scale=scale)
            free(act.activation(rB[:, n, 0:TP], pp(name)[:, 512:512 + TP], ACT.Sqrt, bias=eps, scale=scale), name)

        @block.scalar
        def _(act):
            act.dma_start(cst[:], i["consts"]).then_inc(cst_in, 16)
            act.dma_start(cT[:, 0, :], i["c_ctx"].rearrange("(p k) -> p k", k=KD)).then_inc(cvec_in, 16)
            act.dma_start(cT[:, 1, :], i["c"][0].rearrange("(p k) -> p k", k=KD)).then_inc(cvec_in, 16)
            act.dma_start(wdrow, i["w_dw"][0]).then_inc(vec_in, 16)
            at = 0
            for name in ("b_dw", "conv_ln_g", "conv_ln_b", "q_norm_g", "kv_norm_g"):
                n = i[name].shape[1] // P
                act.dma_start(vrow[at:at + n], i[name][0].rearrange("(m p) -> m p", p=P)).then_inc(vec_in, 16)
                at += n
            act.dma_start(rbias[0:G], i["b_rg"][0].rearrange("(e one) -> e one", one=1)).then_inc(wr_in, 16)
            act.dma_start(rbias[G:G + E], i["b_re"][0].rearrange("(e one) -> e one", one=1)).then_inc(wr_in, 16)
            act.dma_start(x_rg, i["w_rg"][0].rearrange("(p k) e -> p k e", k=KD)).then_inc(wr_in, 16)
            act.dma_start(x_re, i["w_re"][0].rearrange("(p k) e -> p k e", k=KD)).then_inc(wr_in, 16)
            act.wait_ge(cvec_in, 32)
            act.wait_ge(zeroed, 1)
            for v in range(2):
                last = act.activation(csT[:, :, v], cT[:, v, :], ACT.Silu)
            last.then_inc(cs_ready, 1)
            for b in range(NT):
                act.wait_ge(x_in[b], 16)
                act.activation(xn[:, b, :], x[:, b, :], ACT.Square, accum_out=stat[:, 0, b:b + 1]).then_inc(ss_ready, 1)
            act.wait_ge(var_ready, 1)
            act.activation(stat[:, 2, :], stat[:, 1, :], ACT.Sqrt).then_inc(sd_ready, 1)
            act.wait_ge(mod_in, 32)
            for k in range(0, KD, 2):
                name = f"tr{k}"
                landed(act, name)
                act.activation(hT[:, k, TP:], pp(name)[:, 0:TS], ACT.Identity, bias=modT[:, 1, 0, k:k + 1], scale=modT[:, 1, 1, k:k + 1])
                free(act.activation(hT[:, k, 0:TP], pp(name)[:, 512:512 + TP], ACT.Identity,
                                    bias=modT[:, 0, 0, k:k + 1], scale=modT[:, 0, 1, k:k + 1]), name)
            act.drain().then_inc(hT_act, 1)
            for m in range(CM):
                name = f"g{m}"
                landed(act, name)
                if m >= 2:
                    emptied(act, f"a{m - 2}")
                elif m == 0:
                    act.wait_ge(hc_zero, 1)
                act.activation(sg[:, m % 2, 0:TP], pp(name)[:, 512:512 + TP], ACT.Sigmoid)
                free(act.activation(sg[:, m % 2, TP:], pp(name)[:, 0:TS], ACT.Sigmoid), name)
                act.drain().then_inc(sg_ready, 1)
            emptied(act, f"a{CM - 1}")
            for n in range(5):
                act.wait_ge(ada_st[n], 32)
            landed(act, "a3")
            for n, name in enumerate(("q0", "q1", "q2", "kv0", "kv1")):
                landed(act, name)
                g = pp(name)
                if n < QM:
                    act.activation(qa[:, n, TP:], g[:, 0:TS], ACT.Copy)
                    act.activation(qa[:, n, 0:TP], g[:, 512:512 + TP], ACT.Copy)
                else:
                    act.activation(ck[:, n - QM, TP + PAST:], g[:, 0:TS], ACT.Copy)
                    act.activation(ck[:, n - QM, 0:TP], g[:, 512:512 + TP], ACT.Copy)
                act.activation(sq[:, n, TP:], g[:, 0:TS], ACT.Square)
                free(act.activation(sq[:, n, 0:TP], g[:, 512:512 + TP], ACT.Square), name)
                act.drain().then_inc(sq_ready, 1)
                if n == 3:
                    rms(act, "stq", 0, 1.0 / QL)
            rms(act, "stkv", 1, 1.0 / KVL)
            landed(act, "cache")
            act.activation(kr[:, TP:TP + PAST], pp("cache")[:, 0:P], ACT.Copy)
            for m in range(KM):
                last = act.activation(ck[:, m, TP:TP + PAST], pp("cache")[:, (1 + m) * P:(2 + m) * P], ACT.Copy)
            free(last, "cache")
            act.drain().then_inc(cachekv_ready, 1)
            landed(act, "krdup")
            act.activation(kr[:, TP + PAST:], pp("krdup")[:, 0:TS], ACT.Copy)
            free(act.activation(kr[:, 0:TP], pp("krdup")[:, 512:512 + TP], ACT.Copy), "krdup")
            for h in range(H):
                name = f"qn{h}"
                landed(act, name)
                act.activation(qn[:, h, TP:], pp(name)[:, 0:TS], ACT.Copy)
                free(act.activation(qn[:, h, 0:TP], pp(name)[:, 512:512 + TP], ACT.Copy), name)
            landed(act, "state")
            free(act.activation(sto, pp("state")[:, 0:KVL + DR], ACT.Copy), "state")
            emptied(act, "state")
            act.dma_start(state_ckv[0, 0], sto[:, 0:KVL]).then_inc(state_out, 16)
            act.dma_start(state_krope[0, 0], sto[:, KVL:]).then_inc(state_out, 16)
            for h in range(H):
                name = f"k{h}"
                landed(act, name)
                act.activation(kn[:, h, TP + PAST:], pp(name)[:, 0:TS], ACT.Copy)
                free(act.activation(kn[:, h, 0:TP + PAST], pp(name)[:, 512:512 + TP + PAST], ACT.Copy), name)
            for t in range(KT):
                name = f"v{t}"
                landed(act, name)
                free(act.activation(vv[:, t, :], pp(name)[:, 0:512], ACT.Copy), name)
            act.drain().then_inc(proj_act, 1)
            act.wait_ge(state_out, 32)
            for u in range(UNITS + 1):
                if u < UNITS:
                    w = T if u % NT < 4 else TP
                    act.wait_ge(max_ready, u + 1)
                    if u >= 2:
                        landed(act, f"T{u - 2}")
                    free(act.activation(pr[:, u % 2, 0:w], pp(f"S{u}")[:, 0:w], ACT.Exp, bias=amax[:, 1, u:u + 1],
                                        scale=SCALE, accum_out=asum[:, 0, u:u + 1]), f"S{u}")
                if u >= 1:
                    n = u - 1
                    name = f"T{n}"
                    landed(act, name)
                    if n >= NT and n % NT == 0:
                        landed(act, f"O{n // NT - 1}")
                    if n % NT < 4:
                        q = n % NT
                        src = pp(name)[:, 0:T].rearrange("p (t q) -> p t q", q=P)
                        free(act.activation(pT[:, :, q * P:(q + 1) * P], src, ACT.Copy), name)
                    else:
                        free(act.activation(pTp, pp(name)[:, 0:P], ACT.Copy), name)
                        h = n // NT
                        landed(act, f"O{h}")
                        act.activation(mixT[:, CM + h, TP:], pp(f"O{h}")[:, 0:TS], ACT.Copy)
                        free(act.activation(mixT[:, CM + h, 0:TP], pp(f"O{h}")[:, 512:512 + TP], ACT.Copy), f"O{h}")
            landed(act, "lnm")
            act.activation(mB[:, SAMP0:], pp("lnm")[:, 0:TS], ACT.Copy, scale=1.0 / C)
            free(act.activation(mB[:, 0:TP], pp("lnm")[:, 512:512 + TP], ACT.Copy, scale=1.0 / C), "lnm")
            for m in range(CM):
                act.wait_ge(cen_ready, m + 1)
                act.activation(lsq[:, m, TP:], acc[:, m, SAMP0:], ACT.Square)
                act.activation(lsq[:, m, 0:TP], acc[:, m, 0:TP], ACT.Square)
                act.drain().then_inc(lsq_ready, 1)
            landed(act, "lnv")
            act.activation(sB[:, SAMP0:], pp("lnv")[:, 0:TS], ACT.Sqrt, bias=eps, scale=1.0 / C)
            free(act.activation(sB[:, 0:TP], pp("lnv")[:, 512:512 + TP], ACT.Sqrt, bias=eps, scale=1.0 / C), "lnv")
            for m in range(CM):
                act.wait_ge(lnn_ready, m + 1)
                g, bb = vecT[:, CM + m:CM + m + 1], vecT[:, 2 * CM + m:2 * CM + m + 1]
                act.activation(mixT[:, m, TP:], acc[:, m, SAMP0:], ACT.Silu, bias=bb, scale=g)
                act.activation(mixT[:, m, 0:TP], acc[:, m, 0:TP], ACT.Silu, bias=bb, scale=g)
            act.drain().then_inc(mixc_ready, 1)
            for b in range(NT + 2):
                if b < NT:
                    name = f"P{b}"
                    landed(act, name)
                    if b >= 2:
                        act.wait_ge(x1_ready, b - 1)
                    act.activation(po[:, b % 2, :], pp(name)[:, 0:D], ACT.Square, accum_out=stat[:, 3, b:b + 1]).then_inc(pss, 1)
                    act.wait_ge(pvar, b + 1)
                    act.activation(stat[:, 5, b:b + 1], stat[:, 4, b:b + 1], ACT.Sqrt).then_inc(psd, 1)
                    act.wait_ge(x1_ready, b + 1)
                    if b >= 2:
                        act.wait_ge(h2_st[b % 2], 16 * (b // 2))
                        landed(act, f"ht{b - 2}")
                    act.activation(h2[:, b % 2, :], x[:, b, :], ACT.Square, accum_out=stat[:, 6, b:b + 1]).then_inc(xss, 1)
                    act.wait_ge(xvar, b + 1)
                    act.activation(stat[:, 7, b:b + 1], stat[:, 4, b:b + 1], ACT.Sqrt).then_inc(xsd, 1)
                if b >= 2:
                    n = b - 2
                    landed(act, f"ht{n}")
                    if n >= 1:
                        landed(act, f"rt{n - 1}")
                    free(act.activation(h2T.rearrange("p k t -> p (k t)"), pp(f"ht{n}"), ACT.Copy), f"ht{n}")
                    landed(act, f"rt{n}")
                    free(act.activation(lg, pp(f"rt{n}")[0:G + E, 0:P], ACT.Identity, bias=rbias[:]), f"rt{n}")
            act.wait_ge(rgmax, 1)
            act.activation(rt_e, rt_e, ACT.Exp).then_inc(rexp, 1)

            def expert_pair(pair, s, last=False):
                act.wait_ge(e_gu, pair + 1)
                act.activation(he[:, s, :], ps[:, s, 0:FE], ACT.Silu).then_inc(e_silu, 1)
                if not last:
                    act.wait_ge(e_tr, pair + 2)
                    act.activation(xT[:, 1 - s].rearrange("p k t -> p (k t)"), ps[:, 6:8, :].rearrange("p a b -> p (a b)"), ACT.Copy).then_inc(e_xT, 1)
                act.wait_ge(e_ht, pair + 1)
                act.activation(heT[:, s].rearrange("p k t -> p (k t)"), ps[:, s, 0:FE], ACT.Copy).then_inc(e_hT, 1)
                n = act.value_load(extra[0:1, bass.ds(pair, 1)], min_val=0, max_val=ROUNDS - 1)
                with act.If(n > 0):
                    with act.Fori(1, ROUNDS) as r:
                        with act.If(n >= r):
                            at = act.snap(pair * (ROUNDS - 1) + r)
                            act.wait_ge(r_tr, at)
                            act.activation(xTX.rearrange("p k t -> p (k t)"), ps[:, 6:8, :].rearrange("p a b -> p (a b)"), ACT.Copy).then_inc(r_xT, 1)
                            act.wait_ge(r_gu, at)
                            act.activation(heX, ps[:, s, 0:FE], ACT.Silu).then_inc(r_silu, 1)
                            act.wait_ge(r_ht, at)
                            act.activation(heTX.rearrange("p k t -> p (k t)"), ps[:, s, 0:FE], ACT.Copy).then_inc(r_hT, 1)
                            act.drain()
                        with act.Else():
                            act.sem_inc(r_xT, 1)
                            act.sem_inc(r_silu, 1)
                            act.sem_inc(r_hT, 1)
                        act.nop()
                    act.nop()
                with act.Else():
                    act.sem_inc(r_xT, ROUNDS - 1)
                    act.sem_inc(r_silu, ROUNDS - 1)
                    act.sem_inc(r_hT, ROUNDS - 1)
                act.nop()

            act.wait_ge(cnt_ready, 1)
            act.wait_ge(e_tr, 1)
            act.activation(xT[:, 0].rearrange("p k t -> p (k t)"), ps[:, 6:8, :].rearrange("p a b -> p (a b)"), ACT.Copy).then_inc(e_xT, 1)
            with act.Fori(0, PAIRS // 2 - 1) as turn2:
                q = 2 * turn2
                for s in range(2):
                    expert_pair(q + s, s)
            for s in range(2):
                expert_pair(PAIRS - 2 + s, s, last=s == 1)
            for b in range(NT):
                act.wait_ge(f_mix, b + 1)
                act.activation(yjunk, yo[:, b % 2, :], ACT.Square, accum_out=stat[:, 3, b:b + 1]).then_inc(f_ss, 1)
                act.wait_ge(f_var, b + 1)
                act.activation(stat[:, 5, b:b + 1], stat[:, 4, b:b + 1], ACT.Sqrt).then_inc(f_sd, 1)


        @block.vector
        def _(dve):
            landed(dve, "vt")
            dve.tensor_copy(wdw[:], pp("vt")[:, 0:CM * TAPS])
            free(dve.tensor_copy(vecT[:], pp("vt")[:, 512:512 + 17]), "vt")
            dve.wait_ge(ss_ready, NT)
            dve.tensor_scalar(stat[:, 1, :], stat[:, 0, :], 1.0 / D, EPS, ALU.mult, ALU.add).then_inc(var_ready, 1)
            dve.wait_ge(sd_ready, 1)
            dve.reciprocal(stat[:, 2, :], stat[:, 2, :])
            dve.drain()
            for b in range(NT):
                last = dve.tensor_scalar(xn[:, b, :], x[:, b, :], stat[:, 2, b:b + 1], None, ALU.mult)
            last.then_inc(xn_ready, 1)

            def ada_rows(n):
                a, c = ADA[n]
                name = f"ada{n}"
                landed(dve, name)
                free(dve.tensor_tensor(rows[:, a:a + c].rearrange("p n c -> p (n c)"), pp(name)[:, 0:c * P],
                                       rows[:, a:a + c].rearrange("p n c -> p (n c)"), ALU.add), name)
                dve.drain()
                if n == 0:
                    dve.scalar_tensor_tensor(rows[:, 2:4], rows[:, 2:4], 1.0, grow[:, 0:2], ALU.add, ALU.mult)
                elif n == 1:
                    dve.tensor_tensor(rows[:, 4:6], rows[:, 4:6], grow[:, 2:4], ALU.mult)
                elif n == 3:
                    dve.scalar_tensor_tensor(rows[:, 8:10], rows[:, 8:10], 1.0, grow[:, 4:6], ALU.add, ALU.mult)
                elif n == 4:
                    dve.tensor_tensor(rows[:, 10:12], rows[:, 10:12], grow[:, 6:8], ALU.mult)
                dve.drain().then_inc(rows_ready, 1)

            dve.wait_ge(brow_in, 16 * 10)
            ada_rows(0)
            dve.wait_ge(mod_in, 32)
            for k in range(1, KD, 2):
                name = f"tr{k}"
                landed(dve, name)
                dve.tensor_scalar(hT[:, k, TP:], pp(name)[:, 0:TS], modT[:, 1, 1, k:k + 1], modT[:, 1, 0, k:k + 1], ALU.mult, ALU.add)
                free(dve.tensor_scalar(hT[:, k, 0:TP], pp(name)[:, 512:512 + TP], modT[:, 0, 1, k:k + 1], modT[:, 0, 0, k:k + 1],
                                       ALU.mult, ALU.add), name)
            dve.drain().then_inc(hT_dve, 1)
            for m in range(CM):
                name = f"a{m}"
                dve.wait_ge(sg_ready, m + 1)
                landed(dve, name)
                dve.tensor_tensor(hc[:, m, HALF:HALF + TP], pp(name)[:, 512:512 + TP], sg[:, m % 2, 0:TP], ALU.mult)
                free(dve.tensor_tensor(hc[:, m, HALF + SAMP0:HALF + SAMP0 + TS], pp(name)[:, 0:TS], sg[:, m % 2, TP:], ALU.mult), name)
                ada_rows(m + 1)
            steps = [(m, tap) for m in range(CM) for tap in range(TAPS)]
            landed(dve, "a3")
            dve.wait_ge(hc_zero, 1)

            def conv(n):
                for _ in range(min(n, len(steps))):
                    m, tap = steps.pop(0)
                    w = wdw[:, m * TAPS + tap:m * TAPS + tap + 1]
                    src = hc[:, m, tap:tap + CONVW]
                    if tap == 0:
                        dve.tensor_scalar(acc[:, m, :], src, w, vecT[:, m:m + 1], ALU.mult, ALU.add)
                    else:
                        dve.scalar_tensor_tensor(acc[:, m, :], src, w, acc[:, m, :], ALU.mult, ALU.add)
                    dve.drain()
                    if not steps:
                        dve.drain().then_inc(conv_ready, 1)

            conv(2 * TAPS)
            emptied(dve, "stq")
            dve.reciprocal(rB[:, 0, :], rB[:, 0, :])
            dve.drain()
            for n in range(QM):
                dve.scalar_tensor_tensor(qa[:, n, :], qa[:, n, :], vecT[:, 3 * CM + n:3 * CM + n + 1], rB[:, 0, :], ALU.mult, ALU.mult)
            dve.drain().then_inc(qn_ready, 1)
            conv(8)
            landed(dve, "kr")
            dve.tensor_tensor(tk[:, TP:], pp("kr")[:, 0:TS], CS[:, TP:], ALU.mult)
            free(dve.tensor_tensor(tk[:, 0:TP], pp("kr")[:, 512:512 + TP], CS[:, 0:TP], ALU.mult), "kr")
            emptied(dve, "stkv")
            dve.reciprocal(rB[:, 1, :], rB[:, 1, :])
            dve.drain()
            for n in range(KM):
                g = vecT[:, 3 * CM + QM + n:3 * CM + QM + n + 1]
                dve.scalar_tensor_tensor(ck[:, n, TP + PAST:], ck[:, n, TP + PAST:], g, rB[:, 1, TP:], ALU.mult, ALU.mult)
                dve.scalar_tensor_tensor(ck[:, n, 0:TP], ck[:, n, 0:TP], g, rB[:, 1, 0:TP], ALU.mult, ALU.mult)
            dve.drain().then_inc(ckn_ready, 1)
            for h in range(H):
                name = f"qr{h}"
                conv(5)
                landed(dve, name)
                dve.tensor_tensor(qr[:, h, TP:], pp(name)[:, 0:TS], CS[:, TP:], ALU.mult)
                free(dve.tensor_tensor(qr[:, h, 0:TP], pp(name)[:, 512:512 + TP], CS[:, 0:TP], ALU.mult), name)
            dve.drain().then_inc(proj_dve, 1)
            for u in range(UNITS + 1):
                if u < UNITS:
                    w = T if u % NT < 4 else TP
                    landed(dve, f"S{u}")
                    dve.reduce_max(amax[:, 0, u:u + 1], pp(f"S{u}")[:, 0:w], AX.X)
                    dve.drain()
                    dve.tensor_scalar(amax[:, 1, u:u + 1], amax[:, 0, u:u + 1], -SCALE, None, ALU.mult).then_inc(max_ready, 1)
                if u >= 1:
                    n = u - 1
                    w = T if n % NT < 4 else TP
                    emptied(dve, f"S{n}")
                    dve.reciprocal(asum[:, 1, n:n + 1], asum[:, 0, n:n + 1])
                    dve.drain()
                    dve.tensor_scalar(pr[:, n % 2, 0:w], pr[:, n % 2, 0:w], asum[:, 1, n:n + 1], None, ALU.mult).then_inc(p_ready, 1)
                conv(2)
            conv(len(steps))
            landed(dve, "lnm")
            dve.memset(mB[:, TP:SAMP0], 0.0)
            dve.memset(sB[:, TP:SAMP0], 1.0)
            emptied(dve, "lnm")
            dve.drain()
            for m in range(CM):
                dve.tensor_tensor(acc[:, m, :], acc[:, m, :], mB, ALU.subtract).then_inc(cen_ready, 1)
            emptied(dve, "lnv")
            dve.reciprocal(sB, sB)
            dve.drain()
            for m in range(CM):
                dve.tensor_tensor(acc[:, m, :], acc[:, m, :], sB, ALU.mult).then_inc(lnn_ready, 1)
            dve.wait_ge(gg1_in, 32)
            dve.wait_ge(a2_in, 32)
            for b in range(NT + 2):
                if b < NT:
                    name = f"P{b}"
                    v = min(b, 1)
                    dve.wait_ge(pss, b + 1)
                    dve.tensor_scalar(stat[:, 4, b:b + 1], stat[:, 3, b:b + 1], 1.0 / D, EPS, ALU.mult, ALU.add).then_inc(pvar, 1)
                    dve.wait_ge(psd, b + 1)
                    dve.reciprocal(stat[:, 5, b:b + 1], stat[:, 5, b:b + 1])
                    dve.drain()
                    free(dve.scalar_tensor_tensor(po[:, b % 2, :], pp(name)[:, 0:D], stat[:, 5, b:b + 1], gg1[:, v, :], ALU.mult, ALU.mult), name)
                    dve.drain()
                    dve.tensor_tensor(x[:, b, :], x[:, b, :], po[:, b % 2, :], ALU.add).then_inc(x1_ready, 1)
                    dve.wait_ge(xss, b + 1)
                    dve.tensor_scalar(stat[:, 4, b:b + 1], stat[:, 6, b:b + 1], 1.0 / D, EPS, ALU.mult, ALU.add).then_inc(xvar, 1)
                    dve.wait_ge(xsd, b + 1)
                    dve.reciprocal(stat[:, 7, b:b + 1], stat[:, 7, b:b + 1])
                    dve.drain()
                    dve.scalar_tensor_tensor(h2[:, b % 2, :], x[:, b, :], stat[:, 7, b:b + 1], a2[:, v, :], ALU.mult, ALU.mult).then_inc(h2m_ready, 1)
                if b >= 2:
                    name = f"rl{b - 2}"
                    landed(dve, name)
                    free(dve.tensor_copy(L[:, b - 2, :], pp(name)[:, 0:G + E]), name)
            dve.drain()

            def wide(n):
                return rt[:, n, :].rearrange("p (t e) -> p t e", e=E)

            def narrow(n, m, k):
                return rt[:, n, k * NT * m:(k + 1) * NT * m].rearrange("p (t e) -> p t e", e=m)

            Lg, Le = L[:, :, 0:G], L[:, :, G:]
            em, eq, oh1, oh2, pos = (wide(n) for n in range(5))
            goh, geq, pen, m1, m2, top = (narrow(5, G, 0), narrow(5, G, 1), narrow(5, G, 2), narrow(5, 1, 60 // 5 + 4), narrow(5, 1, 20), narrow(5, 1, 24))
            den = narrow(5, 1, 28)
            rankg = cst[:, C_RANK:C_RANK + G].unsqueeze(1).broadcast_to([P, NT, G])
            ranke = cst[:, C_RANK + G:C_RANK + G + E].unsqueeze(1).broadcast_to([P, NT, E])

            def over(v, n):
                return v.broadcast_to([P, NT, n])

            def step(ins):
                dve.drain()

            def first_best(out, v, hit, best, rank, n):
                step(dve.tensor_reduce(best, v, AX.X, ALU.max))
                step(dve.tensor_tensor(hit, v, over(best, n), ALU.is_equal))
                step(dve.tensor_tensor(hit, hit, rank, ALU.mult))
                step(dve.tensor_reduce(top, hit, AX.X, ALU.max))
                step(dve.tensor_tensor(out, hit, over(top, n), ALU.is_equal))

            first_best(goh, Lg, geq, m1, rankg, G)
            dve.tensor_tensor(rt_e[:, :, 0:G], Lg, over(m1, G), ALU.subtract)
            step(dve.tensor_scalar(pen, goh, 1e30, -1e30, ALU.mult, ALU.add))
            for g in range(G):
                part_ = slice(g * EG, (g + 1) * EG)
                dve.tensor_tensor(em[:, :, part_], Le[:, :, part_], goh[:, :, g:g + 1].broadcast_to([P, NT, EG]), ALU.mult)
            dve.drain()
            for g in range(G):
                part_ = slice(g * EG, (g + 1) * EG)
                dve.tensor_tensor(em[:, :, part_], em[:, :, part_], pen[:, :, g:g + 1].broadcast_to([P, NT, EG]), ALU.add)
            dve.drain()
            first_best(oh1, em, eq, m1, ranke, E)
            step(dve.scalar_tensor_tensor(em, oh1, -2e30, em, ALU.mult, ALU.add))
            first_best(oh2, em, eq, m2, ranke, E)
            dve.tensor_tensor(rt_e[:, :, G:G + 1], m2, m1, ALU.subtract)
            dve.tensor_tensor(maskb[:], oh1, oh2, ALU.add)
            dve.drain().then_inc(mask_ready, 1)
            dve.sem_inc(rgmax, 1)
            dve.wait_ge(rexp, 1)
            dve.tensor_reduce(den, rt_e[:, :, 0:G], AX.X, ALU.add)
            step(dve.tensor_scalar(m1, rt_e[:, :, G:G + 1], 1.0, None, ALU.add))
            step(dve.tensor_tensor(den, den, m1, ALU.mult))
            step(dve.reciprocal(wsel[:, 0, :].unsqueeze(2), den))
            dve.tensor_tensor(wsel[:, 1, :].unsqueeze(2), rt_e[:, :, G:G + 1], wsel[:, 0, :].unsqueeze(2), ALU.mult)
            landed(dve, "pos")
            dve.tensor_copy(pos.rearrange("p t e -> p (t e)"), pp("pos")[:, 0:NT * E])
            free(dve.tensor_copy(rt[:, 6, 0:E], pp("pos")[:, 512:512 + E]), "pos")
            dve.drain()
            big = rt[:, 6, E:E + PAIRS]
            more = rt[:, 8, 0:PAIRS]
            sums = [rt[:, 8, (2 + n) * PAIRS:(3 + n) * PAIRS] for n in range(2)]
            shift = rt[:, 9, 0:E].rearrange("p (q j) -> p q j", j=2)
            step(dve.tensor_reduce(big.unsqueeze(2), rt[:, 6, 0:E].rearrange("p (q j) -> p q j", j=2), AX.X, ALU.max))
            step(dve.tensor_scalar(big, big, 1.0, -1.0, ALU.max, ALU.add))
            step(dve.tensor_copy(more_i[:], big))
            step(dve.tensor_scalar(more_i[:], more_i[:], 6, None, ALU.arith_shift_right))
            dve.tensor_copy(extra[:], more_i[0:1, :])
            step(dve.tensor_copy(more, more_i[:]))
            dve.memset(sums[0][:, 0:1], 0.0)
            step(dve.tensor_copy(sums[0][:, 1:], more[:, 0:PAIRS - 1]))
            for n, by in enumerate((1, 2, 4, 8)):
                src, dst = sums[n % 2], sums[1 - n % 2]
                dve.tensor_copy(dst[:, 0:by], src[:, 0:by])
                step(dve.tensor_tensor(dst[:, by:], src[:, by:], src[:, 0:PAIRS - by], ALU.add))
            before = sums[0]
            dve.tensor_copy(first[:], before[0:1, :])
            shift_c = cst[:, C_YB:C_YB + E].rearrange("p (q j) -> p q j", j=2)[:, :, 0]
            for j in range(2):
                dve.scalar_tensor_tensor(shift[:, :, j], shift_c, -1.0 / P, before, ALU.mult, ALU.add)
            dve.drain().then_inc(cnt_ready, 1)
            at = rt[:, 7, 0:2 * NT].rearrange("p (c t) -> p c t", c=2)
            base = rt[:, 7, 16:16 + 6 * NT].rearrange("p (a c t) -> p a c t", a=3, c=2)
            rnd = rt[:, 7, 64:64 + 2 * NT].rearrange("p (c t) -> p c t", c=2)
            late = rt[:, 7, 80:80 + 2 * NT].rearrange("p (c t) -> p c t", c=2)
            rnd_i = idx_r[:, 0:2 * NT].rearrange("p (c t) -> p c t", c=2)
            for c, oh in enumerate((oh1, oh2)):
                step(dve.tensor_tensor(eq, oh, pos, ALU.mult))
                step(dve.tensor_reduce(at[:, c, :].unsqueeze(2), eq, AX.X, ALU.add))
                for a, table in enumerate((cst[:, C_IDB:C_IDB + E], cst[:, C_YB:C_YB + E], rt[:, 9, 0:E])):
                    step(dve.tensor_tensor(eq, oh, table.unsqueeze(1).broadcast_to([P, NT, E]), ALU.mult))
                    step(dve.tensor_reduce(base[:, a, c, :].unsqueeze(2), eq, AX.X, ALU.add))
            step(dve.tensor_copy(rnd_i, at))
            step(dve.tensor_scalar(rnd_i, rnd_i, 6, None, ALU.arith_shift_right))
            step(dve.tensor_copy(rnd, rnd_i))
            for a, (per_at, per_round) in enumerate(((PAIRS, PAIRS * ROWS), (1, -ROWS))):
                step(dve.scalar_tensor_tensor(base[:, a], at, float(per_at), base[:, a], ALU.mult, ALU.add))
                step(dve.scalar_tensor_tensor(base[:, a], rnd, float(per_round), base[:, a], ALU.mult, ALU.add))
            step(dve.scalar_tensor_tensor(base[:, 2], base[:, 2], float(PAIRS - 1), rnd, ALU.add, ALU.add))
            step(dve.tensor_scalar(late, rnd, 1.0, float(P), ALU.min, ALU.mult))
            step(dve.tensor_tensor(base[:, 2], base[:, 2], late, ALU.mult))
            step(dve.tensor_tensor(base[:, 1], base[:, 1], base[:, 2], ALU.add))
            dve.tensor_copy(slot_i[:, 0], base[:, 0])
            dve.tensor_copy(slot_i[:, 1], base[:, 1])
            dve.drain().then_inc(idx_ready, 1)

            def expert_pair(pair, s, stored):
                dve.wait_ge(e_silu, pair + 1)
                dve.tensor_tensor(he[:, s, :], he[:, s, :], ps[:, s, FE:2 * FE], ALU.mult).then_inc(e_h, 1)
                dve.wait_ge(e_y, pair + 1)
                dve.wait_ge(y_st[s], stored)
                dve.tensor_copy(ys[:, s, :], ps[:, 2 + 2 * s:4 + 2 * s, :].rearrange("p a b -> p (a b)")).then_inc(e_ys, 1)
                n = dve.value_load(extra[0:1, bass.ds(pair, 1)], min_val=0, max_val=ROUNDS - 1)
                with dve.If(n > 0):
                    with dve.Fori(1, ROUNDS) as r:
                        with dve.If(n >= r):
                            at = dve.snap(pair * (ROUNDS - 1) + r)
                            dve.wait_ge(r_silu, at)
                            dve.tensor_tensor(heX, heX, ps[:, s, FE:2 * FE], ALU.mult).then_inc(r_h, 1)
                            dve.wait_ge(r_y, at)
                            dve.wait_ge(r_st, 16 * at)
                            dve.tensor_copy(ysX, ps[:, 2 + 2 * s:4 + 2 * s, :].rearrange("p a b -> p (a b)")).then_inc(r_ys, 1)
                            dve.drain()
                        with dve.Else():
                            dve.sem_inc(r_h, 1)
                            dve.sem_inc(r_ys, 1)
                        dve.nop()
                    dve.nop()
                with dve.Else():
                    dve.sem_inc(r_h, ROUNDS - 1)
                    dve.sem_inc(r_ys, ROUNDS - 1)
                dve.nop()

            dve.sem_inc(e_ys, 1)
            dve.sem_inc(r_ys, 1)
            with dve.Fori(0, PAIRS // 2) as turn2:
                q = 2 * turn2
                for s in range(2):
                    expert_pair(q + s, s, 8 * q + 16)
            dve.wait_ge(gg2_in, 32)
            for b in range(NT):
                dve.wait_ge(yg_in[b % 2], 32 * (b // 2 + 1))
                y0, y1, out = yg[:, 2 * (b % 2), :], yg[:, 2 * (b % 2) + 1, :], yo[:, b % 2, :]
                dve.tensor_scalar(out, y0, wsel[:, 0, b:b + 1], None, ALU.mult)
                dve.drain()
                dve.scalar_tensor_tensor(out, y1, wsel[:, 1, b:b + 1], out, ALU.mult, ALU.add).then_inc(f_mix, 1)
                dve.wait_ge(f_ss, b + 1)
                dve.tensor_scalar(stat[:, 4, b:b + 1], stat[:, 3, b:b + 1], 1.0 / D, EPS, ALU.mult, ALU.add).then_inc(f_var, 1)
                dve.wait_ge(f_sd, b + 1)
                dve.reciprocal(stat[:, 5, b:b + 1], stat[:, 5, b:b + 1])
                dve.drain()
                dve.scalar_tensor_tensor(out, out, stat[:, 5, b:b + 1], gg2[:, min(b, 1), :], ALU.mult, ALU.mult)
                dve.drain()
                dve.tensor_tensor(x[:, b, :], x[:, b, :], out, ALU.add).then_inc(f_out, 1)

        @block.tensor
        def _(pe):
            mm = nc.tensor.matmul

            def both(name, lhs, rhs_s, rhs_p, steps, width=TP):
                begin(pe, name)
                for k in range(steps):
                    mm(pp(name)[:, 0:TS], lhs(k), rhs_s(k), start=k == 0, stop=k == steps - 1)
                    last = mm(pp(name)[:, 512:512 + width], lhs(k), rhs_p(k), start=k == 0, stop=k == steps - 1)
                done(last, name)

            def turn(out, in_, n=P):
                return nc.tensor.transpose(out, in_, ident[0:n, 0:n])

            pe.wait_ge(cst_in, 16)
            pe.wait_ge(vec_in, 16 * 6)
            for m in range(CM):
                turn(pp("vt")[:, m * TAPS:(m + 1) * TAPS], wdrow[:, m * P:(m + 1) * P], TAPS)
            done(turn(pp("vt")[:, 512:512 + 17], vrow, 17), "vt")

            def ada(n):
                name = f"ada{n}"
                begin(pe, name)
                for c in range(ADA[n][0], sum(ADA[n])):
                    pe.wait_ge(ada_in[c % RING], 16 * (c // RING + 1))
                    at = (c - ADA[n][0]) * P
                    for k in range(KD):
                        for j in range(4):
                            last = mm(pp(name)[32 * j:32 * j + 32, at:at + P], csT[:, k, :], ring[:, c % RING, k, j * P:(j + 1) * P],
                                      start=k == 0, stop=k == KD - 1)
                    if c < sum(ADA[n]) - 1:
                        last.then_inc(ada_used, 1)
                done(last, name)
                pe.drain().then_inc(ada_used, 1)

            pe.wait_ge(cs_ready, 1)
            ada(0)
            pe.wait_ge(xn_ready, 1)
            for k in range(KD):
                name = f"tr{k}"
                begin(pe, name)
                for b in range(1, NT):
                    turn(pp(name)[:, (b - 1) * P:b * P], xn[:, b, k::KD])
                done(turn(pp(name)[:, 512:512 + TP], xn[:, 0, k::KD]), name)
            pe.wait_ge(hT_act, 1)
            pe.wait_ge(hT_dve, 1)
            pe.wait_ge(wc_in, 16)

            def project(name, lhs):
                both(name, lhs, lambda k: hT[:, k, TP:], lambda k: hT[:, k, 0:TP], KD)

            for m in range(CM):
                project(f"g{m}", lambda k: wC[:, k, C + m * P:C + (m + 1) * P])
                project(f"a{m}", lambda k: wC[:, k, m * P:(m + 1) * P])
                ada(m + 1)
            pe.wait_ge(wq_in, 16)

            def square_sum(name, first, count, width, src):
                begin(pe, name)
                for n in range(first, first + count):
                    mm(pp(name)[:, 0:TS], ones[:], src(n, 1), start=n == first, stop=n == first + count - 1)
                    last = mm(pp(name)[:, 512:512 + TP], ones[:], src(n, 0), start=n == first, stop=n == first + count - 1)
                done(last, name)

            def sq_part(n, sample):
                return sq[:, n, TP:] if sample else sq[:, n, 0:TP]

            def low_rank(n, name):
                project(name, lambda k: wQ[:, k, n * P:(n + 1) * P])

            for n, name in enumerate(("q0", "q1", "q2", "kv0")):
                low_rank(n, name)
            pe.wait_ge(sq_ready, QM)
            square_sum("stq", 0, QM, QL, sq_part)
            low_rank(4, "kv1")
            pe.wait_ge(wkr_ready, 1)
            project("kr", lambda k: wkr[:, k, :])
            pe.wait_ge(sq_ready, QM + KM)
            square_sum("stkv", QM, KM, KVL, sq_part)
            pe.wait_ge(cache_in, 48)
            begin(pe, "cache")
            turn(pp("cache")[:, 0:P], ckr)
            for m in range(KM):
                last = turn(pp("cache")[:, (1 + m) * P:(2 + m) * P], cckv[:, m * P:(m + 1) * P])
            done(last, "cache")
            emptied(pe, "kr")
            both("krdup", lambda k: dup, lambda k: tk[:, TP:], lambda k: tk[:, 0:TP], 1)
            pe.wait_ge(qn_ready, 1)
            pe.wait_ge(wuq_in, 16)
            pe.wait_ge(wqr_ready, 1)
            for h in range(H):
                for name, lhs in ((f"qn{h}", lambda k: wuq[:, k, h * (DN + DR):h * (DN + DR) + DN]),
                                  (f"qr{h}", lambda k: wqr[:, k * H + h, :])):
                    both(name, lhs, lambda k: qa[:, k, TP:], lambda k: qa[:, k, 0:TP], QM)
            pe.wait_ge(ckn_ready, 1)
            begin(pe, "state")
            for m in range(KM):
                turn(pp("state")[:, m * P:(m + 1) * P], ck[:, m, 0:TP])
            done(turn(pp("state")[:, KVL:KVL + DR], tk[0:DR, 0:TP], DR), "state")
            pe.wait_ge(cachekv_ready, 1)
            pe.wait_ge(wukv_in, 16)
            for h in range(H):
                both(f"k{h}", lambda k: wukv[:, k, h * (DN + DV):h * (DN + DV) + DN],
                     lambda k: ck[:, k, TP + PAST:], lambda k: ck[:, k, 0:TP + PAST], KM, TP + PAST)
            for t in range(KT):
                name = f"v{t}"
                begin(pe, name)
                for k in range(KM):
                    last = mm(pp(name)[:, 0:512], ck[:, k, t * P:(t + 1) * P],
                              wukv[:, k, :].rearrange("p (h c) -> p h c", h=H)[:, :, DN:], start=k == 0, stop=k == KM - 1)
                done(last, name)
            pe.wait_ge(proj_act, 1)
            pe.wait_ge(proj_dve, 1)
            for u in range(UNITS + 1):
                if u < UNITS:
                    h, q = divmod(u, NT)
                    name = f"S{u}"
                    begin(pe, name)
                    if q < 4:
                        cols, first = slice(TP + q * P, TP + (q + 1) * P), TP
                        parts = ((0, 512), (512, T))
                    else:
                        cols, first, parts = slice(0, TP), 0, ((0, TP),)
                    for m, (a, b, c) in enumerate(((qn, kn, h), (qr, None, h))):
                        for lo, hi in parts:
                            keys = kn[:, h, first + lo:first + hi] if m == 0 else kr[:, first + lo:first + hi]
                            last = mm(pp(name)[:, lo:hi], a[:, h, cols], keys, start=m == 0, stop=m == 1)
                    done(last, name)
                if u >= 1:
                    n = u - 1
                    h, q = divmod(n, NT)
                    name = f"T{n}"
                    begin(pe, name)
                    pe.wait_ge(p_ready, u)
                    for t in range(5 if q < 4 else 1):
                        last = turn(pp(name)[:, t * P:(t + 1) * P], pr[:, n % 2, t * P:(t + 1) * P])
                    done(last, name)
                    if q == 4:
                        name = f"O{h}"
                        begin(pe, name)
                        for m in range(u - NT, u):
                            emptied(pe, f"T{m}")
                        for t in range(5):
                            mm(pp(name)[:, 0:TS], vv[:, 1 + t, h * DV:(h + 1) * DV], pT[:, t, :], start=t == 0, stop=t == 4)
                        done(mm(pp(name)[:, 512:512 + TP], vv[:, 0, h * DV:(h + 1) * DV], pTp, start=True, stop=True), name)
            pe.wait_ge(conv_ready, 1)
            square_sum("lnm", 0, CM, C, lambda n, s: acc[:, n, SAMP0:] if s else acc[:, n, 0:TP])
            pe.wait_ge(lsq_ready, CM)
            square_sum("lnv", 0, CM, C, lambda n, s: lsq[:, n, TP:] if s else lsq[:, n, 0:TP])
            pe.wait_ge(mixc_ready, 1)
            for h in range(H):
                emptied(pe, f"O{h}")
            pe.wait_ge(wo_in, 16)
            pe.wait_ge(wr_ready, 1)
            for b in range(NT + 2):
                if b < NT:
                    name = f"P{b}"
                    begin(pe, name)
                    for k in range(KD):
                        for half in range(2):
                            last = mm(pp(name)[:, half * 512:(half + 1) * 512], mixT[:, k, b * P:(b + 1) * P],
                                      wo[:, k, half * 512:(half + 1) * 512], start=k == 0, stop=k == KD - 1)
                    done(last, name)
                if b >= 2:
                    n = b - 2
                    name = f"ht{n}"
                    begin(pe, name)
                    pe.wait_ge(h2_ready, n + 1)
                    for k in range(KD):
                        last = turn(pp(name)[:, k * P:(k + 1) * P], h2[:, n % 2, k::KD])
                    done(last, name)
                    name = f"rt{n}"
                    begin(pe, name)
                    emptied(pe, f"ht{n}")
                    for k in range(KD):
                        last = mm(pp(name)[0:G + E, 0:P], wr[:, k, :], h2T[:, k, :], start=k == 0, stop=k == KD - 1)
                    done(last, name)
                    name = f"rl{n}"
                    begin(pe, name)
                    emptied(pe, f"rt{n}")
                    done(turn(pp(name)[:, 0:G + E], lg, G + E), name)
            begin(pe, "pos")
            pe.wait_ge(mask_ready, 1)
            pe.wait_ge(small_ready, 1)
            for b in range(NT):
                for a in range(b + 1):
                    mm(pp("pos")[:, b * E:(b + 1) * E], trib[:] if a == b else onesb[:], maskb[:, a, :], start=a == 0, stop=a == b)
            for a in range(NT):
                last = mm(pp("pos")[:, 512:512 + E], onesb[:], maskb[:, a, :], start=a == 0, stop=a == NT - 1)
            done(last, "pos")

            for s in range(4):
                n = sum(1 for name in order if place[name][0] == s)
                pe.wait_ge(drained[s], n)

            def rows_to_columns(src, inc):
                for k in range(KD):
                    last = turn(ps[:, 6 + k // 4, (k % 4) * P:(k % 4 + 1) * P], src[:, k::KD])
                last.then_inc(inc, 1)

            def gate_up(s, src, inc):
                for k in range(KD):
                    for j in range(2):
                        a = j * ROWS
                        last = mm(ps[a:a + ROWS, s, :], src[:, k, a:a + ROWS], slots[s][:, j, 0:2, k * FE:(k + 1) * FE], start=k == 0, stop=k == KD - 1)
                last.then_inc(inc, 1)

            def hidden_to_columns(s, src, inc):
                for k in range(KF):
                    last = turn(ps[:, s, k * P:(k + 1) * P], src[:, k::KF])
                last.then_inc(inc, 1)

            def down(s, src, inc):
                for k in range(KF):
                    for half in range(2):
                        for j in range(2):
                            a = j * ROWS
                            last = mm(ps[a:a + ROWS, 2 + 2 * s + half, :], src[:, k, a:a + ROWS],
                                      slots[s][:, j, 2, k * D + half * 512:k * D + (half + 1) * 512], start=k == 0, stop=k == KF - 1)
                last.then_inc(inc, 1)

            def expert_pair(pair, s, loaded, gathered, last=False):
                for j in range(2):
                    pe.wait_ge(w_in_s[s][j], loaded)
                pe.wait_ge(e_xT, pair + 1)
                gate_up(s, xT[:, s], e_gu)
                if not last:
                    pe.wait_ge(xg_in[1 - s], gathered)
                    rows_to_columns(xg[:, 1 - s, :], e_tr)
                pe.wait_ge(e_h, pair + 1)
                hidden_to_columns(s, he[:, s, :], e_ht)
                pe.wait_ge(e_hT, pair + 1)
                pe.wait_ge(e_ys, pair + 1)
                down(s, heT[:, s], e_y)
                n = pe.value_load(extra[0:1, bass.ds(pair, 1)], min_val=0, max_val=ROUNDS - 1)
                with pe.If(n > 0):
                    with pe.Fori(1, ROUNDS) as r:
                        with pe.If(n >= r):
                            at = pe.snap(pair * (ROUNDS - 1) + r)
                            pe.wait_ge(r_xg, at)
                            pe.wait_ge(e_xT, pair + (1 if last else 2))
                            rows_to_columns(xgX, r_tr)
                            pe.wait_ge(r_xT, at)
                            gate_up(s, xTX, r_gu)
                            pe.wait_ge(r_h, at)
                            hidden_to_columns(s, heX, r_ht)
                            pe.wait_ge(r_hT, at)
                            pe.wait_ge(e_ys, pair + 2)
                            pe.wait_ge(r_ys, at)
                            down(s, heTX, r_y)
                            pe.drain()
                        with pe.Else():
                            for one in (r_tr, r_gu, r_ht, r_y):
                                pe.sem_inc(one, 1)
                        pe.nop()
                    pe.nop()
                with pe.Else():
                    for one in (r_tr, r_gu, r_ht, r_y):
                        pe.sem_inc(one, ROUNDS - 1)
                pe.drain().then_inc(w_used, 1)

            pe.wait_ge(cnt_ready, 1)
            pe.wait_ge(xg_in[0], 16)
            rows_to_columns(xg[:, 0, :], e_tr)
            with pe.Fori(0, PAIRS // 2 - 1) as turn2:
                q = 2 * turn2
                expert_pair(q, 0, 24 * q + 48, 8 * q + 16)
                expert_pair(q + 1, 1, 24 * q + 48, 8 * q + 32)
            expert_pair(PAIRS - 2, 0, 24 * PAIRS, 8 * PAIRS)
            expert_pair(PAIRS - 1, 1, 24 * PAIRS, 0, last=True)


_INS = ["x_prompt", "x_sample", "cache_ckv", "cache_krope", "c", "c_ctx", "w_ada", "b_ada", "g_pre1", "g_post1",
        "g_pre2", "g_post2", "w_in", "w_dw", "b_dw", "conv_ln_g", "conv_ln_b", "q_norm_g", "kv_norm_g", "w_uq",
        "w_ukv", "w_out", "w_rg", "b_rg", "w_re", "b_re", "w_gate", "w_up", "w_down"]
_OUTS = [(1, TP, D), (1, TS, D), (1, 1, TP, KVL), (1, 1, TP, DR)]


def kernel(**inputs):
    import concourse.bacc as _bacc
    from concourse.bass_utils import run_bass_kernel_spmd as _run

    nc = _bacc.Bacc("TRN2", target_bir_lowering=False, num_devices=1)
    arrays, ins = {}, {}
    for name in _INS:
        arrays[f"in_{name}"] = np.ascontiguousarray(inputs[name])
    arrays["in_consts"] = constants()
    for name, a in arrays.items():
        ins[name[3:]] = nc.dram_tensor(name, a.shape, F32, kind="ExternalInput").ap()
    outs = [nc.dram_tensor(f"out_{n}", shape, F32, kind="ExternalOutput").ap() for n, shape in enumerate(_OUTS)]
    hybrid_layer(nc, ins, outs)
    r = _run(nc, [arrays], core_ids=[0])
    return tuple(r.results[0][f"out_{n}"] for n in range(len(_OUTS)))
```

```python
from contextlib import ExitStack

import numpy as np

import concourse.bass as bass
from concourse import mybir

F32 = mybir.dt.float32
BF16 = mybir.dt.bfloat16
I32 = mybir.dt.int32
ALU = mybir.AluOpType
ACT = mybir.ActivationFunctionType
AX = mybir.AxisListType

P = 128
D = 1024
KD = D // P
TP, TS, PAST = 128, 512, 128
T = TP + TS
NT = T // P
NKEY = TP + PAST + TS
KT = NKEY // P
C = 512
CM = C // P
TAPS = 31
HALF = TAPS // 2
H, DN, DR, DV = 4, 128, 64, 128
QL, KVL = 384, 256
QM, KM = QL // P, KVL // P
QKR = QL + KVL + DR
SCALE = float(DN + DR) ** -0.5
EPS = 1e-6
G, EG, E = 4, 8, 32
FE = 256
KF = FE // P
ROWS = 64
ROUNDS = T // ROWS
PAIRS = E // 2
PAD = 4096
LOOPED = (PAIRS - 6) // 2
PADW = HALF + TP + HALF + TS + HALF
CONVW = PADW - 2 * HALF
SAMP0 = TP + HALF
CHUNK = 512
NCH = 6 * D // CHUNK
ADA = [(0, 4), (4, 2), (6, 2), (8, 2), (10, 2)]
RING = 3
UNITS = H * NT

C_ID, C_DUP, C_TRI, C_CS, C_RANK, C_IDB, C_TOK, C_EPS = 0, 128, 256, 384, 1024, 1060, 1092, 1102
C_N = 1103


def constants():
    t = np.zeros((P, C_N), np.float32)
    p = np.arange(P)
    t[:, C_ID:C_ID + P] = np.eye(P)
    t[:, C_DUP:C_DUP + P] = (p[:, None] % DR) == (p[None, :] % DR)
    t[:, C_TRI:C_TRI + P] = p[:, None] < p[None, :]
    t[:DR, C_CS:C_CS + TP] = 1.0
    tok = np.arange(TS)
    nf = DR // 4
    freqs = (np.float32(10000.0) ** (-np.arange(nf, dtype=np.float32) / nf)).astype(np.float32)
    for d in range(DR):
        place = (tok // 64 if d < DR // 2 else tok % 64).astype(np.float32)
        ang = (place * freqs[d % nf]).astype(np.float32)
        t[d, C_CS + TP:C_CS + T] = np.cos(ang)
        t[DR + d, C_CS + TP:C_CS + T] = np.sin(ang) * (-1.0 if d % 32 < nf else 1.0)
    t[:, C_RANK:C_RANK + G] = G - np.arange(G)
    t[:, C_RANK + G:C_RANK + G + E] = E - np.arange(E)
    e = np.arange(E)
    t[:, C_IDB:C_IDB + E] = (e % 2) * ROWS * PAIRS + e // 2
    t[:, C_TOK:C_TOK + 2 * NT] = np.arange(2 * NT)[None, :] * P + p[:, None]
    t[:, C_EPS] = EPS
    return t


LN_AT = {16: "lnm", 18: "lnv"}
POST = ["P0", "P1", "P2", "ht0", "P3", "rt0", "ht1", "P4", "rl0", "rt1", "ht2", "rl1", "rt2", "ht3", "rl2", "rt3",
        "ht4", "rl3", "rt4", "rl4"]


def pe_groups():
    names = ["ada0", "modt"] + [f"tr{k}" for k in range(KD)] + ["vt"]
    for m in range(CM):
        names += [f"g{m}", f"a{m}", f"ada{m + 1}"]
    names += ["q0", "q1", "q2", "kv0", "stq", "kv1", "kr", "stkv", "cache", "krdup"]
    for h in range(H):
        names += [f"qn{h}", f"qr{h}"]
    names += ["state"] + [f"k{h}" for h in range(H)] + [f"v{t}" for t in range(KT)]
    for u in range(UNITS + 1):
        if u < UNITS:
            names.append(f"S{u}")
        if u >= 1:
            names.append(f"T{u - 1}")
            if u in LN_AT:
                names.append(LN_AT[u])
            if u % NT == 0:
                names.append(f"O{u // NT - 1}")
    return names + POST + ["pos"]


def hybrid_layer(nc, i, outs):
    y_prompt, y_sample, state_ckv, state_krope = outs
    order = pe_groups()
    place = {name: (n % 4, n // 4) for n, name in enumerate(order)}

    with ExitStack() as ctx:
        def sb(name, shape, dt=F32):
            return ctx.enter_context(nc.sbuf_tensor(name, shape, dt))

        def sem(name):
            return ctx.enter_context(nc.semaphore(name))

        def dram(name, shape, dt=F32):
            return nc.dram_tensor(name, shape, dt, kind="Internal").ap()

        def part(t, at, *shape):
            n = int(np.prod(shape))
            v = t[:, at:at + n]
            if len(shape) == 4:
                return v.rearrange("p (a b c d) -> p a b c d", a=shape[0], b=shape[1], c=shape[2])
            if len(shape) == 2:
                return v.rearrange("p (a b) -> p a b", a=shape[0])
            if len(shape) == 3:
                return v.rearrange("p (a b c) -> p a b c", a=shape[0], b=shape[1])
            return v

        ada_d = dram("ada_d", (2, NCH, 4, P))
        h2_d = dram("h2_d", (T, D))
        ids_d = dram("ids_d", (ROUNDS * P * PAIRS, 1), I32)
        y_d = dram("y_d", (2 * T, D))

        x = sb("x", [P, NT, D])
        cst = sb("cst", [P, C_N])
        sizes = (RING * KD * CHUNK, KD * (2 * C + QKR), KD * T, 3 * 768 + 2 * 1024 + 3 * 512, 7936)
        arena = sb("arena", [P, sum(sizes)])
        R1, W, HM, QW, CQ = (arena[:, sum(sizes[:n]):sum(sizes[:n + 1])] for n in range(5))
        ones = sb("ones", [P, P])
        onesb = sb("onesb", [P, P], BF16)
        trib = sb("trib", [P, P], BF16)
        cT = sb("cT", [P, 2, KD])
        csT = sb("csT", [P, KD, 32])
        wr = sb("wr", [P, KD, G + E])
        rbias = sb("rbias", [G + E, 1])
        modT = sb("modT", [P, 4, 4, 2])
        stat = sb("stat", [P, 8, NT])
        vecT = sb("vecT", [P, 17])
        wdw = sb("wdw", [P, CM * TAPS])
        amax = sb("amax", [P, 2, UNITS])
        asum = sb("asum", [P, 2, UNITS])
        wsel = sb("wsel", [P, 2, NT])
        slot_i = sb("slot_i", [P, 2, NT], I32)
        tok_i = sb("tok_i", [P, 2, NT], I32)
        ids = sb("ids", [P, ROUNDS, PAIRS], I32)
        idg = sb("idg", [P, ROUNDS, PAIRS], I32)
        idx = sb("idx", [P, 6], I32)
        extra = sb("extra", [1, 2 * PAIRS], I32)
        idx_r = sb("idx_r", [P, 2 * NT], I32)

        x_rg = sb("x_rg", [P, KD, G])[:]
        x_re = sb("x_re", [P, KD, E])[:]

        ident = cst[:, C_ID:C_ID + P]
        dup = cst[:, C_DUP:C_DUP + P]
        CS = cst[:, C_CS:C_CS + T]
        eps = cst[:, C_EPS:C_EPS + 1]

        wC = part(W, 0, KD, 2 * C)
        wQ = part(W, KD * 2 * C, KD, QKR)
        acc = part(W, 0, CM, CONVW)
        o = CM * CONVW
        sq = part(W, o, 5, T)
        rB = part(W, o + 5 * T, 2, T)
        wkr = part(W, o + 7 * T, KD, P)
        assert o + 7 * T + KD * P <= KD * 2 * C
        wo = part(W, o, KD, D)
        ring = part(R1, 0, RING, KD, CHUNK)
        qn = part(R1, 0, H, T)
        qr = part(R1, 2560, H, T)
        kn = part(R1, 5120, H, NKEY)
        kr = part(R1, 8192, NKEY)
        vv = part(R1, 8960, KT, H * DV)
        wuq = part(QW, 0, QM, H * (DN + DR))
        wukv = part(QW, 2304, KM, H * (DN + DV))
        wqr = part(QW, 4352, QM * H, P)
        gg1 = part(QW, 0, 2, D)
        a2 = part(QW, 2048, 2, D)
        h2T = [part(QW, 4096, KD, P), part(W, CM * CONVW + KD * D, KD, P)]
        wdrow = QW[0:TAPS, 4352:4352 + C]
        vrow = QW[0:17, 4352 + C:4352 + C + P]
        hT = part(HM, 0, KD, T)
        mixT = hT
        xn = part(CQ, 0, NT, D)
        rows = part(CQ, NT * D, NCH, P)
        grow = part(CQ, NT * D + NCH * P, 8, P)
        hc = part(CQ, 0, CM, PADW)
        o = CM * PADW
        sg = part(CQ, o, 2, T)
        qa = part(CQ, o, QM, T)
        ck = part(CQ, o + QM * T, KM, NKEY)
        tk = part(CQ, o + QM * T + KM * NKEY, T)
        ckr = part(CQ, o + QM * T + KM * NKEY + T, P)
        cckv = part(CQ, o + QM * T + KM * NKEY + T + P, KVL)
        sto = part(CQ, o + QM * T + KM * NKEY + T + P + KVL, KVL + DR)
        assert o + QM * T + KM * NKEY + T + P + 2 * KVL + DR <= 7936
        pr = part(CQ, o, 2, T)
        pT = part(CQ, o + 2 * T, 5, TS)
        pTp = part(CQ, o + 2 * T + 5 * TS, P)
        lsq = part(HM, 0, CM, T)
        mB = part(QW, 5120, CONVW)
        sB = part(CQ, 2048, CONVW)
        b2 = part(CQ, 0, 2, D)
        po = part(CQ, o, 2, D)
        h2 = part(CQ, o + 2 * D, 2, D)
        lg = CQ[0:G + E, o + 4 * D:o + 4 * D + P]
        assert o + 4 * D + P <= 7936
        L = part(CQ, o + 4 * D + P, NT, G + E)
        rt = part(CQ, o, 12, NT * E)
        rt_e = rt[:, 11, 0:NT * (G + 1)].rearrange("p (t g) -> p t g", g=G + 1)
        maskb = sb("maskb", [P, NT, E], BF16)
        SLOT = 2 * 3 * KD * FE
        slots = [part(arena, n * SLOT, 2, 3, KD * FE) for n in range(3)]
        xg = part(CQ, 0, 2, D)
        xT = part(CQ, 2048, 2, KD, P)
        he = part(CQ, 4096, 2, FE)
        heT = part(CQ, 4096 + 2 * FE, 2, KF, P)
        ys = part(CQ, 5120, 2, D)
        gg2 = part(arena, SLOT, 2, D)
        yg = part(arena, SLOT + 2 * D, 2, NT, D)
        yo = part(arena, 2 * SLOT, 2, D)
        yjunk = part(arena, 2 * SLOT + 2 * D, D)

        ps = ctx.enter_context(nc.psum_tensor("ps", [P, 8, 512], F32))

        def pp(name):
            s = place[name][0]
            return ps[:, 2 * s:2 * s + 2, :].rearrange("p a b -> p (a b)")

        filled = [sem(f"filled{s}") for s in range(4)]
        drained = [sem(f"drained{s}") for s in range(4)]
        x_in = [sem(f"x_in{b}") for b in range(NT)]
        cst_in, cvec_in, vec_in, brow_in = sem("cst_in"), sem("cvec_in"), sem("vec_in"), sem("brow_in")
        ada_in = [sem(f"ada_in{s}") for s in range(RING)]
        ada_used = sem("ada_used")
        wc_in, wq_in, wuq_in, wukv_in = [sem(f"wc_in{m}") for m in range(CM)], sem("wq_in"), sem("wuq_in"), sem("wukv_in")
        cache_in, wr_in, wo_in = sem("cache_in"), sem("wr_in"), sem("wo_in")
        zeroed, cs_ready, wr_ready, small_ready = sem("zeroed"), sem("cs_ready"), sem("wr_ready"), sem("small_ready")
        ss_ready, var_ready, sd_ready, xn_ready = sem("ss_ready"), sem("var_ready"), sem("sd_ready"), sem("xn_ready")
        rows_ready, ada_st = sem("rows_ready"), [sem(f"ada_st{n}") for n in range(5)]
        hT_act, hT_dve = sem("hT_act"), sem("hT_dve")
        hc_zero, sg_ready = sem("hc_zero"), sem("sg_ready")
        wkr_ready, wqr_ready = sem("wkr_ready"), sem("wqr_ready")
        sq_ready, qn_ready, ckn_ready = sem("sq_ready"), sem("qn_ready"), sem("ckn_ready")
        cachekv_ready, state_out = sem("cachekv_ready"), sem("state_out")
        proj_act, proj_dve = sem("proj_act"), sem("proj_dve")
        max_ready, p_ready = sem("max_ready"), sem("p_ready")
        conv_n, cen_ready, lsq_ready, lnn_ready, mixc_ready = (
            sem("conv_n"), sem("cen_ready"), sem("lsq_ready"), sem("lnn_ready"), sem("mixc_ready"))
        gg1_in, a2_in, b2_in, gg2_in = sem("gg1_in"), sem("a2_in"), sem("b2_in"), sem("gg2_in")
        pss, pvar, psd, x1_ready, xss, xvar, xsd, h2m_ready = (
            sem("pss"), sem("pvar"), sem("psd"), sem("x1_ready"), sem("xss"), sem("xvar"), sem("xsd"), sem("h2m_ready"))
        h2_ready, h2_last = sem("h2_ready"), sem("h2_last")
        h2_st = [sem("h2_st0"), sem("h2_st1")]
        rgmax, rexp, mask_ready, idx_ready, cnt_ready, wsel_ready = sem("rgmax"), sem("rexp"), sem("mask_ready"), sem("idx_ready"), sem("cnt_ready"), sem("wsel_ready")
        ids_pad, ids_st, ids_in, more_in = sem("ids_pad"), sem("ids_st"), sem("ids_in"), sem("more_in")
        w_in_s = [[sem(f"w{s}{j}") for j in range(2)] for s in range(3)]
        w_used = sem("w_used")
        xg_in = [sem("xg_in0"), sem("xg_in1")]
        e_tr, e_xT, e_gu, e_silu, e_h, e_ht, e_hT, e_y, e_ys = (sem(n) for n in (
            "e_tr", "e_xT", "e_gu", "e_silu", "e_h", "e_ht", "e_hT", "e_y", "e_ys"))
        y_st = [sem("y_st0"), sem("y_st1")]
        r_dma, r_xg, r_tr, r_xT, r_gu, r_silu, r_h, r_ht, r_hT, r_y, r_ys, r_st = (sem(n) for n in (
            "r_dma", "r_xg", "r_tr", "r_xT", "r_gu", "r_silu", "r_h", "r_ht", "r_hT", "r_y", "r_ys", "r_st"))
        r_pair = sem("r_pair")
        yg_in, f_first, f_norm, f_mix, f_ss, f_var, f_sd, f_out, out_st = ([sem(f"yg_in{b}") for b in range(NT)], sem("f_first"), sem("f_norm"), sem("f_mix"), sem("f_ss"),
                                                          sem("f_var"), sem("f_sd"), [sem("f_out0"), sem("f_out1")], sem("out_st"))

        def begin(pe, name):
            s, use = place[name]
            if use:
                pe.wait_ge(drained[s], use)

        def done(ins, name):
            return ins.then_inc(filled[place[name][0]], 1)

        def landed(eng, name):
            s, use = place[name]
            eng.wait_ge(filled[s], use + 1)

        def free(ins, name):
            return ins.then_inc(drained[place[name][0]], 1)

        def emptied(eng, name):
            s, use = place[name]
            eng.wait_ge(drained[s], use + 1)

        def next_pair(pair):
            return pair if isinstance(pair, int) and pair == PAIRS - 1 else pair + 1

        def wait_from(eng, one, n):
            if not isinstance(n, int) or n > 0:
                eng.wait_ge(one, n)

        w_in_v = i["w_in"][0].rearrange("(k p) n -> p k n", p=P)
        ada_v = i["w_ada"][0].rearrange("(p k) (c n) -> c p k n", k=KD, n=CHUNK)
        ada_flat = ada_d.rearrange("v n j c -> v (n j c)")

        def bcast(v, vec):
            return ada_flat[v:v + 1, vec * D:(vec + 1) * D].broadcast_to([P, D])

        block = ctx.enter_context(nc.Block())

        @block.sync
        def _(sp):
            def ada_chunk(n):
                if n >= RING:
                    sp.wait_ge(ada_used, n - RING + 1)
                sp.dma_start(ring[:, n % RING], ada_v[n]).then_inc(ada_in[n % RING], 16)

            ada_chunk(0)
            for b in range(NT):
                src = i["x_prompt"][0] if b == 0 else i["x_sample"][0, (b - 1) * P:b * P, :]
                sp.dma_start(x[:, b, :], src).then_inc(x_in[b], 16)
            for n in range(1, 4):
                ada_chunk(n)
            for m in range(CM):
                for a in (C + m * P, m * P):
                    sp.dma_start(wC[:, :, a:a + P], w_in_v[:, :, a:a + P]).then_inc(wc_in[m], 16)
            sp.dma_start(wQ, w_in_v[:, :, 2 * C:]).then_inc(wq_in, 16)
            for n in range(4, 7):
                ada_chunk(n)
            sp.dma_start(wuq, i["w_uq"][0].rearrange("(k p) n -> p k n", p=P)).then_inc(wuq_in, 16)
            sp.dma_start(wukv, i["w_ukv"][0].rearrange("(k p) n -> p k n", p=P)).then_inc(wukv_in, 16)
            for n in range(7, NCH):
                ada_chunk(n)
            emptied(sp, "kr")
            landed(sp, "stkv")
            sp.wait_ge(qn_ready, 1)
            sp.wait_ge(ckn_ready, 1)
            sp.dma_start(wo, i["w_out"][0].rearrange("(k p) n -> p k n", p=P)).then_inc(wo_in, 16)
            landed(sp, "v5")
            sp.wait_ge(ada_st[1], 32)
            sp.wait_ge(ada_st[3], 32)
            for v in range(2):
                sp.dma_start(gg1[:, v, :], bcast(v, 2)).then_inc(gg1_in, 16)
                sp.dma_start(a2[:, v, :], bcast(v, 4)).then_inc(a2_in, 16)
            sp.wait_ge(conv_n, CM * TAPS)
            sp.wait_ge(ada_st[2], 32)
            for v in range(2):
                sp.dma_start(b2[:, v, :], bcast(v, 3)).then_inc(b2_in, 16)

            def load_pair(pair, s, earlier, before=None):
                for piece in range(6):
                    j, n = divmod(piece, 3)
                    if piece >= 2:
                        sp.wait_ge(w_in_s[s][piece % 2], 48 * earlier + 16 * (piece // 2))
                    elif before is not None:
                        sp.wait_ge(w_in_s[before[0]][piece % 2], 48 * before[1])
                    w, k = (("w_gate", KD), ("w_up", KD), ("w_down", KF))[n]
                    src = i[w][0][bass.ds(2 * pair + j, 1)].rearrange("e (p k) f -> p (e k f)", k=k)
                    sp.dma_start(slots[s][:, j, n, :], src).then_inc(w_in_s[s][piece % 2], 16)

            landed(sp, f"O{H - 1}")
            sp.wait_ge(ada_used, NCH)
            load_pair(0, 0, 0)
            for b in range(NT):
                if b < NT - 1:
                    sp.wait_ge(h2_ready, b + 1)
                else:
                    landed(sp, f"P{NT - 1}")
                    sp.wait_ge(mixc_ready, CM)
                    landed(sp, f"rt{NT - 2}")
                    load_pair(1, 1, 0)
                    sp.wait_ge(h2_last, 1)
                sp.dma_start(h2_d[b * P:(b + 1) * P, :], h2[:, b % 2, :]).then_inc(h2_st[b % 2], 16)
            landed(sp, f"rt{NT - 1}")
            load_pair(2, 2, 0, (1, 1))
            sp.wait_ge(w_used, 1)
            load_pair(PAIRS - 1, 0, 1, (2, 1))
            with sp.Fori(0, LOOPED) as turn2:
                for s in range(2):
                    pair = 2 * turn2 + 3 + s
                    sp.wait_ge(w_used, pair - 1)
                    load_pair(pair, 1 + s, turn2 + 1, (2 - s, turn2 + 1 + s))
            for pair in (PAIRS - 3, PAIRS - 2):
                sp.wait_ge(w_used, pair - 1)
                load_pair(pair, 2 - pair % 2, (pair - 1) // 2, (1 + pair % 2, pair // 2))
            sp.wait_ge(w_used, PAIRS - 2)
            sp.wait_ge(ada_st[4], 32)
            for v in range(2):
                sp.dma_start(gg2[:, v, :], bcast(v, 5)).then_inc(gg2_in, 16)
            for s in range(2):
                sp.wait_ge(y_st[s], 16 * PAIRS // 2)
            sp.wait_ge(r_pair, PAIRS)
            sp.wait_ge(w_used, PAIRS)
            for b in range(NT):
                for c in range(2):
                    sp.dma_start(yg[:, c, b, :], y_d[c * T + b * P:c * T + (b + 1) * P, :]).then_inc(yg_in[b], 16)
            for b in range(NT):
                last = b == NT - 1
                sp.wait_ge(f_out[last], 1 if last else b + 1)
                dst = y_prompt[0] if b == 0 else y_sample[0, (b - 1) * P:b * P, :]
                sp.dma_start(dst, x[:, b, :]).then_inc(out_st, 16)
            sp.wait_ge(out_st, 16 * NT)
            sp.wait_ge(state_out, 32)

        @block.gpsimd
        def _(gp):
            gp.memset(ones[:], 1.0)
            gp.memset(onesb[:], 1.0)
            gp.memset(csT[:], 0.0)
            gp.memset(ids[:], PAD)
            gp.memset(rows, 0.0)
            gp.memset(grow, 0.0).then_inc(zeroed, 1)
            gp.wait_ge(zeroed, 1)
            gp.dma_start(ids_d.rearrange("(p n) one -> p (n one)", p=P), ids[:].rearrange("p a b -> p (a b)")).then_inc(ids_pad, 16)
            bv = i["b_ada"][0].rearrange("(n j c) -> j n c", j=4, c=P)
            gains = (("g_pre1", 0), ("g_post1", 2), ("g_pre2", 4), ("g_post2", 6))
            for v in range(2):
                gp.dma_start(rows[v:v + 97:32], bv).then_inc(brow_in, 16)
                for name, at in gains:
                    gp.dma_start(grow[v:v + 97:32, at:at + 2], i[name][0].rearrange("(n j c) -> j n c", j=4, c=P)).then_inc(brow_in, 16)
            gp.wait_ge(cst_in, 16)
            gp.tensor_copy(trib[:], cst[:, C_TRI:C_TRI + P])
            gp.tensor_copy(tok_i[:].rearrange("p c t -> p (c t)"), cst[:, C_TOK:C_TOK + 2 * NT]).then_inc(small_ready, 1)

            def put_rows(n):
                gp.wait_ge(rows_ready, n + 1)
                a, c = ADA[n]
                for v in range(2):
                    gp.dma_start(ada_d[v, a:a + c].rearrange("n j c -> j n c"), rows[v:v + 97:32, a:a + c]).then_inc(ada_st[n], 16)

            landed(gp, "tr7")
            for a, n in ((0, HALF), (HALF + TP, HALF), (PADW - HALF, HALF)):
                last = gp.memset(hc[:, :, a:a + n], 0.0)
            last.then_inc(hc_zero, 1)
            gp.wait_ge(wr_in, 64)
            gp.tensor_copy(wr[:, :, 0:G], x_rg)
            gp.tensor_copy(wr[:, :, G:], x_re).then_inc(wr_ready, 1)
            for n in range(1, 3):
                put_rows(n)
            landed(gp, "a3")
            gp.wait_ge(wq_in, 16)
            krw = wQ[:, :, QL + KVL:]
            gp.tensor_copy(wkr[:, :, 0:DR], krw)
            for half in range(2):
                dst = wkr[:, :, DR:].rearrange("p k (b h c) -> p k b h c", b=2, h=2)[:, :, :, half, :]
                src = krw.rearrange("p k (b h c) -> p k b h c", b=2, h=2)[:, :, :, 1 - half, :]
                last = gp.tensor_copy(dst, src)
            last.then_inc(wkr_ready, 1)
            gp.wait_ge(wuq_in, 16)
            qrw = wuq.rearrange("p k (h c) -> p (k h) c", h=H)[:, :, DN:]
            gp.tensor_copy(wqr[:, :, 0:DR], qrw)
            for half in range(2):
                dst = wqr[:, :, DR:].rearrange("p k (b h c) -> p k b h c", b=2, h=2)[:, :, :, half, :]
                src = qrw.rearrange("p k (b h c) -> p k b h c", b=2, h=2)[:, :, :, 1 - half, :]
                last = gp.tensor_copy(dst, src)
            last.then_inc(wqr_ready, 1)
            for n in range(3, 5):
                put_rows(n)
            for n in range(1, 5):
                gp.wait_ge(ada_st[n], 32)
            for n in range(2):
                gp.dma_start(ckr[:, n * DR:(n + 1) * DR], i["cache_krope"][0, 0]).then_inc(cache_in, 16)
            gp.dma_start(cckv, i["cache_ckv"][0, 0]).then_inc(cache_in, 16)
            gp.wait_ge(b2_in, 32)
            for b in range(NT - 1):
                gp.wait_ge(h2m_ready, b + 1)
                gp.tensor_tensor(h2[:, b % 2, :], h2[:, b % 2, :], b2[:, min(b, 1), :], ALU.add).then_inc(h2_ready, 1)
            gp.wait_ge(idx_ready, 1)
            gp.wait_ge(ids_pad, 16)
            for b in range(NT):
                for c in range(2):
                    gp.indirect_dma_start(ids_d, bass.IndirectOffsetOnAxis(slot_i[:, c, b:b + 1], 0),
                                          tok_i[:, c, b:b + 1], None).then_inc(ids_st, 16)
            gp.wait_ge(ids_st, 16 * 2 * NT)
            ids_v = ids_d.rearrange("(r p q) one -> p r (q one)", r=ROUNDS, q=PAIRS)
            gp.dma_start(ids[:, 0:1], ids_v[:, 0:1]).then_inc(ids_in, 16)
            gp.dma_start(ids[:, 1:], ids_v[:, 1:]).then_inc(more_in, 16)

            def token_rows(a, b):
                gp.tensor_scalar(idg[:, a:b], ids[:, a:b], float(T), float(T), ALU.is_ge, ALU.mult)
                gp.drain()
                gp.tensor_tensor(idg[:, a:b], ids[:, a:b], idg[:, a:b], ALU.subtract)
                gp.drain()

            flat_ids, flat_idg = (t[:].rearrange("p a b -> p (a b)") for t in (ids, idg))

            def gather(dst, at, n, inc):
                gp.tensor_copy(idx[:, n:n + 1], flat_idg[:, bass.ds(at, 1)])
                gp.drain()
                gp.indirect_dma_start(dst, None, h2_d, bass.IndirectOffsetOnAxis(idx[:, n:n + 1], 0),
                                      bounds_check=T - 1, oob_is_err=False).then_inc(inc, 16)

            def scatter(src, at, n, inc):
                gp.tensor_copy(idx[:, n:n + 1], flat_ids[:, bass.ds(at, 1)])
                gp.drain()
                gp.indirect_dma_start(y_d, bass.IndirectOffsetOnAxis(idx[:, n:n + 1], 0), src, None,
                                      bounds_check=2 * T - 1, oob_is_err=False).then_inc(inc, 16)

            gp.wait_ge(ids_in, 16)
            token_rows(0, 1)
            gp.wait_ge(h2_st[0], 16 * 3)
            gp.wait_ge(h2_st[1], 16 * 2)
            gp.wait_ge(cnt_ready, 1)
            for s in range(2):
                gather(xg[:, s, :], s, s, xg_in[s])
            gp.wait_ge(more_in, 16)
            token_rows(1, ROUNDS)
            gp.sem_inc(r_st, 1)

            def expert_pair(pair, s, stored, ahead=True):
                if ahead:
                    gp.wait_ge(e_tr, pair + 1)
                    gather(xg[:, s, :], pair + 2, s, xg_in[s])
                gp.wait_ge(e_ys, pair + 1)
                wait_from(gp, y_st[s], stored)
                scatter(ys[:, s, :], pair, 2 + s, y_st[s])
                n = gp.value_load(extra[0:1, bass.ds(pair, 1)], min_val=0, max_val=ROUNDS - 1)
                with gp.If(n > 0):
                    before = gp.value_load(extra[0:1, bass.ds(pair + PAIRS, 1)], min_val=0, max_val=PAIRS * (ROUNDS - 1))
                    with gp.Fori(1, n + 1) as r:
                        at = gp.snap(before + r)
                        gp.wait_ge(e_tr, next_pair(pair) + 1)
                        gp.wait_ge(r_st, at)
                        gather(xg[:, 1 - s, :], r * PAIRS + pair, 4, r_dma)
                        gp.drain().then_inc(r_xg, 1)
                        gp.wait_ge(r_ys, at + 1)
                        scatter(ys[:, s, :], r * PAIRS + pair, 5, r_dma)
                        gp.drain().then_inc(r_st, 1)
                gp.sem_inc(r_pair, 1)

            for pair in range(3):
                expert_pair(pair, pair % 2, 16 * (pair // 2))
            with gp.Fori(0, LOOPED) as turn2:
                for s in range(2):
                    expert_pair(2 * turn2 + 3 + s, 1 - s, 16 * turn2 + 16 * (1 + s))
            for pair in range(PAIRS - 3, PAIRS):
                expert_pair(pair, pair % 2, 16 * (pair // 2), ahead=pair + 2 < PAIRS)
            for b in range(NT - 1):
                gp.wait_ge(f_norm, b + 1)
                gp.tensor_tensor(x[:, b, :], x[:, b, :], yo[:, b % 2, :], ALU.add).then_inc(f_out[0], 1)

        def rms(act, name, n, scale):
            landed(act, name)
            act.activation(rB[:, n, TP:], pp(name)[:, 0:TS], ACT.Sqrt, bias=eps, scale=scale)
            free(act.activation(rB[:, n, 0:TP], pp(name)[:, 512:512 + TP], ACT.Sqrt, bias=eps, scale=scale), name)

        def shift1(k, v):
            return modT[:, k // 4, k % 4, v:v + 1]

        def scale1(k, v):
            return modT[:, 2 + k // 4, k % 4, v:v + 1]

        @block.scalar
        def _(act):
            act.dma_start(cst[:], i["consts"]).then_inc(cst_in, 16)
            act.dma_start(cT[:, 0, :], i["c_ctx"].rearrange("(p k) -> p k", k=KD)).then_inc(cvec_in, 16)
            act.dma_start(cT[:, 1, :], i["c"][0].rearrange("(p k) -> p k", k=KD)).then_inc(cvec_in, 16)
            act.dma_start(wdrow, i["w_dw"][0]).then_inc(vec_in, 16)
            at = 0
            for name in ("b_dw", "conv_ln_g", "conv_ln_b", "q_norm_g", "kv_norm_g"):
                n = i[name].shape[1] // P
                act.dma_start(vrow[at:at + n], i[name][0].rearrange("(m p) -> m p", p=P)).then_inc(vec_in, 16)
                at += n
            act.wait_ge(cvec_in, 32)
            act.wait_ge(zeroed, 1)
            for v in range(2):
                last = act.activation(csT[:, :, v], cT[:, v, :], ACT.Silu)
            last.then_inc(cs_ready, 1)
            for b in range(NT):
                act.wait_ge(x_in[b], 16)
                act.activation(xn[:, b, :], x[:, b, :], ACT.Square, accum_out=stat[:, 0, b:b + 1]).then_inc(ss_ready, 1)
            act.wait_ge(var_ready, 1)
            act.activation(stat[:, 2, :], stat[:, 1, :], ACT.Sqrt).then_inc(sd_ready, 1)
            act.dma_start(rbias[0:G], i["b_rg"][0].rearrange("(e one) -> e one", one=1)).then_inc(wr_in, 16)
            act.dma_start(rbias[G:G + E], i["b_re"][0].rearrange("(e one) -> e one", one=1)).then_inc(wr_in, 16)
            act.dma_start(x_rg, i["w_rg"][0].rearrange("(p k) e -> p k e", k=KD)).then_inc(wr_in, 16)
            act.dma_start(x_re, i["w_re"][0].rearrange("(p k) e -> p k e", k=KD)).then_inc(wr_in, 16)
            emptied(act, "modt")
            for k in range(0, KD, 2):
                name = f"tr{k}"
                landed(act, name)
                act.activation(hT[:, k, TP:], pp(name)[:, 0:TS], ACT.Identity, bias=shift1(k, 1), scale=scale1(k, 1))
                free(act.activation(hT[:, k, 0:TP], pp(name)[:, 512:512 + TP], ACT.Identity, bias=shift1(k, 0), scale=scale1(k, 0)), name)
            act.drain().then_inc(hT_act, 1)
            for m in range(CM):
                name = f"g{m}"
                landed(act, name)
                if m >= 2:
                    emptied(act, f"a{m - 2}")
                elif m == 0:
                    act.wait_ge(hc_zero, 1)
                act.activation(sg[:, m % 2, 0:TP], pp(name)[:, 512:512 + TP], ACT.Sigmoid)
                free(act.activation(sg[:, m % 2, TP:], pp(name)[:, 0:TS], ACT.Sigmoid), name)
                act.drain().then_inc(sg_ready, 1)
            emptied(act, f"a{CM - 1}")
            for n in range(1, 5):
                act.wait_ge(ada_st[n], 32)
            landed(act, "a3")
            for n, name in enumerate(("q0", "q1", "q2", "kv0", "kv1")):
                landed(act, name)
                g = pp(name)
                if n < QM:
                    act.activation(qa[:, n, TP:], g[:, 0:TS], ACT.Copy)
                    act.activation(qa[:, n, 0:TP], g[:, 512:512 + TP], ACT.Copy)
                else:
                    act.activation(ck[:, n - QM, TP + PAST:], g[:, 0:TS], ACT.Copy)
                    act.activation(ck[:, n - QM, 0:TP], g[:, 512:512 + TP], ACT.Copy)
                act.activation(sq[:, n, TP:], g[:, 0:TS], ACT.Square)
                free(act.activation(sq[:, n, 0:TP], g[:, 512:512 + TP], ACT.Square), name)
                act.drain().then_inc(sq_ready, 1)
                if n == 3:
                    rms(act, "stq", 0, 1.0 / QL)
            rms(act, "stkv", 1, 1.0 / KVL)
            landed(act, "cache")
            act.activation(kr[:, TP:TP + PAST], pp("cache")[:, 0:P], ACT.Copy)
            for m in range(KM):
                last = act.activation(ck[:, m, TP:TP + PAST], pp("cache")[:, (1 + m) * P:(2 + m) * P], ACT.Copy)
            free(last, "cache")
            act.drain().then_inc(cachekv_ready, 1)
            landed(act, "krdup")
            act.activation(kr[:, TP + PAST:], pp("krdup")[:, 0:TS], ACT.Copy)
            free(act.activation(kr[:, 0:TP], pp("krdup")[:, 512:512 + TP], ACT.Copy), "krdup")
            for h in range(H):
                name = f"qn{h}"
                landed(act, name)
                act.activation(qn[:, h, TP:], pp(name)[:, 0:TS], ACT.Copy)
                free(act.activation(qn[:, h, 0:TP], pp(name)[:, 512:512 + TP], ACT.Copy), name)
            landed(act, "state")
            free(act.activation(sto, pp("state")[:, 0:KVL + DR], ACT.Copy), "state")
            emptied(act, "state")
            act.dma_start(state_ckv[0, 0], sto[:, 0:KVL]).then_inc(state_out, 16)
            act.dma_start(state_krope[0, 0], sto[:, KVL:]).then_inc(state_out, 16)
            for h in range(H):
                name = f"k{h}"
                landed(act, name)
                act.activation(kn[:, h, TP + PAST:], pp(name)[:, 0:TS], ACT.Copy)
                free(act.activation(kn[:, h, 0:TP + PAST], pp(name)[:, 512:512 + TP + PAST], ACT.Copy), name)
            for t in range(KT):
                name = f"v{t}"
                landed(act, name)
                free(act.activation(vv[:, t, :], pp(name)[:, 0:512], ACT.Copy), name)
            act.drain().then_inc(proj_act, 1)
            act.wait_ge(state_out, 32)
            def ln_act(u):
                if u == 16:
                    landed(act, "lnm")
                    act.activation(mB[:, SAMP0:], pp("lnm")[:, 0:TS], ACT.Copy, scale=1.0 / C)
                    free(act.activation(mB[:, 0:TP], pp("lnm")[:, 512:512 + TP], ACT.Copy, scale=1.0 / C), "lnm")
                elif u == 17:
                    for m in range(CM):
                        act.wait_ge(cen_ready, m + 1)
                        act.activation(lsq[:, m, TP:], acc[:, m, SAMP0:], ACT.Square)
                        act.activation(lsq[:, m, 0:TP], acc[:, m, 0:TP], ACT.Square).then_inc(lsq_ready, 1)
                elif u == 18:
                    landed(act, "lnv")
                    act.activation(sB[:, SAMP0:], pp("lnv")[:, 0:TS], ACT.Sqrt, bias=eps, scale=1.0 / C)
                    free(act.activation(sB[:, 0:TP], pp("lnv")[:, 512:512 + TP], ACT.Sqrt, bias=eps, scale=1.0 / C), "lnv")
                elif u == 20:
                    for m in range(CM):
                        act.wait_ge(lnn_ready, m + 1)
                        g, bb = vecT[:, CM + m:CM + m + 1], vecT[:, 2 * CM + m:2 * CM + m + 1]
                        act.activation(mixT[:, m, TP:], acc[:, m, SAMP0:], ACT.Silu, bias=bb, scale=g)
                        act.activation(mixT[:, m, 0:TP], acc[:, m, 0:TP], ACT.Silu, bias=bb, scale=g).then_inc(mixc_ready, 1)

            for u in range(UNITS + 1):
                if u < UNITS:
                    w = T if u % NT < 4 else TP
                    act.wait_ge(max_ready, u + 1)
                    if u >= 2:
                        landed(act, f"T{u - 2}")
                    free(act.activation(pr[:, u % 2, 0:w], pp(f"S{u}")[:, 0:w], ACT.Exp, bias=amax[:, 1, u:u + 1],
                                        scale=SCALE, accum_out=asum[:, 0, u:u + 1]), f"S{u}")
                if u >= 1:
                    n = u - 1
                    name = f"T{n}"
                    landed(act, name)
                    if n >= NT and n % NT == 0:
                        landed(act, f"O{n // NT - 1}")
                    if n % NT < 4:
                        q = n % NT
                        src = pp(name)[:, 0:T].rearrange("p (t q) -> p t q", q=P)
                        free(act.activation(pT[:, :, q * P:(q + 1) * P], src, ACT.Copy), name)
                    else:
                        free(act.activation(pTp, pp(name)[:, 0:P], ACT.Copy), name)
                        h = n // NT
                        landed(act, f"O{h}")
                        act.activation(mixT[:, CM + h, TP:], pp(f"O{h}")[:, 0:TS], ACT.Copy)
                        free(act.activation(mixT[:, CM + h, 0:TP], pp(f"O{h}")[:, 512:512 + TP], ACT.Copy), f"O{h}")
                ln_act(u)
            for name in POST:
                kind, b = name[:-1], int(name[-1])
                if kind == "P":
                    landed(act, name)
                    if b >= 2:
                        act.wait_ge(x1_ready, b - 1)
                    act.activation(po[:, b % 2, :], pp(name)[:, 0:D], ACT.Square, accum_out=stat[:, 3, b:b + 1]).then_inc(pss, 1)
                    act.wait_ge(pvar, b + 1)
                    act.activation(stat[:, 5, b:b + 1], stat[:, 4, b:b + 1], ACT.Sqrt).then_inc(psd, 1)
                    act.wait_ge(x1_ready, b + 1)
                    if b >= 2:
                        act.wait_ge(h2_st[b % 2], 16 * (b // 2))
                        landed(act, f"ht{b - 2}")
                    act.activation(h2[:, b % 2, :], x[:, b, :], ACT.Square, accum_out=stat[:, 6, b:b + 1]).then_inc(xss, 1)
                    act.wait_ge(xvar, b + 1)
                    act.activation(stat[:, 7, b:b + 1], stat[:, 4, b:b + 1], ACT.Sqrt).then_inc(xsd, 1)
                elif kind == "ht":
                    landed(act, name)
                    if b >= 2:
                        landed(act, f"rt{b - 2}")
                    free(act.activation(h2T[b % 2].rearrange("p k t -> p (k t)"), pp(name), ACT.Copy), name)
                elif kind == "rt":
                    landed(act, name)
                    if b:
                        landed(act, f"rl{b - 1}")
                    free(act.activation(lg, pp(name)[0:G + E, 0:P], ACT.Identity, bias=rbias[:]), name)
            act.wait_ge(rgmax, 1)
            act.activation(rt_e, rt_e, ACT.Exp).then_inc(rexp, 1)

            def columns_out(dst, bank, count):
                return act.activation(dst.rearrange("p k t -> p (k t)"), bank.rearrange("p a b -> p (a b)")[:, 0:count], ACT.Copy)

            def expert_pair(pair, s, last=False):
                act.wait_ge(e_gu, pair + 1)
                act.activation(he[:, s, :], ps[:, s, 0:FE], ACT.Silu).then_inc(e_silu, 1)
                if not last:
                    act.wait_ge(e_tr, pair + 2)
                    columns_out(xT[:, 1 - s], ps[:, 6:8, :], D).then_inc(e_xT, 1)
                act.wait_ge(e_ht, pair + 1)
                columns_out(heT[:, s], ps[:, s:s + 1, :], FE).then_inc(e_hT, 1)
                n = act.value_load(extra[0:1, bass.ds(pair, 1)], min_val=0, max_val=ROUNDS - 1)
                with act.If(n > 0):
                    before = act.value_load(extra[0:1, bass.ds(pair + PAIRS, 1)], min_val=0, max_val=PAIRS * (ROUNDS - 1))
                    with act.Fori(1, n + 1) as r:
                        at = act.snap(before + r)
                        act.wait_ge(r_tr, at)
                        columns_out(xT[:, s], ps[:, 6:8, :], D).then_inc(r_xT, 1)
                        act.wait_ge(r_gu, at)
                        act.activation(he[:, s, :], ps[:, s, 0:FE], ACT.Silu).then_inc(r_silu, 1)
                        act.wait_ge(r_ht, at)
                        columns_out(heT[:, s], ps[:, s:s + 1, :], FE).then_inc(r_hT, 1)

            act.wait_ge(wsel_ready, 1)
            act.wait_ge(e_tr, 1)
            columns_out(xT[:, 0], ps[:, 6:8, :], D).then_inc(e_xT, 1)
            for pair in range(3):
                expert_pair(pair, pair % 2)
            with act.Fori(0, LOOPED) as turn2:
                for s in range(2):
                    expert_pair(2 * turn2 + 3 + s, 1 - s)
            for pair in range(PAIRS - 3, PAIRS):
                expert_pair(pair, pair % 2, last=pair == PAIRS - 1)
            def norm_sum(b):
                act.wait_ge(f_mix, b + 1)
                act.activation(yjunk, yg[:, 1, b, :], ACT.Square, accum_out=stat[:, 3, b:b + 1]).then_inc(f_ss, 1)
                act.wait_ge(f_var, b + 1)
                act.activation(stat[:, 5, b:b + 1], stat[:, 4, b:b + 1], ACT.Sqrt).then_inc(f_sd, 1)

            for b in range(NT):
                act.wait_ge(yg_in[b], 32)
                act.activation(yg[:, 0, b, :], yg[:, 0, b, :], ACT.Copy, scale=wsel[:, 0, b:b + 1]).then_inc(f_first, 1)
                if b:
                    norm_sum(b - 1)
            norm_sum(NT - 1)

        @block.vector
        def _(dve):
            dve.wait_ge(ss_ready, NT)
            dve.tensor_scalar(stat[:, 1, :], stat[:, 0, :], 1.0 / D, EPS, ALU.mult, ALU.add).then_inc(var_ready, 1)
            dve.wait_ge(sd_ready, 1)
            dve.reciprocal(stat[:, 2, :], stat[:, 2, :])
            dve.drain()
            for b in range(NT):
                last = dve.tensor_scalar(xn[:, b, :], x[:, b, :], stat[:, 2, b:b + 1], None, ALU.mult)
            last.then_inc(xn_ready, 1)

            def ada_rows(n):
                a, c = ADA[n]
                name = f"ada{n}"
                landed(dve, name)
                free(dve.tensor_tensor(rows[:, a:a + c].rearrange("p n c -> p (n c)"), pp(name)[:, 0:c * P],
                                       rows[:, a:a + c].rearrange("p n c -> p (n c)"), ALU.add), name)
                dve.drain()
                if n == 0:
                    dve.scalar_tensor_tensor(rows[:, 2:4], rows[:, 2:4], 1.0, grow[:, 0:2], ALU.add, ALU.mult)
                elif n == 1:
                    dve.tensor_tensor(rows[:, 4:6], rows[:, 4:6], grow[:, 2:4], ALU.mult)
                elif n == 3:
                    dve.scalar_tensor_tensor(rows[:, 8:10], rows[:, 8:10], 1.0, grow[:, 4:6], ALU.add, ALU.mult)
                elif n == 4:
                    dve.tensor_tensor(rows[:, 10:12], rows[:, 10:12], grow[:, 6:8], ALU.mult)
                dve.drain().then_inc(rows_ready, 1)

            dve.wait_ge(brow_in, 16 * 10)
            ada_rows(0)
            landed(dve, "modt")
            turned = pp("modt")[:, 0:512].rearrange("p (n j c) -> p n j c", n=4, j=4)[:, :, :, 0:2]
            free(dve.tensor_copy(modT[:], turned), "modt")
            dve.drain()
            for k in range(1, KD, 2):
                name = f"tr{k}"
                landed(dve, name)
                dve.tensor_scalar(hT[:, k, TP:], pp(name)[:, 0:TS], scale1(k, 1), shift1(k, 1), ALU.mult, ALU.add)
                free(dve.tensor_scalar(hT[:, k, 0:TP], pp(name)[:, 512:512 + TP], scale1(k, 0), shift1(k, 0), ALU.mult, ALU.add), name)
            dve.drain().then_inc(hT_dve, 1)
            landed(dve, "vt")
            dve.tensor_copy(wdw[:], pp("vt")[:, 0:CM * TAPS])
            free(dve.tensor_copy(vecT[:], pp("vt")[:, 512:512 + 17]), "vt")
            for m in range(CM):
                name = f"a{m}"
                dve.wait_ge(sg_ready, m + 1)
                landed(dve, name)
                dve.tensor_tensor(hc[:, m, HALF:HALF + TP], pp(name)[:, 512:512 + TP], sg[:, m % 2, 0:TP], ALU.mult)
                free(dve.tensor_tensor(hc[:, m, HALF + SAMP0:HALF + SAMP0 + TS], pp(name)[:, 0:TS], sg[:, m % 2, TP:], ALU.mult), name)
                ada_rows(m + 1)
            steps = [(m + j, tap) for m in range(0, CM, 2) for tap in range(TAPS) for j in range(2)]
            todo = list(enumerate(steps))
            landed(dve, "a3")
            dve.wait_ge(hc_zero, 1)
            dve.drain()

            def conv(n):
                for _ in range(min(n, len(todo))):
                    at, (m, tap) = todo.pop(0)
                    w = wdw[:, m * TAPS + tap:m * TAPS + tap + 1]
                    src = hc[:, m, tap:tap + CONVW]
                    if tap == 0:
                        ins = dve.tensor_scalar(acc[:, m, :], src, w, vecT[:, m:m + 1], ALU.mult, ALU.add)
                    else:
                        dve.wait_ge(conv_n, at - 1)
                        ins = dve.scalar_tensor_tensor(acc[:, m, :], src, w, acc[:, m, :], ALU.mult, ALU.add)
                    ins.then_inc(conv_n, 1)

            conv(50)
            emptied(dve, "stq")
            dve.reciprocal(rB[:, 0, :], rB[:, 0, :])
            dve.drain()
            for n in range(QM):
                dve.scalar_tensor_tensor(qa[:, n, :], qa[:, n, :], vecT[:, 3 * CM + n:3 * CM + n + 1], rB[:, 0, :], ALU.mult, ALU.mult)
            dve.drain().then_inc(qn_ready, 1)
            conv(16)
            landed(dve, "kr")
            dve.tensor_tensor(tk[:, TP:], pp("kr")[:, 0:TS], CS[:, TP:], ALU.mult)
            free(dve.tensor_tensor(tk[:, 0:TP], pp("kr")[:, 512:512 + TP], CS[:, 0:TP], ALU.mult), "kr")
            emptied(dve, "stkv")
            dve.reciprocal(rB[:, 1, :], rB[:, 1, :])
            dve.drain()
            for n in range(KM):
                g = vecT[:, 3 * CM + QM + n:3 * CM + QM + n + 1]
                dve.scalar_tensor_tensor(ck[:, n, TP + PAST:], ck[:, n, TP + PAST:], g, rB[:, 1, TP:], ALU.mult, ALU.mult)
                dve.scalar_tensor_tensor(ck[:, n, 0:TP], ck[:, n, 0:TP], g, rB[:, 1, 0:TP], ALU.mult, ALU.mult)
            dve.drain().then_inc(ckn_ready, 1)
            for h in range(H):
                name = f"qr{h}"
                conv(5)
                landed(dve, name)
                dve.tensor_tensor(qr[:, h, TP:], pp(name)[:, 0:TS], CS[:, TP:], ALU.mult)
                free(dve.tensor_tensor(qr[:, h, 0:TP], pp(name)[:, 512:512 + TP], CS[:, 0:TP], ALU.mult), name)
            dve.drain().then_inc(proj_dve, 1)

            def ln_dve(u):
                if u == 17:
                    emptied(dve, "lnm")
                    dve.memset(mB[:, TP:SAMP0], 0.0)
                    dve.drain()
                    for m in range(CM):
                        dve.tensor_tensor(acc[:, m, :], acc[:, m, :], mB, ALU.subtract).then_inc(cen_ready, 1)
                elif u == 19:
                    emptied(dve, "lnv")
                    dve.memset(sB[:, TP:SAMP0], 1.0)
                    dve.drain()
                    dve.reciprocal(sB, sB)
                    dve.drain()
                    for m in range(CM):
                        dve.tensor_tensor(acc[:, m, :], acc[:, m, :], sB, ALU.mult).then_inc(lnn_ready, 1)

            for u in range(UNITS + 1):
                if u < UNITS:
                    w = T if u % NT < 4 else TP
                    landed(dve, f"S{u}")
                    dve.reduce_max(amax[:, 0, u:u + 1], pp(f"S{u}")[:, 0:w], AX.X)
                    dve.drain()
                    dve.tensor_scalar(amax[:, 1, u:u + 1], amax[:, 0, u:u + 1], -SCALE, None, ALU.mult).then_inc(max_ready, 1)
                if u >= 1:
                    n = u - 1
                    w = T if n % NT < 4 else TP
                    emptied(dve, f"S{n}")
                    dve.reciprocal(asum[:, 1, n:n + 1], asum[:, 0, n:n + 1])
                    dve.drain()
                    dve.tensor_scalar(pr[:, n % 2, 0:w], pr[:, n % 2, 0:w], asum[:, 1, n:n + 1], None, ALU.mult).then_inc(p_ready, 1)
                conv(3 if u < 14 else len(todo))
                ln_dve(u)
            dve.wait_ge(gg1_in, 32)
            dve.wait_ge(a2_in, 32)
            dve.wait_ge(b2_in, 32)
            for name in POST:
                kind, b = name[:-1], int(name[-1])
                if kind == "P":
                    v = min(b, 1)
                    dve.wait_ge(pss, b + 1)
                    dve.tensor_scalar(stat[:, 4, b:b + 1], stat[:, 3, b:b + 1], 1.0 / D, EPS, ALU.mult, ALU.add).then_inc(pvar, 1)
                    dve.wait_ge(psd, b + 1)
                    dve.reciprocal(stat[:, 5, b:b + 1], stat[:, 5, b:b + 1])
                    dve.drain()
                    free(dve.scalar_tensor_tensor(po[:, b % 2, :], pp(name)[:, 0:D], stat[:, 5, b:b + 1], gg1[:, v, :], ALU.mult, ALU.mult), name)
                    dve.drain()
                    dve.tensor_tensor(x[:, b, :], x[:, b, :], po[:, b % 2, :], ALU.add).then_inc(x1_ready, 1)
                    dve.wait_ge(xss, b + 1)
                    dve.tensor_scalar(stat[:, 4, b:b + 1], stat[:, 6, b:b + 1], 1.0 / D, EPS, ALU.mult, ALU.add).then_inc(xvar, 1)
                    dve.wait_ge(xsd, b + 1)
                    dve.reciprocal(stat[:, 7, b:b + 1], stat[:, 7, b:b + 1])
                    dve.drain()
                    ins = dve.scalar_tensor_tensor(h2[:, b % 2, :], x[:, b, :], stat[:, 7, b:b + 1], a2[:, v, :], ALU.mult, ALU.mult)
                    if b < NT - 1:
                        ins.then_inc(h2m_ready, 1)
                    else:
                        dve.drain()
                        dve.tensor_tensor(h2[:, b % 2, :], h2[:, b % 2, :], b2[:, v, :], ALU.add).then_inc(h2_last, 1)
                elif kind == "rl":
                    landed(dve, name)
                    free(dve.tensor_copy(L[:, b, :], pp(name)[:, 0:G + E]), name)
            dve.drain()

            def wide(n):
                return rt[:, n, :].rearrange("p (t e) -> p t e", e=E)

            def narrow(n, m, k):
                return rt[:, n, k * NT * m:(k + 1) * NT * m].rearrange("p (t e) -> p t e", e=m)

            Lg, Le = L[:, :, 0:G], L[:, :, G:]
            em, eq, oh1, oh2, pos = (wide(n) for n in range(5))
            goh, geq, pen, m1, m2, top = (narrow(5, G, 0), narrow(5, G, 1), narrow(5, G, 2), narrow(5, 1, 60 // 5 + 4), narrow(5, 1, 20), narrow(5, 1, 24))
            den = narrow(5, 1, 28)
            rankg = cst[:, C_RANK:C_RANK + G].unsqueeze(1).broadcast_to([P, NT, G])
            ranke = cst[:, C_RANK + G:C_RANK + G + E].unsqueeze(1).broadcast_to([P, NT, E])

            def over(v, n):
                return v.broadcast_to([P, NT, n])

            def step(ins):
                dve.drain()

            def first_best(out, v, hit, best, rank, n):
                step(dve.tensor_reduce(best, v, AX.X, ALU.max))
                step(dve.tensor_tensor(hit, v, over(best, n), ALU.is_equal))
                step(dve.tensor_tensor(hit, hit, rank, ALU.mult))
                step(dve.tensor_reduce(top, hit, AX.X, ALU.max))
                step(dve.tensor_tensor(out, hit, over(top, n), ALU.is_equal))

            first_best(goh, Lg, geq, m1, rankg, G)
            dve.tensor_tensor(rt_e[:, :, 0:G], Lg, over(m1, G), ALU.subtract)
            step(dve.tensor_scalar(pen, goh, 1e30, -1e30, ALU.mult, ALU.add))
            for g in range(G):
                part_ = slice(g * EG, (g + 1) * EG)
                dve.tensor_tensor(em[:, :, part_], Le[:, :, part_], goh[:, :, g:g + 1].broadcast_to([P, NT, EG]), ALU.mult)
            dve.drain()
            for g in range(G):
                part_ = slice(g * EG, (g + 1) * EG)
                dve.tensor_tensor(em[:, :, part_], em[:, :, part_], pen[:, :, g:g + 1].broadcast_to([P, NT, EG]), ALU.add)
            dve.drain()
            first_best(oh1, em, eq, m1, ranke, E)
            step(dve.scalar_tensor_tensor(em, oh1, -2e30, em, ALU.mult, ALU.add))
            first_best(oh2, em, eq, m2, ranke, E)
            dve.tensor_tensor(rt_e[:, :, G:G + 1], m2, m1, ALU.subtract)
            dve.tensor_tensor(maskb[:], oh1, oh2, ALU.add)
            dve.drain().then_inc(mask_ready, 1)
            dve.sem_inc(rgmax, 1)
            landed(dve, "pos")
            dve.tensor_copy(rt[:, 6, 0:E], pp("pos")[:, 512:512 + E])
            step(free(dve.tensor_copy(pos.rearrange("p t e -> p (t e)"), pp("pos")[:, 0:NT * E]), "pos"))
            at = rt[:, 7, 0:2 * NT].rearrange("p (c t) -> p c t", c=2)
            base = rt[:, 7, 16:16 + 2 * NT].rearrange("p (c t) -> p c t", c=2)
            rnd = rt[:, 7, 32:32 + 2 * NT].rearrange("p (c t) -> p c t", c=2)
            rnd_i = idx_r[:, 0:2 * NT].rearrange("p (c t) -> p c t", c=2)
            table = cst[:, C_IDB:C_IDB + E].unsqueeze(1).broadcast_to([P, NT, E])
            dve.tensor_tensor(eq, oh1, pos, ALU.mult)
            dve.tensor_tensor(em, oh2, pos, ALU.mult)
            dve.tensor_tensor(wide(8), oh1, table, ALU.mult)
            step(dve.tensor_tensor(wide(9), oh2, table, ALU.mult))
            for c, (a, b) in enumerate(((eq, wide(8)), (em, wide(9)))):
                dve.tensor_reduce(at[:, c, :].unsqueeze(2), a, AX.X, ALU.add)
                dve.tensor_reduce(base[:, c, :].unsqueeze(2), b, AX.X, ALU.add)
            dve.drain()
            dve.tensor_copy(rnd_i, at)
            step(dve.scalar_tensor_tensor(base, at, float(PAIRS), base, ALU.mult, ALU.add))
            step(dve.tensor_scalar(rnd_i, rnd_i, ROWS.bit_length() - 1, None, ALU.arith_shift_right))
            step(dve.tensor_copy(rnd, rnd_i))
            step(dve.scalar_tensor_tensor(base, rnd, float(PAIRS * (P - ROWS)), base, ALU.mult, ALU.add))
            dve.tensor_copy(slot_i[:], base).then_inc(idx_ready, 1)
            cnt = rt[0:1, 6, 0:E].rearrange("p (q j) -> p q j", j=2)
            big = rt[0:1, 6, E:E + PAIRS]
            step(dve.tensor_reduce(big.unsqueeze(2), cnt, AX.X, ALU.max))
            step(dve.tensor_scalar(big, big, 1.0, -1.0, ALU.max, ALU.add))
            step(dve.tensor_copy(extra[:, 0:PAIRS], big))
            step(dve.tensor_scalar(extra[:, 0:PAIRS], extra[:, 0:PAIRS], ROWS.bit_length() - 1, None, ALU.arith_shift_right))
            runs = [rt[0:1, 8, 2 * n * PAIRS:2 * (n + 1) * PAIRS] for n in range(2)]
            dve.memset(rt[0:1, 8, 0:4 * PAIRS], 0.0)
            step(None)
            step(dve.tensor_copy(runs[0][:, PAIRS:], extra[:, 0:PAIRS]))
            for n in range(PAIRS.bit_length() - 1):
                a, b = runs[n % 2], runs[1 - n % 2]
                step(dve.tensor_tensor(b[:, PAIRS:], a[:, PAIRS:], a[:, PAIRS - 2 ** n:2 * PAIRS - 2 ** n], ALU.add))
            dve.tensor_copy(extra[:, PAIRS:], runs[0][:, PAIRS - 1:2 * PAIRS - 1]).then_inc(cnt_ready, 1)
            dve.wait_ge(rexp, 1)
            dve.tensor_reduce(den, rt_e[:, :, 0:G], AX.X, ALU.add)
            step(dve.tensor_scalar(m1, rt_e[:, :, G:G + 1], 1.0, None, ALU.add))
            step(dve.tensor_tensor(den, den, m1, ALU.mult))
            step(dve.reciprocal(wsel[:, 0, :].unsqueeze(2), den))
            dve.tensor_tensor(wsel[:, 1, :].unsqueeze(2), rt_e[:, :, G:G + 1], wsel[:, 0, :].unsqueeze(2), ALU.mult)
            dve.drain().then_inc(wsel_ready, 1)

            def expert_pair(pair, s, stored):
                dve.wait_ge(e_silu, pair + 1)
                dve.tensor_tensor(he[:, s, :], he[:, s, :], ps[:, s, FE:2 * FE], ALU.mult).then_inc(e_h, 1)
                dve.wait_ge(e_y, pair + 1)
                if not isinstance(stored, int) or stored > 0:
                    dve.wait_ge(y_st[s], stored)
                    dve.wait_ge(r_pair, pair - 1)
                dve.tensor_copy(ys[:, s, :], ps[:, 2 + 2 * s:4 + 2 * s, :].rearrange("p a b -> p (a b)")).then_inc(e_ys, 1)
                n = dve.value_load(extra[0:1, bass.ds(pair, 1)], min_val=0, max_val=ROUNDS - 1)
                with dve.If(n > 0):
                    before = dve.value_load(extra[0:1, bass.ds(pair + PAIRS, 1)], min_val=0, max_val=PAIRS * (ROUNDS - 1))
                    with dve.Fori(1, n + 1) as r:
                        at = dve.snap(before + r)
                        dve.wait_ge(r_silu, at)
                        dve.tensor_tensor(he[:, s, :], he[:, s, :], ps[:, s, FE:2 * FE], ALU.mult).then_inc(r_h, 1)
                        dve.wait_ge(r_y, at)
                        dve.wait_ge(y_st[s], stored + 16)
                        dve.wait_ge(r_st, at)
                        dve.tensor_copy(ys[:, s, :], ps[:, 2 + 2 * s:4 + 2 * s, :].rearrange("p a b -> p (a b)")).then_inc(r_ys, 1)

            dve.sem_inc(r_ys, 1)
            for pair in range(3):
                expert_pair(pair, pair % 2, 16 * (pair // 2))
            with dve.Fori(0, LOOPED) as turn2:
                for s in range(2):
                    expert_pair(2 * turn2 + 3 + s, 1 - s, 16 * turn2 + 16 * (1 + s))
            for pair in range(PAIRS - 3, PAIRS):
                expert_pair(pair, pair % 2, 16 * (pair // 2))
            dve.wait_ge(gg2_in, 32)
            for b in range(NT + 1):
                if b < NT:
                    dve.wait_ge(f_first, b + 1)
                    dve.scalar_tensor_tensor(yg[:, 1, b, :], yg[:, 1, b, :], wsel[:, 1, b:b + 1], yg[:, 0, b, :], ALU.mult, ALU.add)\
                        .then_inc(f_mix, 1)
                if b:
                    n = b - 1
                    dve.wait_ge(f_ss, n + 1)
                    dve.tensor_scalar(stat[:, 4, n:n + 1], stat[:, 3, n:n + 1], 1.0 / D, EPS, ALU.mult, ALU.add).then_inc(f_var, 1)
                    dve.wait_ge(f_sd, n + 1)
                    dve.reciprocal(stat[:, 5, n:n + 1], stat[:, 5, n:n + 1])
                    dve.drain()
                    if n >= 2:
                        dve.wait_ge(f_out[0], n - 1)
                    ins = dve.scalar_tensor_tensor(yo[:, n % 2, :], yg[:, 1, n, :], stat[:, 5, n:n + 1], gg2[:, min(n, 1), :], ALU.mult, ALU.mult)
                    if n < NT - 1:
                        ins.then_inc(f_norm, 1)
                    else:
                        dve.drain()
                        dve.tensor_tensor(x[:, n, :], x[:, n, :], yo[:, n % 2, :], ALU.add).then_inc(f_out[1], 1)

        @block.tensor
        def _(pe):
            mm = nc.tensor.matmul

            def both(name, lhs, rhs_s, rhs_p, steps, width=TP):
                begin(pe, name)
                for k in range(steps):
                    mm(pp(name)[:, 0:TS], lhs(k), rhs_s(k), start=k == 0, stop=k == steps - 1)
                    last = mm(pp(name)[:, 512:512 + width], lhs(k), rhs_p(k), start=k == 0, stop=k == steps - 1)
                done(last, name)

            def turn(out, in_, n=P):
                return nc.tensor.transpose(out, in_, ident[0:n, 0:n])

            pe.wait_ge(cst_in, 16)
            def ada(n):
                name = f"ada{n}"
                begin(pe, name)
                for c in range(ADA[n][0], sum(ADA[n])):
                    pe.wait_ge(ada_in[c % RING], 16 * (c // RING + 1))
                    at = (c - ADA[n][0]) * P
                    for k in range(KD):
                        for j in range(4):
                            last = mm(pp(name)[32 * j:32 * j + 32, at:at + P], csT[:, k, :], ring[:, c % RING, k, j * P:(j + 1) * P],
                                      start=k == 0, stop=k == KD - 1)
                    if c < sum(ADA[n]) - 1:
                        last.then_inc(ada_used, 1)
                done(last, name)
                pe.drain().then_inc(ada_used, 1)

            pe.wait_ge(cs_ready, 1)
            ada(0)
            begin(pe, "modt")
            pe.wait_ge(rows_ready, 1)
            for n in range(4):
                last = turn(pp("modt")[:, n * P:(n + 1) * P], rows[:, n, :])
            done(last, "modt")
            pe.wait_ge(xn_ready, 1)
            for k in range(KD):
                name = f"tr{k}"
                begin(pe, name)
                for b in range(1, NT):
                    turn(pp(name)[:, (b - 1) * P:b * P], xn[:, b, k * P:(k + 1) * P])
                done(turn(pp(name)[:, 512:512 + TP], xn[:, 0, k * P:(k + 1) * P]), name)
            begin(pe, "vt")
            pe.wait_ge(vec_in, 16 * 6)
            for m in range(CM):
                turn(pp("vt")[:, m * TAPS:(m + 1) * TAPS], wdrow[:, m * P:(m + 1) * P], TAPS)
            done(turn(pp("vt")[:, 512:512 + 17], vrow, 17), "vt")
            pe.wait_ge(hT_act, 1)
            pe.wait_ge(hT_dve, 1)

            def project(name, lhs):
                both(name, lhs, lambda k: hT[:, k, TP:], lambda k: hT[:, k, 0:TP], KD)

            for m in range(CM):
                pe.wait_ge(wc_in[m], 32)
                project(f"g{m}", lambda k: wC[:, k, C + m * P:C + (m + 1) * P])
                project(f"a{m}", lambda k: wC[:, k, m * P:(m + 1) * P])
                ada(m + 1)
            pe.wait_ge(wq_in, 16)

            def square_sum(name, first, count, width, src):
                begin(pe, name)
                for n in range(first, first + count):
                    mm(pp(name)[:, 0:TS], ones[:], src(n, 1), start=n == first, stop=n == first + count - 1)
                    last = mm(pp(name)[:, 512:512 + TP], ones[:], src(n, 0), start=n == first, stop=n == first + count - 1)
                done(last, name)

            def sq_part(n, sample):
                return sq[:, n, TP:] if sample else sq[:, n, 0:TP]

            def low_rank(n, name):
                project(name, lambda k: wQ[:, k, n * P:(n + 1) * P])

            for n, name in enumerate(("q0", "q1", "q2", "kv0")):
                low_rank(n, name)
            pe.wait_ge(sq_ready, QM)
            square_sum("stq", 0, QM, QL, sq_part)
            low_rank(4, "kv1")
            pe.wait_ge(wkr_ready, 1)
            project("kr", lambda k: wkr[:, k, :])
            pe.wait_ge(sq_ready, QM + KM)
            square_sum("stkv", QM, KM, KVL, sq_part)
            pe.wait_ge(cache_in, 48)
            begin(pe, "cache")
            turn(pp("cache")[:, 0:P], ckr)
            for m in range(KM):
                last = turn(pp("cache")[:, (1 + m) * P:(2 + m) * P], cckv[:, m * P:(m + 1) * P])
            done(last, "cache")
            emptied(pe, "kr")
            both("krdup", lambda k: dup, lambda k: tk[:, TP:], lambda k: tk[:, 0:TP], 1)
            pe.wait_ge(qn_ready, 1)
            pe.wait_ge(wuq_in, 16)
            pe.wait_ge(wqr_ready, 1)
            for h in range(H):
                for name, lhs in ((f"qn{h}", lambda k: wuq[:, k, h * (DN + DR):h * (DN + DR) + DN]),
                                  (f"qr{h}", lambda k: wqr[:, k * H + h, :])):
                    both(name, lhs, lambda k: qa[:, k, TP:], lambda k: qa[:, k, 0:TP], QM)
            pe.wait_ge(ckn_ready, 1)
            begin(pe, "state")
            for m in range(KM):
                turn(pp("state")[:, m * P:(m + 1) * P], ck[:, m, 0:TP])
            done(turn(pp("state")[:, KVL:KVL + DR], tk[0:DR, 0:TP], DR), "state")
            pe.wait_ge(cachekv_ready, 1)
            pe.wait_ge(wukv_in, 16)
            for h in range(H):
                both(f"k{h}", lambda k: wukv[:, k, h * (DN + DV):h * (DN + DV) + DN],
                     lambda k: ck[:, k, TP + PAST:], lambda k: ck[:, k, 0:TP + PAST], KM, TP + PAST)
            for t in range(KT):
                name = f"v{t}"
                begin(pe, name)
                for k in range(KM):
                    last = mm(pp(name)[:, 0:512], ck[:, k, t * P:(t + 1) * P],
                              wukv[:, k, :].rearrange("p (h c) -> p h c", h=H)[:, :, DN:], start=k == 0, stop=k == KM - 1)
                done(last, name)
            pe.wait_ge(proj_act, 1)
            pe.wait_ge(proj_dve, 1)
            for u in range(UNITS + 1):
                if u < UNITS:
                    h, q = divmod(u, NT)
                    name = f"S{u}"
                    begin(pe, name)
                    if q < 4:
                        cols, first = slice(TP + q * P, TP + (q + 1) * P), TP
                        parts = ((0, 512), (512, T))
                    else:
                        cols, first, parts = slice(0, TP), 0, ((0, TP),)
                    for m, (a, b, c) in enumerate(((qn, kn, h), (qr, None, h))):
                        for lo, hi in parts:
                            keys = kn[:, h, first + lo:first + hi] if m == 0 else kr[:, first + lo:first + hi]
                            last = mm(pp(name)[:, lo:hi], a[:, h, cols], keys, start=m == 0, stop=m == 1)
                    done(last, name)
                if u >= 1:
                    n = u - 1
                    h, q = divmod(n, NT)
                    name = f"T{n}"
                    begin(pe, name)
                    pe.wait_ge(p_ready, u)
                    for t in range(5 if q < 4 else 1):
                        last = turn(pp(name)[:, t * P:(t + 1) * P], pr[:, n % 2, t * P:(t + 1) * P])
                    done(last, name)
                    if LN_AT.get(u) == "lnm":
                        pe.wait_ge(conv_n, CM * TAPS)
                        square_sum("lnm", 0, CM, C, lambda n, s: acc[:, n, SAMP0:] if s else acc[:, n, 0:TP])
                    elif LN_AT.get(u) == "lnv":
                        pe.wait_ge(lsq_ready, CM)
                        square_sum("lnv", 0, CM, C, lambda n, s: lsq[:, n, TP:] if s else lsq[:, n, 0:TP])
                    if q == 4:
                        name = f"O{h}"
                        begin(pe, name)
                        for m in range(u - NT, u):
                            emptied(pe, f"T{m}")
                        for t in range(5):
                            mm(pp(name)[:, 0:TS], vv[:, 1 + t, h * DV:(h + 1) * DV], pT[:, t, :], start=t == 0, stop=t == 4)
                        done(mm(pp(name)[:, 512:512 + TP], vv[:, 0, h * DV:(h + 1) * DV], pTp, start=True, stop=True), name)
            pe.wait_ge(wo_in, 16)
            pe.wait_ge(wr_ready, 1)
            for name in POST:
                kind, b = name[:-1], int(name[-1])
                begin(pe, name)
                if kind == "P":
                    if b == 0:
                        for h in range(H):
                            emptied(pe, f"O{h}")
                    for k in (*range(CM, KD), *range(CM)):
                        if b == 0 and k == 0:
                            pe.wait_ge(mixc_ready, CM)
                        for half in range(2):
                            last = mm(pp(name)[:, half * 512:(half + 1) * 512], mixT[:, k, b * P:(b + 1) * P],
                                      wo[:, k, half * 512:(half + 1) * 512], start=k == CM, stop=k == CM - 1)
                elif kind == "ht":
                    if b < NT - 1:
                        pe.wait_ge(h2_ready, b + 1)
                    else:
                        pe.wait_ge(h2_last, 1)
                    for k in range(KD):
                        last = turn(pp(name)[:, k * P:(k + 1) * P], h2[:, b % 2, k::KD])
                elif kind == "rt":
                    emptied(pe, f"ht{b}")
                    for k in range(KD):
                        last = mm(pp(name)[0:G + E, 0:P], wr[:, k, :], h2T[b % 2][:, k, :], start=k == 0, stop=k == KD - 1)
                else:
                    emptied(pe, f"rt{b}")
                    last = turn(pp(name)[:, 0:G + E], lg, G + E)
                done(last, name)
            begin(pe, "pos")
            pe.wait_ge(mask_ready, 1)
            pe.wait_ge(small_ready, 1)
            for b in range(NT):
                for a in range(b + 1):
                    mm(pp("pos")[:, b * E:(b + 1) * E], trib[:] if a == b else onesb[:], maskb[:, a, :], start=a == 0, stop=a == b)
            for a in range(NT):
                last = mm(pp("pos")[:, 512:512 + E], onesb[:], maskb[:, a, :], start=a == 0, stop=a == NT - 1)
            done(last, "pos")

            for s in range(4):
                n = sum(1 for name in order if place[name][0] == s)
                pe.wait_ge(drained[s], n)

            def rows_to_columns(src, inc):
                for k in range(KD):
                    last = turn(ps[:, 6 + k // 4, (k % 4) * P:(k % 4 + 1) * P], src[:, k::KD])
                last.then_inc(inc, 1)

            def gate_up(s, w, src, inc):
                for k in range(KD):
                    for j in range(2):
                        a = j * ROWS
                        last = mm(ps[a:a + ROWS, s, :], src[:, k, a:a + ROWS], slots[w][:, j, 0:2, k * FE:(k + 1) * FE], start=k == 0, stop=k == KD - 1)
                last.then_inc(inc, 1)

            def hidden_to_columns(s, src, inc):
                for k in range(KF):
                    last = turn(ps[:, s, k * P:(k + 1) * P], src[:, k::KF])
                last.then_inc(inc, 1)

            def down(s, w, src, inc):
                for k in range(KF):
                    for half in range(2):
                        for j in range(2):
                            a = j * ROWS
                            last = mm(ps[a:a + ROWS, 2 + 2 * s + half, :], src[:, k, a:a + ROWS],
                                      slots[w][:, j, 2, k * D + half * 512:k * D + (half + 1) * 512], start=k == 0, stop=k == KF - 1)
                last.then_inc(inc, 1)

            def expert_pair(pair, s, w, loaded, gathered, last=False):
                for j in range(2):
                    pe.wait_ge(w_in_s[w][j], loaded)
                pe.wait_ge(e_xT, pair + 1)
                gate_up(s, w, xT[:, s], e_gu)
                if not last:
                    pe.wait_ge(xg_in[1 - s], gathered)
                    rows_to_columns(xg[:, 1 - s, :], e_tr)
                pe.wait_ge(e_h, pair + 1)
                hidden_to_columns(s, he[:, s, :], e_ht)
                pe.wait_ge(e_hT, pair + 1)
                wait_from(pe, e_ys, pair)
                down(s, w, heT[:, s], e_y)
                n = pe.value_load(extra[0:1, bass.ds(pair, 1)], min_val=0, max_val=ROUNDS - 1)
                with pe.If(n > 0):
                    before = pe.value_load(extra[0:1, bass.ds(pair + PAIRS, 1)], min_val=0, max_val=PAIRS * (ROUNDS - 1))
                    with pe.Fori(1, n + 1) as r:
                        at = pe.snap(before + r)
                        pe.wait_ge(r_xg, at)
                        pe.wait_ge(e_xT, next_pair(pair) + 1)
                        rows_to_columns(xg[:, 1 - s, :], r_tr)
                        pe.wait_ge(r_xT, at)
                        gate_up(s, w, xT[:, s], r_gu)
                        pe.wait_ge(r_h, at)
                        hidden_to_columns(s, he[:, s, :], r_ht)
                        pe.wait_ge(r_hT, at)
                        pe.wait_ge(e_ys, pair + 1)
                        pe.wait_ge(r_ys, at)
                        down(s, w, heT[:, s], r_y)
                pe.drain().then_inc(w_used, 1)

            pe.wait_ge(cnt_ready, 1)
            pe.wait_ge(xg_in[0], 16)
            rows_to_columns(xg[:, 0, :], e_tr)
            expert_pair(0, 0, 0, 48, 16)
            expert_pair(1, 1, 1, 48, 32)
            expert_pair(2, 0, 2, 48, 32)
            with pe.Fori(0, LOOPED) as turn2:
                expert_pair(2 * turn2 + 3, 1, 1, 48 * turn2 + 96, 16 * turn2 + 48)
                expert_pair(2 * turn2 + 4, 0, 2, 48 * turn2 + 96, 16 * turn2 + 48)
            for pair in (PAIRS - 3, PAIRS - 2):
                expert_pair(pair, pair % 2, 2 - pair % 2, 48 * ((pair + 1) // 2), 16 * ((pair + 1) // 2 + 1))
            expert_pair(PAIRS - 1, 1, 0, 96, 0, last=True)


_INS = ["x_prompt", "x_sample", "cache_ckv", "cache_krope", "c", "c_ctx", "w_ada", "b_ada", "g_pre1", "g_post1",
        "g_pre2", "g_post2", "w_in", "w_dw", "b_dw", "conv_ln_g", "conv_ln_b", "q_norm_g", "kv_norm_g", "w_uq",
        "w_ukv", "w_out", "w_rg", "b_rg", "w_re", "b_re", "w_gate", "w_up", "w_down"]
_OUTS = [(1, TP, D), (1, TS, D), (1, 1, TP, KVL), (1, 1, TP, DR)]


def kernel(**inputs):
    import concourse.bacc as _bacc
    from concourse.bass_utils import run_bass_kernel_spmd as _run

    nc = _bacc.Bacc("TRN2", target_bir_lowering=False, num_devices=1)
    arrays, ins = {}, {}
    for name in _INS:
        arrays[f"in_{name}"] = np.ascontiguousarray(inputs[name])
    arrays["in_consts"] = constants()
    for name, a in arrays.items():
        ins[name[3:]] = nc.dram_tensor(name, a.shape, F32, kind="ExternalInput").ap()
    outs = [nc.dram_tensor(f"out_{n}", shape, F32, kind="ExternalOutput").ap() for n, shape in enumerate(_OUTS)]
    hybrid_layer(nc, ins, outs)
    r = _run(nc, [arrays], core_ids=[0])
    return tuple(r.results[0][f"out_{n}"] for n in range(len(_OUTS)))
```

```python
from contextlib import ExitStack

import numpy as np

import concourse.bass as bass
from concourse import mybir

F32 = mybir.dt.float32
BF16 = mybir.dt.bfloat16
I32 = mybir.dt.int32
ALU = mybir.AluOpType
ACT = mybir.ActivationFunctionType
AX = mybir.AxisListType

P = 128
D = 1024
KD = D // P
TP, TS, PAST = 128, 512, 128
T = TP + TS
NT = T // P
NKEY = TP + PAST + TS
KT = NKEY // P
C = 512
CM = C // P
TAPS = 31
HALF = TAPS // 2
H, DN, DR, DV = 4, 128, 64, 128
QL, KVL = 384, 256
QM, KM = QL // P, KVL // P
QKR = QL + KVL + DR
SCALE = float(DN + DR) ** -0.5
EPS = 1e-6
G, EG, E = 4, 8, 32
FE = 256
KF = FE // P
ROWS = 64
ROUNDS = T // ROWS
PAIRS = E // 2
PAD = 4096
LOOPED = (PAIRS - 6) // 2
PADW = HALF + TP + HALF + TS + HALF
CONVW = PADW - 2 * HALF
SAMP0 = TP + HALF
CHUNK = 512
NCH = 6 * D // CHUNK
ADA = [(0, 4), (4, 2), (6, 2), (8, 2), (10, 2)]
RING = 2
CONV_STEPS = CM * (TAPS + 1)
LAG = 2
UNITS = H * NT

C_ID, C_DUP, C_TRI, C_CS, C_RANK, C_IDB, C_TOK, C_EPS, C_HI, C_LO, C_IOTA = 0, 128, 256, 384, 1024, 1060, 1092, 1102, 1103, 1113, 1114
C_N = C_IOTA + ROWS


def constants():
    t = np.zeros((P, C_N), np.float32)
    p = np.arange(P)
    t[:, C_ID:C_ID + P] = np.eye(P)
    t[:, C_DUP:C_DUP + P] = (p[:, None] % DR) == (p[None, :] % DR)
    t[:, C_TRI:C_TRI + P] = p[:, None] < p[None, :]
    t[:DR, C_CS:C_CS + TP] = 1.0
    tok = np.arange(TS)
    nf = DR // 4
    freqs = (np.float32(10000.0) ** (-np.arange(nf, dtype=np.float32) / nf)).astype(np.float32)
    for d in range(DR):
        place = (tok // 64 if d < DR // 2 else tok % 64).astype(np.float32)
        ang = (place * freqs[d % nf]).astype(np.float32)
        t[d, C_CS + TP:C_CS + T] = np.cos(ang)
        t[DR + d, C_CS + TP:C_CS + T] = np.sin(ang) * (-1.0 if d % 32 < nf else 1.0)
    t[:, C_RANK:C_RANK + G] = G - np.arange(G)
    t[:, C_RANK + G:C_RANK + G + E] = E - np.arange(E)
    e = np.arange(E)
    t[:, C_IDB:C_IDB + E] = (e % 2) * ROWS * PAIRS + e // 2
    t[:, C_TOK:C_TOK + 2 * NT] = np.arange(2 * NT)[None, :] * P + p[:, None]
    t[:, C_EPS] = EPS
    t[:, C_HI:C_HI + 2 * NT] = (t[:, C_TOK:C_TOK + 2 * NT] - PAD) // 32
    t[:, C_LO] = p % 32
    t[:, C_IOTA:C_IOTA + ROWS] = np.arange(ROWS)
    return t


POST = ["P0", "P1", "P2", "ht0", "P3", "rt0", "ht1", "P4", "rl0", "rt1", "ht2", "ht3", "rl1", "rt2", "rl2", "rt3",
        "rl3", "ht4", "rt4", "rl4"]
BETWEEN = (("rl0", "rt1", "ht2"), ("ht3", "rl1", "rt2", "rl2", "rt3", "rl3"))


def unit_groups(u):
    names = [f"S{u}"] if u < UNITS else []
    if u > LAG and (u - LAG) % NT == 0:
        names.append(f"O{(u - LAG) // NT - 1}")
    return names + ([f"T{u - LAG}"] if LAG <= u < UNITS + LAG else [])


def pe_groups():
    names = [f"tr{k}" for k in range(KD)] + ["ada0", "modt", "vt"]
    for m in range(CM):
        names += [f"g{m}", f"a{m}", f"ada{m + 1}"]
    names += ["q0", "q1", "q2", "kv0", "stq", "kv1", "kr", "lnm", "stkv", "cache", "krdup"]
    for h in range(H):
        names += [f"qn{h}", f"qr{h}"]
        if h == 1:
            names.append("lnv")
    names += ["state"] + [f"k{h}" for h in range(H)] + [f"v{t}" for t in range(KT)]
    for u in range(UNITS + LAG + 1):
        names += unit_groups(u)
    return names + POST + ["pos", "table"]


def hybrid_layer(nc, i, outs):
    y_prompt, y_sample, state_ckv, state_krope = outs
    order = pe_groups()
    place = {name: (n % 4, n // 4) for n, name in enumerate(order)}

    with ExitStack() as ctx:
        def sb(name, shape, dt=F32):
            return ctx.enter_context(nc.sbuf_tensor(name, shape, dt))

        def sem(name):
            return ctx.enter_context(nc.semaphore(name))

        def dram(name, shape, dt=F32):
            return nc.dram_tensor(name, shape, dt, kind="Internal").ap()

        def part(t, at, *shape):
            n = int(np.prod(shape))
            v = t[:, at:at + n]
            if len(shape) == 4:
                return v.rearrange("p (a b c d) -> p a b c d", a=shape[0], b=shape[1], c=shape[2])
            if len(shape) == 2:
                return v.rearrange("p (a b) -> p a b", a=shape[0])
            if len(shape) == 3:
                return v.rearrange("p (a b c) -> p a b c", a=shape[0], b=shape[1])
            return v

        ada_d = dram("ada_d", (2, NCH, 4, P))
        h2_d = dram("h2_d", (T, D))
        ids_d = dram("ids_d", (ROUNDS * P * PAIRS, 1), I32)
        y_d = dram("y_d", (2 * T, D))

        x = sb("x", [P, NT, D])
        cst = sb("cst", [P, C_N])
        sizes = (2 * 3 * KD * FE, KD * (2 * C + QKR), KD * T, 3 * 768 + 2 * 1024 + 3 * 512, 7936)
        arena = sb("arena", [P, sum(sizes)])
        R1, W, HM, QW, CQ = (arena[:, sum(sizes[:n]):sum(sizes[:n + 1])] for n in range(5))
        ones = sb("ones", [P, P])
        onesb = sb("onesb", [P, P], BF16)
        trib = sb("trib", [P, P], BF16)
        wr = sb("wr", [P, KD, G + E])
        rbias = sb("rbias", [G + E, 1])
        stat = sb("stat", [P, 8, NT])
        vecT = sb("vecT", [P, 17])
        amax = sb("amax", [P, 2, UNITS])
        asum = sb("asum", [P, 2, UNITS])
        wsel = sb("wsel", [P, 2, NT])
        slot_i = sb("slot_i", [P, 2, NT], I32)
        tok_i = sb("tok_i", [P, 2, NT], I32)
        ids = sb("ids", [P, ROUNDS, PAIRS], I32)
        idg = sb("idg", [P, ROUNDS, PAIRS], I32)
        idx = sb("idx", [P, 6], I32)
        extra = sb("extra", [1, 2 * PAIRS], I32)
        idx_r = sb("idx_r", [P, 2 * NT], I32)

        ident = cst[:, C_ID:C_ID + P]
        dup = cst[:, C_DUP:C_DUP + P]
        CS = cst[:, C_CS:C_CS + T]
        eps = cst[:, C_EPS:C_EPS + 1]

        wC = part(W, 0, KD, 2 * C)
        wQ = part(W, KD * 2 * C, KD, QKR)
        mB = W[:, 0:CONVW]
        sB = W[:, CONVW:2 * CONVW]
        csum = part(W, 2 * CONVW, 2, CONVW)
        o = CM * CONVW
        sq = part(W, o, 5, T)
        rB = part(W, o + 5 * T, 2, T)
        wkr = part(W, o + 7 * T, KD, P)
        assert o + 7 * T + KD * P <= KD * 2 * C
        wo = part(W, o, KD, D)
        ring = part(R1, 0, RING, KD, CHUNK)
        first_chunks = [ring[:, 0], ring[:, 1], part(W, KD * 2 * C, KD, CHUNK), part(QW, 0, KD, CHUNK)]
        qn = part(R1, 0, H, T)
        qr = part(R1, 2560, H, T)
        kn = part(R1, 5120, H, NKEY)
        kr = part(R1, 8192, NKEY)
        vv = part(R1, 8960, KT, H * DV)
        acc = part(R1, 2 * 3 * KD * FE - CM * CONVW, CM, CONVW)
        odd = R1[:, RING * KD * CHUNK:RING * KD * CHUNK + CONVW]
        lsq = part(R1, 5120, CM, T)
        o = RING * KD * CHUNK + CONVW
        csT = part(R1, o, KD, 32)
        wdw = R1[:, o + KD * 32:o + KD * 32 + CM * TAPS]
        o += KD * 32 + CM * TAPS
        modT = part(R1, o, 4, 8).rearrange("p n (j v) -> p n j v", v=2)
        cT = part(R1, o + 32, 2, KD)
        assert o + 32 + 2 * KD <= 2 * 3 * KD * FE - CM * CONVW
        wuq = part(QW, 0, QM, H * (DN + DR))
        wukv = part(QW, 2304, KM, H * (DN + DV))
        wqr = part(QW, 4352, QM * H, P)
        gg1 = part(QW, 0, 2, D)
        a2 = part(QW, 2048, 2, D)
        h2T = [part(QW, 4096, KD, P), part(W, CM * CONVW + KD * D, KD, P)]
        wdrow = QW[0:TAPS, 4352:4352 + C]
        vrow = QW[0:17, 4352 + C:4352 + C + P]
        x_rg = part(QW, 4352 + C + P, KD, G)
        x_re = part(QW, 4352 + C + P + KD * G, KD, E)
        hT = part(HM, 0, KD, T)
        mixT = hT
        xn = part(CQ, 0, NT, D)
        rows = part(CQ, NT * D, NCH, P)
        grow = part(CQ, NT * D + NCH * P, 8, P)
        hc = part(CQ, 0, CM, PADW)
        o = CM * PADW
        sg = part(CQ, o, 2, T)
        qa = part(CQ, o, QM, T)
        ck = part(CQ, o + QM * T, KM, NKEY)
        tk = part(CQ, o + QM * T + KM * NKEY, T)
        ckr = part(CQ, o + QM * T + KM * NKEY + T, P)
        cckv = part(CQ, o + QM * T + KM * NKEY + T + P, KVL)
        sto = part(CQ, o + QM * T + KM * NKEY + T + P + KVL, KVL + DR)
        assert o + QM * T + KM * NKEY + T + P + 2 * KVL + DR <= 7936
        pr = part(CQ, o, LAG + 1, T)
        pT = part(CQ, o + (LAG + 1) * T, 5, TS)
        pTp = part(CQ, o + (LAG + 1) * T + 5 * TS, P)
        assert o + (LAG + 1) * T + 5 * TS + P <= 7936
        b2 = part(CQ, 0, 2, D)
        po = part(CQ, o, 2, D)
        h2 = part(CQ, o + 2 * D, 2, D)
        lg = CQ[0:G + E, o + 4 * D:o + 4 * D + P]
        assert o + 4 * D + P <= 7936
        L = part(CQ, o + 4 * D + P, NT, G + E)
        rt = part(CQ, o, 12, NT * E)
        rt_e = rt[:, 11, 0:NT * (G + 1)].rearrange("p (t g) -> p t g", g=G + 1)
        maskb = sb("maskb", [P, NT, E], BF16)
        place1 = sb("place1", [P, 2, NT, ROWS], BF16)
        number = sb("number", [P, 2, NT, 2, E], BF16)
        SLOT = 2 * 3 * KD * FE
        slots = [part(arena, n * SLOT, 2, 3, KD * FE) for n in range(3)]
        xg = part(CQ, 0, 2, D)
        xT = part(CQ, 5120, 2, KD, P)
        he = part(CQ, 4096, 2, FE)
        heT = part(CQ, 4096 + 2 * FE, 2, KF, P)
        ys = part(CQ, 2048, 2, D)
        gg2 = part(arena, 0, 2, D)
        yg = part(arena, SLOT + 2 * D, 2, NT, D)
        yo = part(arena, 2 * SLOT, 2, D)
        yjunk = part(arena, 2 * SLOT + 2 * D, D)

        ps = ctx.enter_context(nc.psum_tensor("ps", [P, 8, 512], F32))

        def pp(name):
            s = place[name][0]
            return ps[:, 2 * s:2 * s + 2, :].rearrange("p a b -> p (a b)")

        filled = [sem(f"filled{s}") for s in range(4)]
        drained = [sem(f"drained{s}") for s in range(4)]
        x_in = [sem(f"x_in{b}") for b in range(NT)]
        cst_in, cvec_in, vec_in, brow_in = sem("cst_in"), sem("cvec_in"), sem("vec_in"), sem("brow_in")
        ada_in = [sem(f"ada_in{s}") for s in range(len(first_chunks))]
        ada_used = sem("ada_used")
        wc_in, wq_in, wuq_in, wukv_in = [sem(f"wc_in{m}") for m in range(CM)], sem("wq_in"), sem("wuq_in"), sem("wukv_in")
        cache_in, wr_in, wo_in = sem("cache_in"), sem("wr_in"), sem("wo_in")
        zeroed, cs_ready, wr_ready, small_ready = sem("zeroed"), sem("cs_ready"), sem("wr_ready"), sem("small_ready")
        ss_ready, var_ready, sd_ready, xn_ready = sem("ss_ready"), sem("var_ready"), sem("sd_ready"), sem("xn_ready")
        rows_ready, ada_st = sem("rows_ready"), [sem(f"ada_st{n}") for n in range(5)]
        hT_act, hT_dve = sem("hT_act"), sem("hT_dve")
        hc_zero, sg_ready = sem("hc_zero"), sem("sg_ready")
        wkr_ready, wqr_ready = sem("wkr_ready"), sem("wqr_ready")
        sq_ready, qn_ready, ckn_ready = sem("sq_ready"), sem("qn_ready"), sem("ckn_ready")
        qsum_ready, csum_ready = sem("qsum_ready"), sem("csum_ready")
        place_ready, table_ready = sem("place_ready"), sem("table_ready")
        cachekv_ready, state_out = sem("cachekv_ready"), sem("state_out")
        proj_act, proj_dve = sem("proj_act"), sem("proj_dve")
        max_ready, p_ready = sem("max_ready"), sem("p_ready")
        conv_n, cen_ready, lsq_ready, lnn_ready, mixc_ready = (
            sem("conv_n"), sem("cen_ready"), sem("lsq_ready"), sem("lnn_ready"), sem("mixc_ready"))
        gg1_in, a2_in, b2_in, gg2_in = sem("gg1_in"), sem("a2_in"), sem("b2_in"), sem("gg2_in")
        pss, pvar, psd, x1_ready, xss, xvar, xsd, h2m_ready = (
            sem("pss"), sem("pvar"), sem("psd"), sem("x1_ready"), sem("xss"), sem("xvar"), sem("xsd"), sem("h2m_ready"))
        h2_ready, h2_last = sem("h2_ready"), sem("h2_last")
        h2_st = [sem("h2_st0"), sem("h2_st1")]
        rgmax, rexp, mask_ready, idx_ready, cnt_ready, wsel_ready = sem("rgmax"), sem("rexp"), sem("mask_ready"), sem("idx_ready"), sem("cnt_ready"), sem("wsel_ready")
        ids_pad, ids_st, more_in = sem("ids_pad"), sem("ids_st"), sem("more_in")
        w_in_s = [[sem(f"w{s}{j}") for j in range(2)] for s in range(3)]
        w_used = sem("w_used")
        xg_in = [sem("xg_in0"), sem("xg_in1")]
        e_tr, e_xT, e_gu, e_silu, e_h, e_ht, e_hT, e_y, e_ys = (sem(n) for n in (
            "e_tr", "e_xT", "e_gu", "e_silu", "e_h", "e_ht", "e_hT", "e_y", "e_ys"))
        y_st = [sem("y_st0"), sem("y_st1")]
        r_dma, r_xg, r_tr, r_xT, r_gu, r_silu, r_h, r_ht, r_hT, r_y, r_ys, r_st = (sem(n) for n in (
            "r_dma", "r_xg", "r_tr", "r_xT", "r_gu", "r_silu", "r_h", "r_ht", "r_hT", "r_y", "r_ys", "r_st"))
        r_pair = sem("r_pair")
        yg_in, f_first, f_norm, f_mix, f_ss, f_var, f_sd, f_out, out_st = ([sem(f"yg_in{b}") for b in range(NT)], sem("f_first"), sem("f_norm"), sem("f_mix"), sem("f_ss"),
                                                          sem("f_var"), sem("f_sd"), [sem("f_out0"), sem("f_out1")], sem("out_st"))

        def begin(pe, name):
            s, use = place[name]
            if use:
                pe.wait_ge(drained[s], use)

        def done(ins, name):
            return ins.then_inc(filled[place[name][0]], 1)

        def landed(eng, name):
            s, use = place[name]
            eng.wait_ge(filled[s], use + 1)

        def free(ins, name):
            return ins.then_inc(drained[place[name][0]], 1)

        def emptied(eng, name):
            s, use = place[name]
            eng.wait_ge(drained[s], use + 1)

        def chunk_place(n):
            if n < len(first_chunks):
                return first_chunks[n], ada_in[n], 1
            return ring[:, n % RING], ada_in[n % RING], (n - len(first_chunks)) // RING + 2

        def next_pair(pair):
            return pair if isinstance(pair, int) and pair == PAIRS - 1 else pair + 1

        def wait_from(eng, one, n):
            if not isinstance(n, int) or n > 0:
                eng.wait_ge(one, n)

        w_in_v = i["w_in"][0].rearrange("(k p) n -> p k n", p=P)
        ada_v = i["w_ada"][0].rearrange("(p k) (c n) -> c p k n", k=KD, n=CHUNK)
        ada_flat = ada_d.rearrange("v n j c -> v (n j c)")

        def bcast(v, vec):
            return ada_flat[v:v + 1, vec * D:(vec + 1) * D].broadcast_to([P, D])

        block = ctx.enter_context(nc.Block())

        @block.sync
        def _(sp):
            def ada_chunk(n):
                place, arrived, loads = chunk_place(n)
                if loads > 1:
                    sp.wait_ge(ada_used, n % RING + 1 if loads == 2 else n - RING + 1)
                sp.dma_start(place, ada_v[n]).then_inc(arrived, 16)

            for b in range(NT):
                src = i["x_prompt"][0] if b == 0 else i["x_sample"][0, (b - 1) * P:b * P, :]
                sp.dma_start(x[:, b, :], src).then_inc(x_in[b], 16)
            ada_chunk(0)
            sp.wait_ge(zeroed, 1)
            gains = (("g_pre1", 0), ("g_post1", 2), ("g_pre2", 4), ("g_post2", 6))
            for v in range(2):
                sp.dma_start(rows[v:v + 97:32], i["b_ada"][0].rearrange("(n j c) -> j n c", j=4, c=P)).then_inc(brow_in, 16)
                for name, at in gains:
                    sp.dma_start(grow[v:v + 97:32, at:at + 2], i[name][0].rearrange("(n j c) -> j n c", j=4, c=P)).then_inc(brow_in, 16)
            for n in range(1, 4):
                ada_chunk(n)
            for m in range(CM):
                for a in (C + m * P, m * P):
                    sp.dma_start(wC[:, :, a:a + P], w_in_v[:, :, a:a + P]).then_inc(wc_in[m], 16)
            for n in range(4, 6):
                ada_chunk(n)
            sp.wait_ge(ada_used, ADA[0][1])
            sp.dma_start(wQ, w_in_v[:, :, 2 * C:]).then_inc(wq_in, 16)
            sp.dma_start(wuq, i["w_uq"][0].rearrange("(k p) n -> p k n", p=P)).then_inc(wuq_in, 16)
            sp.dma_start(wukv, i["w_ukv"][0].rearrange("(k p) n -> p k n", p=P)).then_inc(wukv_in, 16)
            for n in range(6, NCH):
                ada_chunk(n)
            emptied(sp, "kr")
            landed(sp, "stkv")
            sp.wait_ge(qn_ready, 1)
            sp.wait_ge(ckn_ready, 1)
            sp.dma_start(wo, i["w_out"][0].rearrange("(k p) n -> p k n", p=P)).then_inc(wo_in, 16)
            landed(sp, "v5")
            sp.wait_ge(ada_st[1], 32)
            sp.wait_ge(ada_st[3], 32)
            for v in range(2):
                sp.dma_start(gg1[:, v, :], bcast(v, 2)).then_inc(gg1_in, 16)
                sp.dma_start(a2[:, v, :], bcast(v, 4)).then_inc(a2_in, 16)
            sp.wait_ge(conv_n, CONV_STEPS)
            sp.wait_ge(ada_st[2], 32)
            for v in range(2):
                sp.dma_start(b2[:, v, :], bcast(v, 3)).then_inc(b2_in, 16)

            def load_pair(pair, s, earlier, before=None):
                for piece in range(6):
                    j, n = divmod(piece, 3)
                    if piece >= 2:
                        sp.wait_ge(w_in_s[s][piece % 2], 48 * earlier + 16 * (piece // 2))
                    elif before is not None:
                        sp.wait_ge(w_in_s[before[0]][piece % 2], 48 * before[1])
                    w, k = (("w_gate", KD), ("w_up", KD), ("w_down", KF))[n]
                    src = i[w][0][bass.ds(2 * pair + j, 1)].rearrange("e (p k) f -> p (e k f)", k=k)
                    sp.dma_start(slots[s][:, j, n, :], src).then_inc(w_in_s[s][piece % 2], 16)

            landed(sp, f"O{H - 1}")
            sp.wait_ge(ada_used, NCH)
            load_pair(0, 0, 0)
            for b in range(NT):
                if b < NT - 1:
                    sp.wait_ge(h2_ready, b + 1)
                else:
                    landed(sp, f"P{NT - 1}")
                    sp.wait_ge(mixc_ready, CM)
                    landed(sp, f"rt{NT - 2}")
                    load_pair(1, 1, 0)
                    sp.wait_ge(h2_last, 1)
                sp.dma_start(h2_d[b * P:(b + 1) * P, :], h2[:, b % 2, :]).then_inc(h2_st[b % 2], 16)
            landed(sp, f"rt{NT - 1}")
            sp.wait_ge(more_in, 16)
            load_pair(2, 2, 0, (1, 1))
            sp.wait_ge(w_used, 1)
            load_pair(PAIRS - 3, 0, 1, (2, 1))
            with sp.Fori(0, LOOPED) as turn2:
                for s in range(2):
                    pair = 2 * turn2 + 3 + s
                    sp.wait_ge(w_used, pair - 1)
                    load_pair(pair, 1 + s, turn2 + 1, (2 - s, turn2 + 1 + s))
            for s in range(2):
                pair = PAIRS - 2 + s
                sp.wait_ge(w_used, pair - 2)
                load_pair(pair, 1 + s, LOOPED + 1, (2 - s, LOOPED + 1 + s))
            sp.wait_ge(w_used, PAIRS - 2)
            sp.wait_ge(ada_st[4], 32)
            for v in range(2):
                sp.dma_start(gg2[:, v, :], bcast(v, 5)).then_inc(gg2_in, 16)
            for s in range(2):
                sp.wait_ge(y_st[s], 16 * PAIRS // 2)
            sp.wait_ge(r_pair, PAIRS)
            sp.wait_ge(w_used, PAIRS)
            for b in range(NT):
                for c in range(2):
                    sp.dma_start(yg[:, c, b, :], y_d[c * T + b * P:c * T + (b + 1) * P, :]).then_inc(yg_in[b], 16)
            for b in range(NT):
                last = b == NT - 1
                sp.wait_ge(f_out[last], 1 if last else b + 1)
                dst = y_prompt[0] if b == 0 else y_sample[0, (b - 1) * P:b * P, :]
                sp.dma_start(dst, x[:, b, :]).then_inc(out_st, 16)
            sp.wait_ge(out_st, 16 * NT)
            sp.wait_ge(state_out, 32)

        @block.gpsimd
        def _(gp):
            gp.memset(ones[:], 1.0)
            gp.memset(onesb[:], 1.0)
            gp.memset(csT, 0.0)
            gp.memset(ids[:], PAD)
            gp.memset(rows, 0.0)
            gp.memset(grow, 0.0).then_inc(zeroed, 1)
            gp.wait_ge(zeroed, 1)
            gp.dma_start(ids_d.rearrange("(p n) one -> p (n one)", p=P), ids[:].rearrange("p a b -> p (a b)")).then_inc(ids_pad, 16)
            gp.wait_ge(cst_in, 16)
            gp.tensor_copy(trib[:], cst[:, C_TRI:C_TRI + P])
            gp.tensor_copy(tok_i[:].rearrange("p c t -> p (c t)"), cst[:, C_TOK:C_TOK + 2 * NT]).then_inc(small_ready, 1)

            def put_rows(n):
                gp.wait_ge(rows_ready, n + 1)
                a, c = ADA[n]
                for v in range(2):
                    gp.dma_start(ada_d[v, a:a + c].rearrange("n j c -> j n c"), rows[v:v + 97:32, a:a + c]).then_inc(ada_st[n], 16)

            landed(gp, "tr7")
            for a, n in ((0, HALF), (HALF + TP, HALF), (PADW - HALF, HALF)):
                last = gp.memset(hc[:, :, a:a + n], 0.0)
            last.then_inc(hc_zero, 1)
            gp.wait_ge(wr_in, 64)
            gp.tensor_copy(wr[:, :, 0:G], x_rg)
            gp.tensor_copy(wr[:, :, G:], x_re).then_inc(wr_ready, 1)
            for n in range(1, 3):
                put_rows(n)
            landed(gp, "a3")
            gp.wait_ge(wq_in, 16)
            krw = wQ[:, :, QL + KVL:]
            gp.tensor_copy(wkr[:, :, 0:DR], krw)
            for half in range(2):
                dst = wkr[:, :, DR:].rearrange("p k (b h c) -> p k b h c", b=2, h=2)[:, :, :, half, :]
                src = krw.rearrange("p k (b h c) -> p k b h c", b=2, h=2)[:, :, :, 1 - half, :]
                last = gp.tensor_copy(dst, src)
            last.then_inc(wkr_ready, 1)
            gp.wait_ge(wuq_in, 16)
            gp.wait_ge(wr_ready, 1)
            qrw = wuq.rearrange("p k (h c) -> p (k h) c", h=H)[:, :, DN:]
            gp.tensor_copy(wqr[:, :, 0:DR], qrw)
            for half in range(2):
                dst = wqr[:, :, DR:].rearrange("p k (b h c) -> p k b h c", b=2, h=2)[:, :, :, half, :]
                src = qrw.rearrange("p k (b h c) -> p k b h c", b=2, h=2)[:, :, :, 1 - half, :]
                last = gp.tensor_copy(dst, src)
            last.then_inc(wqr_ready, 1)
            for n in range(3, 5):
                put_rows(n)
            for n in range(1, 5):
                gp.wait_ge(ada_st[n], 32)
            for n in range(2):
                gp.dma_start(ckr[:, n * DR:(n + 1) * DR], i["cache_krope"][0, 0]).then_inc(cache_in, 16)
            gp.dma_start(cckv, i["cache_ckv"][0, 0]).then_inc(cache_in, 16)

            def add(out, a, b):
                return gp.tensor_tensor(out, a, b, ALU.add)

            gp.wait_ge(conv_n, CONV_STEPS // 2)
            add(csum[:, 0], acc[:, 0], acc[:, 1])
            gp.wait_ge(sq_ready, 2)
            add(sq[:, 0], sq[:, 0], sq[:, 1])
            gp.drain()
            gp.wait_ge(sq_ready, QM)
            add(sq[:, 0], sq[:, 0], sq[:, 2]).then_inc(qsum_ready, 1)
            gp.wait_ge(conv_n, CONV_STEPS)
            add(csum[:, 1], acc[:, 2], acc[:, 3])
            gp.drain()
            add(csum[:, 0], csum[:, 0], csum[:, 1]).then_inc(csum_ready, 1)
            landed(gp, "lnm")
            for m in range(0, CM, 2):
                gp.wait_ge(lsq_ready, m + 2)
                add(csum[:, m // 2, 0:T], lsq[:, m], lsq[:, m + 1])
            gp.drain()
            add(csum[:, 0, 0:T], csum[:, 0, 0:T], csum[:, 1, 0:T]).then_inc(csum_ready, 1)
            gp.wait_ge(b2_in, 32)
            for b in range(NT - 1):
                gp.wait_ge(h2m_ready, b + 1)
                gp.tensor_tensor(h2[:, b % 2, :], h2[:, b % 2, :], b2[:, min(b, 1), :], ALU.add).then_inc(h2_ready, 1)
            flat_ids, flat_idg = (t[:].rearrange("p a b -> p (a b)") for t in (ids, idg))

            def gather(dst, at, n, inc, places=None):
                if places is None:
                    gp.tensor_copy(idx[:, n:n + 1], flat_idg[:, bass.ds(at, 1)])
                    gp.drain()
                    places = idx[:, n:n + 1]
                gp.indirect_dma_start(dst, None, h2_d, bass.IndirectOffsetOnAxis(places, 0),
                                      bounds_check=T - 1, oob_is_err=False).then_inc(inc, 16)

            def scatter(src, at, n, inc):
                gp.tensor_copy(idx[:, n:n + 1], flat_ids[:, bass.ds(at, 1)])
                gp.drain()
                gp.indirect_dma_start(y_d, bass.IndirectOffsetOnAxis(idx[:, n:n + 1], 0), src, None,
                                      bounds_check=2 * T - 1, oob_is_err=False).then_inc(inc, 16)

            gp.wait_ge(table_ready, 1)
            gp.wait_ge(h2_st[0], 16 * 3)
            gp.wait_ge(h2_st[1], 16 * 2)
            for s in range(2):
                gather(xg[:, s, :], s, s, xg_in[s], flat_idg[:, s:s + 1])
            gp.wait_ge(idx_ready, 1)
            gp.wait_ge(ids_pad, 16)
            for b in range(NT):
                for c in range(2):
                    gp.indirect_dma_start(ids_d, bass.IndirectOffsetOnAxis(slot_i[:, c, b:b + 1], 0),
                                          tok_i[:, c, b:b + 1], None).then_inc(ids_st, 16)
            gp.wait_ge(e_tr, 1)
            gather(xg[:, 0, :], 2, 0, xg_in[0], flat_idg[:, 2:3])
            gp.wait_ge(ids_st, 16 * 2 * NT)
            ids_v = ids_d.rearrange("(r p q) one -> p r (q one)", r=ROUNDS, q=PAIRS)
            gp.dma_start(ids[:, 1:], ids_v[:, 1:]).then_inc(more_in, 16)
            gp.wait_ge(more_in, 16)
            gp.tensor_scalar(idg[:, 1:], ids[:, 1:], float(T), float(T), ALU.is_ge, ALU.mult)
            gp.drain()
            gp.tensor_tensor(idg[:, 1:], ids[:, 1:], idg[:, 1:], ALU.subtract)
            gp.drain()
            gp.wait_ge(cnt_ready, 1)
            gp.sem_inc(r_st, 1)

            def expert_pair(pair, s, stored, ahead=True):
                if ahead:
                    gp.wait_ge(e_tr, pair + 1)
                    gather(xg[:, s, :], pair + 2, s, xg_in[s])
                n = gp.value_load(extra[0:1, bass.ds(pair, 1)], min_val=0, max_val=ROUNDS - 1)

                def more_rows(r):
                    gather(xg[:, 1 - s, :], r * PAIRS + pair, 4, r_dma)
                    gp.drain().then_inc(r_xg, 1)

                with gp.If(n > 0):
                    gp.wait_ge(e_tr, next_pair(pair) + 1)
                    more_rows(1)
                gp.wait_ge(e_ys, pair + 1)
                wait_from(gp, y_st[s], stored)
                scatter(ys[:, s, :], pair, 2 + s, y_st[s])
                with gp.If(n > 0):
                    before = gp.value_load(extra[0:1, bass.ds(pair + PAIRS, 1)], min_val=0, max_val=PAIRS * (ROUNDS - 1))
                    with gp.Fori(1, n + 1) as r:
                        at = gp.snap(before + r)
                        with gp.If(r > 1):
                            more_rows(r)
                        gp.wait_ge(r_ys, at + 1)
                        scatter(ys[:, s, :], r * PAIRS + pair, 5, r_dma)
                        gp.drain().then_inc(r_st, 1)
                gp.sem_inc(r_pair, 1)

            for pair in range(3):
                expert_pair(pair, pair % 2, 16 * (pair // 2), ahead=pair > 0)
            with gp.Fori(0, LOOPED) as turn2:
                for s in range(2):
                    expert_pair(2 * turn2 + 3 + s, 1 - s, 16 * turn2 + 16 * (1 + s))
            for pair in range(PAIRS - 3, PAIRS):
                expert_pair(pair, pair % 2, 16 * (pair // 2), ahead=pair + 2 < PAIRS)
            for b in range(NT - 1):
                gp.wait_ge(f_norm, b + 1)
                gp.tensor_tensor(x[:, b, :], x[:, b, :], yo[:, b % 2, :], ALU.add).then_inc(f_out[0], 1)

        def rms(act, name, n, scale):
            landed(act, name)
            act.activation(rB[:, n, TP:], pp(name)[:, 0:TS], ACT.Sqrt, bias=eps, scale=scale)
            free(act.activation(rB[:, n, 0:TP], pp(name)[:, 512:512 + TP], ACT.Sqrt, bias=eps, scale=scale), name)

        def shift1(k, v):
            return modT[:, k // 4, k % 4, v:v + 1]

        def scale1(k, v):
            return modT[:, 2 + k // 4, k % 4, v:v + 1]

        @block.scalar
        def _(act):
            act.dma_start(cst[:], i["consts"]).then_inc(cst_in, 16)
            act.dma_start(cT[:, 0, :], i["c_ctx"].rearrange("(p k) -> p k", k=KD)).then_inc(cvec_in, 16)
            act.dma_start(cT[:, 1, :], i["c"][0].rearrange("(p k) -> p k", k=KD)).then_inc(cvec_in, 16)
            act.dma_start(wdrow, i["w_dw"][0]).then_inc(vec_in, 16)
            at = 0
            for name in ("b_dw", "conv_ln_g", "conv_ln_b", "q_norm_g", "kv_norm_g"):
                n = i[name].shape[1] // P
                act.dma_start(vrow[at:at + n], i[name][0].rearrange("(m p) -> m p", p=P)).then_inc(vec_in, 16)
                at += n
            act.wait_ge(cvec_in, 32)
            act.wait_ge(zeroed, 1)
            for v in range(2):
                last = act.activation(csT[:, :, v], cT[:, v, :], ACT.Silu)
            last.then_inc(cs_ready, 1)
            for b in range(NT):
                act.wait_ge(x_in[b], 16)
                act.activation(xn[:, b, :], x[:, b, :], ACT.Square, accum_out=stat[:, 0, b:b + 1]).then_inc(ss_ready, 1)
            act.wait_ge(var_ready, 1)
            act.activation(stat[:, 2, :], stat[:, 1, :], ACT.Sqrt).then_inc(sd_ready, 1)
            act.dma_start(rbias[0:G], i["b_rg"][0].rearrange("(e one) -> e one", one=1)).then_inc(wr_in, 16)
            act.dma_start(rbias[G:G + E], i["b_re"][0].rearrange("(e one) -> e one", one=1)).then_inc(wr_in, 16)
            act.dma_start(x_rg, i["w_rg"][0].rearrange("(p k) e -> p k e", k=KD)).then_inc(wr_in, 16)
            act.dma_start(x_re, i["w_re"][0].rearrange("(p k) e -> p k e", k=KD)).then_inc(wr_in, 16)
            for k in range(0, KD, 2):
                name = f"tr{k}"
                landed(act, name)
                act.activation(hT[:, k, TP:], pp(name)[:, 0:TS], ACT.Copy)
                free(act.activation(hT[:, k, 0:TP], pp(name)[:, 512:512 + TP], ACT.Copy), name)
            emptied(act, "modt")
            act.drain()
            for k in range(0, KD, 2):
                act.activation(hT[:, k, TP:], hT[:, k, TP:], ACT.Identity, bias=shift1(k, 1), scale=scale1(k, 1))
                act.activation(hT[:, k, 0:TP], hT[:, k, 0:TP], ACT.Identity, bias=shift1(k, 0), scale=scale1(k, 0)).then_inc(hT_act, 1)
            for m in range(CM):
                name = f"g{m}"
                landed(act, name)
                if m >= 2:
                    emptied(act, f"a{m - 2}")
                elif m == 0:
                    act.wait_ge(hc_zero, 1)
                act.activation(sg[:, m % 2, 0:TP], pp(name)[:, 512:512 + TP], ACT.Sigmoid)
                free(act.activation(sg[:, m % 2, TP:], pp(name)[:, 0:TS], ACT.Sigmoid), name)
                act.drain().then_inc(sg_ready, 1)
            emptied(act, f"a{CM - 1}")
            for n in range(1, 5):
                act.wait_ge(ada_st[n], 32)
            landed(act, "a3")
            for n, name in enumerate(("q0", "q1", "q2", "kv0", "kv1")):
                landed(act, name)
                g = pp(name)
                if n < QM:
                    act.activation(qa[:, n, TP:], g[:, 0:TS], ACT.Copy)
                    act.activation(qa[:, n, 0:TP], g[:, 512:512 + TP], ACT.Copy)
                else:
                    act.activation(ck[:, n - QM, TP + PAST:], g[:, 0:TS], ACT.Copy)
                    act.activation(ck[:, n - QM, 0:TP], g[:, 512:512 + TP], ACT.Copy)
                act.activation(sq[:, n, TP:], g[:, 0:TS], ACT.Square)
                free(act.activation(sq[:, n, 0:TP], g[:, 512:512 + TP], ACT.Square), name)
                act.drain().then_inc(sq_ready, 1)
                if n == 3:
                    rms(act, "stq", 0, 1.0 / QL)
            landed(act, "lnm")
            act.activation(mB[:, SAMP0:], pp("lnm")[:, 0:TS], ACT.Copy, scale=1.0 / C)
            free(act.activation(mB[:, 0:TP], pp("lnm")[:, 512:512 + TP], ACT.Copy, scale=1.0 / C), "lnm")
            rms(act, "stkv", 1, 1.0 / KVL)
            act.wait_ge(conv_n, CONV_STEPS)
            landed(act, "cache")
            act.activation(kr[:, TP:TP + PAST], pp("cache")[:, 0:P], ACT.Copy)
            for m in range(KM):
                last = act.activation(ck[:, m, TP:TP + PAST], pp("cache")[:, (1 + m) * P:(2 + m) * P], ACT.Copy)
            free(last, "cache")
            act.drain().then_inc(cachekv_ready, 1)
            landed(act, "krdup")
            act.activation(kr[:, TP + PAST:], pp("krdup")[:, 0:TS], ACT.Copy)
            free(act.activation(kr[:, 0:TP], pp("krdup")[:, 512:512 + TP], ACT.Copy), "krdup")
            for m in range(CM):
                act.wait_ge(cen_ready, m + 1)
                act.activation(lsq[:, m, TP:], acc[:, m, SAMP0:], ACT.Square)
                act.activation(lsq[:, m, 0:TP], acc[:, m, 0:TP], ACT.Square).then_inc(lsq_ready, 1)
            for h in range(H):
                name = f"qn{h}"
                landed(act, name)
                act.activation(qn[:, h, TP:], pp(name)[:, 0:TS], ACT.Copy)
                free(act.activation(qn[:, h, 0:TP], pp(name)[:, 512:512 + TP], ACT.Copy), name)
                if h == 1:
                    landed(act, "lnv")
                    act.activation(sB[:, SAMP0:], pp("lnv")[:, 0:TS], ACT.Sqrt, bias=eps, scale=1.0 / C)
                    free(act.activation(sB[:, 0:TP], pp("lnv")[:, 512:512 + TP], ACT.Sqrt, bias=eps, scale=1.0 / C), "lnv")
            for m in range(CM):
                act.wait_ge(lnn_ready, m + 1)
                g, bb = vecT[:, CM + m:CM + m + 1], vecT[:, 2 * CM + m:2 * CM + m + 1]
                act.activation(mixT[:, m, TP:], acc[:, m, SAMP0:], ACT.Silu, bias=bb, scale=g)
                act.activation(mixT[:, m, 0:TP], acc[:, m, 0:TP], ACT.Silu, bias=bb, scale=g).then_inc(mixc_ready, 1)
            landed(act, "state")
            free(act.activation(sto, pp("state")[:, 0:KVL + DR], ACT.Copy), "state")
            emptied(act, "state")
            act.dma_start(state_ckv[0, 0], sto[:, 0:KVL]).then_inc(state_out, 16)
            act.dma_start(state_krope[0, 0], sto[:, KVL:]).then_inc(state_out, 16)
            for h in range(H):
                name = f"k{h}"
                landed(act, name)
                act.activation(kn[:, h, TP + PAST:], pp(name)[:, 0:TS], ACT.Copy)
                free(act.activation(kn[:, h, 0:TP + PAST], pp(name)[:, 512:512 + TP + PAST], ACT.Copy), name)
            for t in range(KT):
                name = f"v{t}"
                landed(act, name)
                free(act.activation(vv[:, t, :], pp(name)[:, 0:512], ACT.Copy), name)
            act.drain().then_inc(proj_act, 1)
            act.wait_ge(state_out, 32)

            for u in range(UNITS + LAG + 1):
                for name in unit_groups(u):
                    kind, n = name[0], int(name[1:])
                    g = pp(name)
                    if kind == "S":
                        w = T if n % NT < 4 else TP
                        act.wait_ge(max_ready, n + 1)
                        if n > LAG:
                            landed(act, f"T{n - LAG - 1}")
                        free(act.activation(pr[:, n % (LAG + 1), 0:w], g[:, 0:w], ACT.Exp, bias=amax[:, 1, n:n + 1],
                                            scale=SCALE, accum_out=asum[:, 0, n:n + 1]), name)
                    elif kind == "T":
                        landed(act, name)
                        q = n % NT
                        if n >= NT and q == 0:
                            landed(act, f"O{n // NT - 1}")
                        if q < 4:
                            free(act.activation(pT[:, :, q * P:(q + 1) * P], g[:, 0:T].rearrange("p (t q) -> p t q", q=P), ACT.Copy), name)
                        else:
                            free(act.activation(pTp, g[:, 0:P], ACT.Copy), name)
                    else:
                        landed(act, name)
                        act.activation(mixT[:, CM + n, TP:], g[:, 0:TS], ACT.Copy)
                        free(act.activation(mixT[:, CM + n, 0:TP], g[:, 512:512 + TP], ACT.Copy), name)
            def read_out(name):
                kind, b = name[:-1], int(name[-1])
                landed(act, name)
                if kind == "ht":
                    if b >= 2:
                        landed(act, f"rt{b - 2}")
                    free(act.activation(h2T[b % 2].rearrange("p k t -> p (k t)"), pp(name), ACT.Copy), name)
                elif kind == "rt":
                    if b:
                        landed(act, f"rl{b - 1}")
                    free(act.activation(lg, pp(name)[0:G + E, 0:P], ACT.Identity, bias=rbias[:]), name)
                else:
                    free(act.activation(L[:, b, :], pp(name)[:, 0:G + E], ACT.Copy), name)

            for name in POST:
                b = int(name[-1])
                if name[0] == "P":
                    last = b == NT - 1
                    landed(act, name)
                    if b >= 2:
                        act.wait_ge(x1_ready, b - 1)
                    act.activation(po[:, b % 2, :], pp(name)[:, 0:D], ACT.Square, accum_out=stat[:, 3, b:b + 1]).then_inc(pss, 1)
                    act.wait_ge(pvar, b + 1)
                    act.activation(stat[:, 5, b:b + 1], stat[:, 4, b:b + 1], ACT.Sqrt).then_inc(psd, 1)
                    for other in BETWEEN[0] if last else ():
                        read_out(other)
                    act.wait_ge(x1_ready, b + 1)
                    if b >= 2:
                        act.wait_ge(h2_st[b % 2], 16 * (b // 2))
                        landed(act, f"ht{b - 2}")
                    act.activation(h2[:, b % 2, :], x[:, b, :], ACT.Square, accum_out=stat[:, 6, b:b + 1]).then_inc(xss, 1)
                    act.wait_ge(xvar, b + 1)
                    act.activation(stat[:, 7, b:b + 1], stat[:, 4, b:b + 1], ACT.Sqrt).then_inc(xsd, 1)
                    for other in BETWEEN[1] if last else ():
                        read_out(other)
                elif not any(name in some for some in BETWEEN):
                    read_out(name)
            act.wait_ge(rgmax, 1)
            act.activation(rt_e, rt_e, ACT.Exp).then_inc(rexp, 1)

            def columns_out(dst, bank, count):
                return act.activation(dst.rearrange("p k t -> p (k t)"), bank.rearrange("p a b -> p (a b)")[:, 0:count], ACT.Copy)

            def expert_pair(pair, s, last=False):
                act.wait_ge(e_gu, pair + 1)
                act.activation(he[:, s, :], ps[:, s, 0:FE], ACT.Silu).then_inc(e_silu, 1)
                if not last:
                    act.wait_ge(e_tr, pair + 2)
                    columns_out(xT[:, 1 - s], ps[:, 6:8, :], D).then_inc(e_xT, 1)
                act.wait_ge(e_ht, pair + 1)
                columns_out(heT[:, s], ps[:, s:s + 1, :], FE).then_inc(e_hT, 1)
                n = act.value_load(extra[0:1, bass.ds(pair, 1)], min_val=0, max_val=ROUNDS - 1)
                with act.If(n > 0):
                    before = act.value_load(extra[0:1, bass.ds(pair + PAIRS, 1)], min_val=0, max_val=PAIRS * (ROUNDS - 1))
                    with act.Fori(1, n + 1) as r:
                        at = act.snap(before + r)
                        act.wait_ge(r_tr, at)
                        columns_out(xT[:, s], ps[:, 6:8, :], D).then_inc(r_xT, 1)
                        act.wait_ge(r_gu, at)
                        act.activation(he[:, s, :], ps[:, s, 0:FE], ACT.Silu).then_inc(r_silu, 1)
                        act.wait_ge(r_ht, at)
                        columns_out(heT[:, s], ps[:, s:s + 1, :], FE).then_inc(r_hT, 1)

            act.wait_ge(e_tr, 1)
            columns_out(xT[:, 0], ps[:, 6:8, :], D).then_inc(e_xT, 1)
            act.wait_ge(wsel_ready, 1)
            for pair in range(3):
                expert_pair(pair, pair % 2)
            with act.Fori(0, LOOPED) as turn2:
                for s in range(2):
                    expert_pair(2 * turn2 + 3 + s, 1 - s)
            for pair in range(PAIRS - 3, PAIRS):
                expert_pair(pair, pair % 2, last=pair == PAIRS - 1)
            def norm_sum(b):
                act.wait_ge(f_mix, b + 1)
                act.activation(yjunk, yg[:, 1, b, :], ACT.Square, accum_out=stat[:, 3, b:b + 1]).then_inc(f_ss, 1)
                act.wait_ge(f_var, b + 1)
                act.activation(stat[:, 5, b:b + 1], stat[:, 4, b:b + 1], ACT.Sqrt).then_inc(f_sd, 1)

            for b in range(NT):
                act.wait_ge(yg_in[b], 32)
                act.activation(yg[:, 0, b, :], yg[:, 0, b, :], ACT.Copy, scale=wsel[:, 0, b:b + 1]).then_inc(f_first, 1)
                if b:
                    norm_sum(b - 1)
            norm_sum(NT - 1)

        @block.vector
        def _(dve):
            dve.wait_ge(ss_ready, NT)
            dve.tensor_scalar(stat[:, 1, :], stat[:, 0, :], 1.0 / D, EPS, ALU.mult, ALU.add).then_inc(var_ready, 1)
            dve.wait_ge(sd_ready, 1)
            dve.reciprocal(stat[:, 2, :], stat[:, 2, :])
            dve.drain()
            for b in range(NT):
                last = dve.tensor_scalar(xn[:, b, :], x[:, b, :], stat[:, 2, b:b + 1], None, ALU.mult)
            last.then_inc(xn_ready, 1)

            def ada_rows(n):
                a, c = ADA[n]
                name = f"ada{n}"
                landed(dve, name)
                free(dve.tensor_tensor(rows[:, a:a + c].rearrange("p n c -> p (n c)"), pp(name)[:, 0:c * P],
                                       rows[:, a:a + c].rearrange("p n c -> p (n c)"), ALU.add), name)
                dve.drain()
                if n == 0:
                    dve.scalar_tensor_tensor(rows[:, 2:4], rows[:, 2:4], 1.0, grow[:, 0:2], ALU.add, ALU.mult)
                elif n == 1:
                    dve.tensor_tensor(rows[:, 4:6], rows[:, 4:6], grow[:, 2:4], ALU.mult)
                elif n == 3:
                    dve.scalar_tensor_tensor(rows[:, 8:10], rows[:, 8:10], 1.0, grow[:, 4:6], ALU.add, ALU.mult)
                elif n == 4:
                    dve.tensor_tensor(rows[:, 10:12], rows[:, 10:12], grow[:, 6:8], ALU.mult)
                dve.drain().then_inc(rows_ready, 1)

            for k in range(1, KD, 2):
                name = f"tr{k}"
                landed(dve, name)
                dve.tensor_copy(hT[:, k, TP:], pp(name)[:, 0:TS])
                free(dve.tensor_copy(hT[:, k, 0:TP], pp(name)[:, 512:512 + TP]), name)
            dve.wait_ge(brow_in, 16 * 10)
            ada_rows(0)
            landed(dve, "modt")
            turned = pp("modt")[:, 0:512].rearrange("p (n j c) -> p n j c", n=4, j=4)[:, :, :, 0:2]
            free(dve.tensor_copy(modT, turned), "modt")
            dve.drain()
            for k in range(1, KD, 2):
                dve.tensor_scalar(hT[:, k, TP:], hT[:, k, TP:], scale1(k, 1), shift1(k, 1), ALU.mult, ALU.add)
                dve.tensor_scalar(hT[:, k, 0:TP], hT[:, k, 0:TP], scale1(k, 0), shift1(k, 0), ALU.mult, ALU.add).then_inc(hT_dve, 1)
            landed(dve, "vt")
            dve.tensor_copy(wdw, pp("vt")[:, 0:CM * TAPS])
            free(dve.tensor_copy(vecT[:], pp("vt")[:, 512:512 + 17]), "vt")
            todo = [(m, tap) for m in range(CM) for tap in range(TAPS + 1)]

            def conv(n):
                for _ in range(min(n, len(todo))):
                    at = CONV_STEPS - len(todo)
                    m, tap = todo.pop(0)
                    dst = odd if tap % 2 else acc[:, m, :]
                    if tap < TAPS:
                        w = wdw[:, m * TAPS + tap:m * TAPS + tap + 1]
                        src = hc[:, m, tap:tap + CONVW]
                    if tap == 0:
                        ins = dve.tensor_scalar(dst, src, w, vecT[:, m:m + 1], ALU.mult, ALU.add)
                    elif tap == 1:
                        if m:
                            dve.wait_ge(conv_n, at - 1)
                        ins = dve.tensor_scalar(dst, src, w, None, ALU.mult)
                    elif tap < TAPS:
                        dve.wait_ge(conv_n, at - 1)
                        ins = dve.scalar_tensor_tensor(dst, src, w, dst, ALU.mult, ALU.add)
                    else:
                        dve.wait_ge(conv_n, at)
                        ins = dve.tensor_tensor(acc[:, m, :], acc[:, m, :], odd, ALU.add)
                    ins.then_inc(conv_n, 1)

            dve.wait_ge(hc_zero, 1)
            for m in range(CM):
                name = f"a{m}"
                dve.wait_ge(sg_ready, m + 1)
                landed(dve, name)
                dve.tensor_tensor(hc[:, m, HALF:HALF + TP], pp(name)[:, 512:512 + TP], sg[:, m % 2, 0:TP], ALU.mult)
                free(dve.tensor_tensor(hc[:, m, HALF + SAMP0:HALF + SAMP0 + TS], pp(name)[:, 0:TS], sg[:, m % 2, TP:], ALU.mult), name)
                ada_rows(m + 1)
                conv(26 if m < CM - 1 else len(todo))
            emptied(dve, "stq")
            dve.reciprocal(rB[:, 0, :], rB[:, 0, :])
            dve.drain()
            for n in range(QM):
                dve.scalar_tensor_tensor(qa[:, n, :], qa[:, n, :], vecT[:, 3 * CM + n:3 * CM + n + 1], rB[:, 0, :], ALU.mult, ALU.mult)
            dve.drain().then_inc(qn_ready, 1)
            landed(dve, "kr")
            dve.tensor_tensor(tk[:, TP:], pp("kr")[:, 0:TS], CS[:, TP:], ALU.mult)
            free(dve.tensor_tensor(tk[:, 0:TP], pp("kr")[:, 512:512 + TP], CS[:, 0:TP], ALU.mult), "kr")
            dve.memset(mB[:, TP:SAMP0], 0.0)
            dve.memset(sB[:, TP:SAMP0], 1.0)
            emptied(dve, "lnm")
            dve.drain()
            for m in range(CM):
                dve.tensor_tensor(acc[:, m, :], acc[:, m, :], mB, ALU.subtract).then_inc(cen_ready, 1)
            emptied(dve, "stkv")
            dve.reciprocal(rB[:, 1, :], rB[:, 1, :])
            dve.drain()
            for n in range(KM):
                g = vecT[:, 3 * CM + QM + n:3 * CM + QM + n + 1]
                dve.scalar_tensor_tensor(ck[:, n, TP + PAST:], ck[:, n, TP + PAST:], g, rB[:, 1, TP:], ALU.mult, ALU.mult)
                dve.scalar_tensor_tensor(ck[:, n, 0:TP], ck[:, n, 0:TP], g, rB[:, 1, 0:TP], ALU.mult, ALU.mult)
            dve.drain().then_inc(ckn_ready, 1)
            for h in range(H):
                name = f"qr{h}"
                landed(dve, name)
                dve.tensor_tensor(qr[:, h, TP:], pp(name)[:, 0:TS], CS[:, TP:], ALU.mult)
                free(dve.tensor_tensor(qr[:, h, 0:TP], pp(name)[:, 512:512 + TP], CS[:, 0:TP], ALU.mult), name)
                if h == 1:
                    emptied(dve, "lnv")
                    dve.reciprocal(sB, sB)
                    dve.drain()
                    for m in range(CM):
                        dve.tensor_tensor(acc[:, m, :], acc[:, m, :], sB, ALU.mult).then_inc(lnn_ready, 1)
            dve.drain().then_inc(proj_dve, 1)

            for u in range(UNITS + 1):
                if u < UNITS:
                    w = T if u % NT < 4 else TP
                    landed(dve, f"S{u}")
                    dve.reduce_max(amax[:, 0, u:u + 1], pp(f"S{u}")[:, 0:w], AX.X)
                    dve.drain()
                    dve.tensor_scalar(amax[:, 1, u:u + 1], amax[:, 0, u:u + 1], -SCALE, None, ALU.mult).then_inc(max_ready, 1)
                if u >= 1:
                    n = u - 1
                    w = T if n % NT < 4 else TP
                    emptied(dve, f"S{n}")
                    dve.reciprocal(asum[:, 1, n:n + 1], asum[:, 0, n:n + 1])
                    dve.drain()
                    dve.tensor_scalar(pr[:, n % (LAG + 1), 0:w], pr[:, n % (LAG + 1), 0:w], asum[:, 1, n:n + 1], None, ALU.mult).then_inc(p_ready, 1)
            dve.wait_ge(gg1_in, 32)
            dve.wait_ge(a2_in, 32)
            dve.wait_ge(b2_in, 32)
            for name in POST:
                kind, b = name[:-1], int(name[-1])
                if kind == "P":
                    v = min(b, 1)
                    dve.wait_ge(pss, b + 1)
                    dve.tensor_scalar(stat[:, 4, b:b + 1], stat[:, 3, b:b + 1], 1.0 / D, EPS, ALU.mult, ALU.add).then_inc(pvar, 1)
                    dve.wait_ge(psd, b + 1)
                    dve.reciprocal(stat[:, 5, b:b + 1], stat[:, 5, b:b + 1])
                    dve.drain()
                    free(dve.scalar_tensor_tensor(po[:, b % 2, :], pp(name)[:, 0:D], stat[:, 5, b:b + 1], gg1[:, v, :], ALU.mult, ALU.mult), name)
                    dve.drain()
                    dve.tensor_tensor(x[:, b, :], x[:, b, :], po[:, b % 2, :], ALU.add).then_inc(x1_ready, 1)
                    dve.wait_ge(xss, b + 1)
                    dve.tensor_scalar(stat[:, 4, b:b + 1], stat[:, 6, b:b + 1], 1.0 / D, EPS, ALU.mult, ALU.add).then_inc(xvar, 1)
                    dve.wait_ge(xsd, b + 1)
                    dve.reciprocal(stat[:, 7, b:b + 1], stat[:, 7, b:b + 1])
                    dve.drain()
                    ins = dve.scalar_tensor_tensor(h2[:, b % 2, :], x[:, b, :], stat[:, 7, b:b + 1], a2[:, v, :], ALU.mult, ALU.mult)
                    if b < NT - 1:
                        ins.then_inc(h2m_ready, 1)
                    else:
                        dve.drain()
                        dve.tensor_tensor(h2[:, b % 2, :], h2[:, b % 2, :], b2[:, v, :], ALU.add).then_inc(h2_last, 1)
            emptied(dve, f"rl{NT - 1}")

            def wide(n):
                return rt[:, n, :].rearrange("p (t e) -> p t e", e=E)

            def narrow(n, m, k):
                return rt[:, n, k * NT * m:(k + 1) * NT * m].rearrange("p (t e) -> p t e", e=m)

            Lg, Le = L[:, :, 0:G], L[:, :, G:]
            em, eq, oh1, oh2, pos = (wide(n) for n in range(5))
            goh, geq, pen, m1, m2, top = (narrow(5, G, 0), narrow(5, G, 1), narrow(5, G, 2), narrow(5, 1, 16), narrow(5, 1, 20), narrow(5, 1, 24))
            den, m0 = narrow(5, 1, 28), narrow(5, 1, 30)
            rankg = cst[:, C_RANK:C_RANK + G].unsqueeze(1).broadcast_to([P, NT, G])
            ranke = cst[:, C_RANK + G:C_RANK + G + E].unsqueeze(1).broadcast_to([P, NT, E])

            def over(v, n):
                return v.broadcast_to([P, NT, n])

            def step(ins):
                dve.drain()

            def first_best(out, v, hit, best, rank, n):
                step(dve.tensor_reduce(best, v, AX.X, ALU.max))
                step(dve.tensor_tensor(hit, v, over(best, n), ALU.is_equal))
                step(dve.tensor_tensor(hit, hit, rank, ALU.mult))
                step(dve.tensor_reduce(top, hit, AX.X, ALU.max))
                step(dve.tensor_tensor(out, hit, over(top, n), ALU.is_equal))

            first_best(goh, Lg, geq, m0, rankg, G)
            step(dve.tensor_scalar(pen, goh, 1e30, -1e30, ALU.mult, ALU.add))
            for g in range(G):
                part_ = slice(g * EG, (g + 1) * EG)
                dve.tensor_tensor(em[:, :, part_], Le[:, :, part_], pen[:, :, g:g + 1].broadcast_to([P, NT, EG]), ALU.add)
            dve.drain()
            first_best(oh1, em, eq, m1, ranke, E)
            step(dve.scalar_tensor_tensor(em, oh1, -2e30, em, ALU.mult, ALU.add))
            first_best(oh2, em, eq, m2, ranke, E)
            dve.tensor_tensor(maskb[:], oh1, oh2, ALU.add).then_inc(mask_ready, 1)
            for c, hit in enumerate((oh1, oh2)):
                high = cst[:, C_HI + c * NT:C_HI + (c + 1) * NT].unsqueeze(2).broadcast_to([P, NT, E])
                dve.tensor_tensor(number[:, c, :, 0, :], hit, high, ALU.mult)
                dve.tensor_scalar(number[:, c, :, 1, :], hit, cst[:, C_LO:C_LO + 1], None, ALU.mult)
            dve.tensor_tensor(rt_e[:, :, 0:G], Lg, over(m0, G), ALU.subtract)
            dve.tensor_tensor(rt_e[:, :, G:G + 1], m2, m1, ALU.subtract).then_inc(rgmax, 1)
            landed(dve, "pos")
            dve.tensor_copy(rt[:, 6, 0:E], pp("pos")[:, 512:512 + E])
            step(free(dve.tensor_copy(pos.rearrange("p t e -> p (t e)"), pp("pos")[:, 0:NT * E]), "pos"))
            at = rt[:, 7, 0:2 * NT].rearrange("p (c t) -> p c t", c=2)
            base = rt[:, 7, 16:16 + 2 * NT].rearrange("p (c t) -> p c t", c=2)
            rnd = rt[:, 7, 32:32 + 2 * NT].rearrange("p (c t) -> p c t", c=2)
            rnd_i = idx_r[:, 0:2 * NT].rearrange("p (c t) -> p c t", c=2)
            table = cst[:, C_IDB:C_IDB + E].unsqueeze(1).broadcast_to([P, NT, E])
            dve.tensor_tensor(eq, oh1, pos, ALU.mult)
            step(dve.tensor_tensor(em, oh2, pos, ALU.mult))
            for c, a in enumerate((eq, em)):
                last = dve.tensor_reduce(at[:, c, :].unsqueeze(2), a, AX.X, ALU.add)
            step(last)
            for c in range(2):
                last = dve.tensor_tensor(place1[:, c], cst[:, C_IOTA:C_IOTA + ROWS].unsqueeze(1).broadcast_to([P, NT, ROWS]),
                                         at[:, c, :].unsqueeze(2).broadcast_to([P, NT, ROWS]), ALU.is_equal)
            last.then_inc(place_ready, 1)
            dve.tensor_tensor(wide(8), oh1, table, ALU.mult)
            step(dve.tensor_tensor(wide(9), oh2, table, ALU.mult))
            for c in range(2):
                dve.tensor_reduce(base[:, c, :].unsqueeze(2), wide(8 + c), AX.X, ALU.add)
            step(dve.tensor_copy(rnd_i, at))
            dve.tensor_scalar(rnd_i, rnd_i, ROWS.bit_length() - 1, None, ALU.arith_shift_right)
            step(dve.scalar_tensor_tensor(base, at, float(PAIRS), base, ALU.mult, ALU.add))
            landed(dve, "table")
            got = rt[:, 10, 0:3 * PAIRS].rearrange("p (n q) -> p n q", n=3)
            step(dve.tensor_copy(got[:, 1:3, :].rearrange("p n q -> p (n q)"), pp("table")[:, 0:2 * PAIRS]))
            step(dve.scalar_tensor_tensor(got[:, 0, :], got[:, 1, :], 32.0, got[:, 2, :], ALU.mult, ALU.add))
            free(dve.tensor_scalar(got[:, 0, :], got[:, 0, :], float(PAD), None, ALU.add), "table")
            dve.drain()
            dve.tensor_scalar(got[:, 1, :], got[:, 0, :], float(T), float(-T), ALU.is_ge, ALU.mult)
            step(dve.tensor_copy(ids[:, 0, :], got[:, 0, :]))
            dve.tensor_tensor(idg[:, 0, :], got[:, 0, :], got[:, 1, :], ALU.add).then_inc(table_ready, 1)
            step(dve.tensor_copy(rnd, rnd_i))
            step(dve.scalar_tensor_tensor(base, rnd, float(PAIRS * (P - ROWS)), base, ALU.mult, ALU.add))
            dve.tensor_copy(slot_i[:], base).then_inc(idx_ready, 1)
            cnt = rt[0:1, 6, 0:E].rearrange("p (q j) -> p q j", j=2)
            big = rt[0:1, 6, E:E + PAIRS]
            step(dve.tensor_reduce(big.unsqueeze(2), cnt, AX.X, ALU.max))
            step(dve.tensor_scalar(big, big, 1.0, -1.0, ALU.max, ALU.add))
            step(dve.tensor_copy(extra[:, 0:PAIRS], big))
            step(dve.tensor_scalar(extra[:, 0:PAIRS], extra[:, 0:PAIRS], ROWS.bit_length() - 1, None, ALU.arith_shift_right))
            runs = [rt[0:1, 8, 2 * n * PAIRS:2 * (n + 1) * PAIRS] for n in range(2)]
            dve.memset(rt[0:1, 8, 0:4 * PAIRS], 0.0)
            step(None)
            step(dve.tensor_copy(runs[0][:, PAIRS:], extra[:, 0:PAIRS]))
            for n in range(PAIRS.bit_length() - 1):
                a, b = runs[n % 2], runs[1 - n % 2]
                step(dve.tensor_tensor(b[:, PAIRS:], a[:, PAIRS:], a[:, PAIRS - 2 ** n:2 * PAIRS - 2 ** n], ALU.add))
            dve.tensor_copy(extra[:, PAIRS:], runs[0][:, PAIRS - 1:2 * PAIRS - 1]).then_inc(cnt_ready, 1)
            dve.wait_ge(rexp, 1)
            dve.tensor_reduce(den, rt_e[:, :, 0:G], AX.X, ALU.add)
            step(dve.tensor_scalar(m1, rt_e[:, :, G:G + 1], 1.0, None, ALU.add))
            step(dve.tensor_tensor(den, den, m1, ALU.mult))
            step(dve.reciprocal(wsel[:, 0, :].unsqueeze(2), den))
            dve.tensor_tensor(wsel[:, 1, :].unsqueeze(2), rt_e[:, :, G:G + 1], wsel[:, 0, :].unsqueeze(2), ALU.mult)
            dve.drain().then_inc(wsel_ready, 1)

            def expert_pair(pair, s, stored):
                dve.wait_ge(e_silu, pair + 1)
                dve.tensor_tensor(he[:, s, :], he[:, s, :], ps[:, s, FE:2 * FE], ALU.mult).then_inc(e_h, 1)
                dve.wait_ge(e_y, pair + 1)
                if not isinstance(stored, int) or stored > 0:
                    dve.wait_ge(y_st[s], stored)
                    dve.wait_ge(r_pair, pair - 1)
                dve.tensor_copy(ys[:, s, :], ps[:, 2 + 2 * s:4 + 2 * s, :].rearrange("p a b -> p (a b)")).then_inc(e_ys, 1)
                n = dve.value_load(extra[0:1, bass.ds(pair, 1)], min_val=0, max_val=ROUNDS - 1)
                with dve.If(n > 0):
                    before = dve.value_load(extra[0:1, bass.ds(pair + PAIRS, 1)], min_val=0, max_val=PAIRS * (ROUNDS - 1))
                    with dve.Fori(1, n + 1) as r:
                        at = dve.snap(before + r)
                        dve.wait_ge(r_silu, at)
                        dve.tensor_tensor(he[:, s, :], he[:, s, :], ps[:, s, FE:2 * FE], ALU.mult).then_inc(r_h, 1)
                        dve.wait_ge(r_y, at)
                        dve.wait_ge(y_st[s], stored + 16)
                        dve.wait_ge(r_st, at)
                        dve.tensor_copy(ys[:, s, :], ps[:, 2 + 2 * s:4 + 2 * s, :].rearrange("p a b -> p (a b)")).then_inc(r_ys, 1)

            dve.sem_inc(r_ys, 1)
            for pair in range(3):
                expert_pair(pair, pair % 2, 16 * (pair // 2))
            with dve.Fori(0, LOOPED) as turn2:
                for s in range(2):
                    expert_pair(2 * turn2 + 3 + s, 1 - s, 16 * turn2 + 16 * (1 + s))
            for pair in range(PAIRS - 3, PAIRS):
                expert_pair(pair, pair % 2, 16 * (pair // 2))
            dve.wait_ge(gg2_in, 32)
            for b in range(NT + 1):
                if b < NT:
                    dve.wait_ge(f_first, b + 1)
                    dve.scalar_tensor_tensor(yg[:, 1, b, :], yg[:, 1, b, :], wsel[:, 1, b:b + 1], yg[:, 0, b, :], ALU.mult, ALU.add)\
                        .then_inc(f_mix, 1)
                if b:
                    n = b - 1
                    dve.wait_ge(f_ss, n + 1)
                    dve.tensor_scalar(stat[:, 4, n:n + 1], stat[:, 3, n:n + 1], 1.0 / D, EPS, ALU.mult, ALU.add).then_inc(f_var, 1)
                    dve.wait_ge(f_sd, n + 1)
                    dve.reciprocal(stat[:, 5, n:n + 1], stat[:, 5, n:n + 1])
                    dve.drain()
                    if n >= 2:
                        dve.wait_ge(f_out[0], n - 1)
                    ins = dve.scalar_tensor_tensor(yo[:, n % 2, :], yg[:, 1, n, :], stat[:, 5, n:n + 1], gg2[:, min(n, 1), :], ALU.mult, ALU.mult)
                    if n < NT - 1:
                        ins.then_inc(f_norm, 1)
                    else:
                        dve.drain()
                        dve.tensor_tensor(x[:, n, :], x[:, n, :], yo[:, n % 2, :], ALU.add).then_inc(f_out[1], 1)

        @block.tensor
        def _(pe):
            mm = nc.tensor.matmul

            def both(name, lhs, rhs_s, rhs_p, steps, width=TP):
                begin(pe, name)
                for k in range(steps):
                    mm(pp(name)[:, 0:TS], lhs(k), rhs_s(k), start=k == 0, stop=k == steps - 1)
                    last = mm(pp(name)[:, 512:512 + width], lhs(k), rhs_p(k), start=k == 0, stop=k == steps - 1)
                done(last, name)

            def turn(out, in_, n=P):
                return nc.tensor.transpose(out, in_, ident[0:n, 0:n])

            pe.wait_ge(cst_in, 16)
            def ada(n):
                name = f"ada{n}"
                begin(pe, name)
                for c in range(ADA[n][0], sum(ADA[n])):
                    chunk, arrived, loads = chunk_place(c)
                    pe.wait_ge(arrived, 16 * loads)
                    at = (c - ADA[n][0]) * P
                    for k in range(KD):
                        for j in range(4):
                            last = mm(pp(name)[32 * j:32 * j + 32, at:at + P], csT[:, k, :], chunk[:, k, j * P:(j + 1) * P],
                                      start=k == 0, stop=k == KD - 1)
                    if c < sum(ADA[n]) - 1:
                        last.then_inc(ada_used, 1)
                done(last, name)
                pe.drain().then_inc(ada_used, 1)

            pe.wait_ge(xn_ready, 1)
            for k in range(KD):
                name = f"tr{k}"
                begin(pe, name)
                for b in range(1, NT):
                    turn(pp(name)[:, (b - 1) * P:b * P], xn[:, b, k * P:(k + 1) * P])
                done(turn(pp(name)[:, 512:512 + TP], xn[:, 0, k * P:(k + 1) * P]), name)
            pe.wait_ge(cs_ready, 1)
            ada(0)
            begin(pe, "modt")
            pe.wait_ge(rows_ready, 1)
            for n in range(4):
                last = turn(pp("modt")[:, n * P:(n + 1) * P], rows[:, n, :])
            done(last, "modt")
            begin(pe, "vt")
            pe.wait_ge(vec_in, 16 * 6)
            for m in range(CM):
                turn(pp("vt")[:, m * TAPS:(m + 1) * TAPS], wdrow[:, m * P:(m + 1) * P], TAPS)
            done(turn(pp("vt")[:, 512:512 + 17], vrow, 17), "vt")

            def project(name, lhs):
                def columns(k):
                    if name == "g0":
                        pe.wait_ge(hT_dve if k % 2 else hT_act, k // 2 + 1)
                    return hT[:, k, TP:]

                both(name, lhs, columns, lambda k: hT[:, k, 0:TP], KD)

            for m in range(CM):
                pe.wait_ge(wc_in[m], 32)
                project(f"g{m}", lambda k: wC[:, k, C + m * P:C + (m + 1) * P])
                project(f"a{m}", lambda k: wC[:, k, m * P:(m + 1) * P])
                ada(m + 1)
            pe.wait_ge(wq_in, 16)

            def square_sum(name, first, count, src):
                begin(pe, name)
                for n in range(first, first + count):
                    mm(pp(name)[:, 0:TS], ones[:], src(n, 1), start=n == first, stop=n == first + count - 1)
                    last = mm(pp(name)[:, 512:512 + TP], ones[:], src(n, 0), start=n == first, stop=n == first + count - 1)
                done(last, name)

            def sq_part(n, sample):
                return sq[:, n, TP:] if sample else sq[:, n, 0:TP]

            def low_rank(n, name):
                project(name, lambda k: wQ[:, k, n * P:(n + 1) * P])

            for n, name in enumerate(("q0", "q1", "q2", "kv0")):
                low_rank(n, name)
            pe.wait_ge(qsum_ready, 1)
            square_sum("stq", 0, 1, sq_part)
            low_rank(4, "kv1")
            pe.wait_ge(wkr_ready, 1)
            project("kr", lambda k: wkr[:, k, :])
            pe.wait_ge(csum_ready, 1)
            square_sum("lnm", 0, 1, lambda n, s: csum[:, 0, SAMP0:] if s else csum[:, 0, 0:TP])
            pe.wait_ge(sq_ready, QM + KM)
            square_sum("stkv", QM, KM, sq_part)
            pe.wait_ge(cache_in, 48)
            begin(pe, "cache")
            turn(pp("cache")[:, 0:P], ckr)
            for m in range(KM):
                last = turn(pp("cache")[:, (1 + m) * P:(2 + m) * P], cckv[:, m * P:(m + 1) * P])
            done(last, "cache")
            emptied(pe, "kr")
            both("krdup", lambda k: dup, lambda k: tk[:, TP:], lambda k: tk[:, 0:TP], 1)
            pe.wait_ge(qn_ready, 1)
            pe.wait_ge(wuq_in, 16)
            pe.wait_ge(wqr_ready, 1)
            for h in range(H):
                for name, lhs in ((f"qn{h}", lambda k: wuq[:, k, h * (DN + DR):h * (DN + DR) + DN]),
                                  (f"qr{h}", lambda k: wqr[:, k * H + h, :])):
                    both(name, lhs, lambda k: qa[:, k, TP:], lambda k: qa[:, k, 0:TP], QM)
                if h == 1:
                    pe.wait_ge(csum_ready, 2)
                    square_sum("lnv", 0, 1, lambda n, s: csum[:, 0, TP:T] if s else csum[:, 0, 0:TP])
            pe.wait_ge(ckn_ready, 1)
            begin(pe, "state")
            for m in range(KM):
                turn(pp("state")[:, m * P:(m + 1) * P], ck[:, m, 0:TP])
            done(turn(pp("state")[:, KVL:KVL + DR], tk[0:DR, 0:TP], DR), "state")
            pe.wait_ge(cachekv_ready, 1)
            pe.wait_ge(wukv_in, 16)
            for h in range(H):
                both(f"k{h}", lambda k: wukv[:, k, h * (DN + DV):h * (DN + DV) + DN],
                     lambda k: ck[:, k, TP + PAST:], lambda k: ck[:, k, 0:TP + PAST], KM, TP + PAST)
            for t in range(KT):
                name = f"v{t}"
                begin(pe, name)
                for k in range(KM):
                    last = mm(pp(name)[:, 0:512], ck[:, k, t * P:(t + 1) * P],
                              wukv[:, k, :].rearrange("p (h c) -> p h c", h=H)[:, :, DN:], start=k == 0, stop=k == KM - 1)
                done(last, name)
            pe.wait_ge(proj_act, 1)
            pe.wait_ge(proj_dve, 1)
            for u in range(UNITS + LAG + 1):
                for name in unit_groups(u):
                    kind, n = name[0], int(name[1:])
                    h, q = divmod(n, NT)
                    g = pp(name)
                    begin(pe, name)
                    if kind == "S":
                        if q < 4:
                            cols, first = slice(TP + q * P, TP + (q + 1) * P), TP
                            parts = ((0, 512), (512, T))
                        else:
                            cols, first, parts = slice(0, TP), 0, ((0, TP),)
                        for m, a in enumerate((qn, qr)):
                            for lo, hi in parts:
                                keys = kn[:, h, first + lo:first + hi] if m == 0 else kr[:, first + lo:first + hi]
                                last = mm(g[:, lo:hi], a[:, h, cols], keys, start=m == 0, stop=m == 1)
                    elif kind == "T":
                        pe.wait_ge(p_ready, n + 1)
                        for t in range(5 if q < 4 else 1):
                            last = turn(g[:, t * P:(t + 1) * P], pr[:, n % (LAG + 1), t * P:(t + 1) * P])
                    else:
                        for m in range(n * NT, (n + 1) * NT):
                            emptied(pe, f"T{m}")
                        for t in range(5):
                            mm(g[:, 0:TS], vv[:, 1 + t, n * DV:(n + 1) * DV], pT[:, t, :], start=t == 0, stop=t == 4)
                        last = mm(g[:, 512:512 + TP], vv[:, 0, n * DV:(n + 1) * DV], pTp, start=True, stop=True)
                    done(last, name)
            pe.wait_ge(wo_in, 16)
            pe.wait_ge(wr_ready, 1)
            for name in POST:
                kind, b = name[:-1], int(name[-1])
                begin(pe, name)
                if kind == "P":
                    if b == 0:
                        for h in range(H):
                            emptied(pe, f"O{h}")
                    for k in (*range(CM, KD), *range(CM)):
                        if b == 0 and k == 0:
                            pe.wait_ge(mixc_ready, CM)
                        for half in range(2):
                            last = mm(pp(name)[:, half * 512:(half + 1) * 512], mixT[:, k, b * P:(b + 1) * P],
                                      wo[:, k, half * 512:(half + 1) * 512], start=k == CM, stop=k == CM - 1)
                elif kind == "ht":
                    if b < NT - 1:
                        pe.wait_ge(h2_ready, b + 1)
                    else:
                        pe.wait_ge(h2_last, 1)
                    for k in range(KD):
                        last = turn(pp(name)[:, k * P:(k + 1) * P], h2[:, b % 2, k::KD])
                elif kind == "rt":
                    emptied(pe, f"ht{b}")
                    for k in range(KD):
                        last = mm(pp(name)[0:G + E, 0:P], wr[:, k, :], h2T[b % 2][:, k, :], start=k == 0, stop=k == KD - 1)
                else:
                    emptied(pe, f"rt{b}")
                    last = turn(pp(name)[:, 0:G + E], lg, G + E)
                done(last, name)
            begin(pe, "pos")
            pe.wait_ge(mask_ready, 1)
            pe.wait_ge(small_ready, 1)
            for b in range(NT):
                for a in range(b + 1):
                    mm(pp("pos")[:, b * E:(b + 1) * E], trib[:] if a == b else onesb[:], maskb[:, a, :], start=a == 0, stop=a == b)
            for a in range(NT):
                last = mm(pp("pos")[:, 512:512 + E], onesb[:], maskb[:, a, :], start=a == 0, stop=a == NT - 1)
            done(last, "pos")
            begin(pe, "table")
            pe.wait_ge(place_ready, 1)
            for c in range(2):
                for b in range(NT):
                    for j in range(2):
                        last = mm(pp("table")[j * ROWS:(j + 1) * ROWS, 0:2 * PAIRS], place1[:, c, b, :], number[:, c, b, :, j::2],
                                  start=c == b == 0, stop=c == 1 and b == NT - 1)
            done(last, "table")

            for s in range(4):
                n = sum(1 for name in order if place[name][0] == s)
                pe.wait_ge(drained[s], n)

            def rows_to_columns(src, inc):
                for k in range(KD):
                    last = turn(ps[:, 6 + k // 4, (k % 4) * P:(k % 4 + 1) * P], src[:, k::KD])
                last.then_inc(inc, 1)

            def gate_up(s, w, src, inc):
                for k in range(KD):
                    for j in range(2):
                        a = j * ROWS
                        last = mm(ps[a:a + ROWS, s, :], src[:, k, a:a + ROWS], slots[w][:, j, 0:2, k * FE:(k + 1) * FE], start=k == 0, stop=k == KD - 1)
                last.then_inc(inc, 1)

            def hidden_to_columns(s, src, inc):
                for k in range(KF):
                    last = turn(ps[:, s, k * P:(k + 1) * P], src[:, k::KF])
                last.then_inc(inc, 1)

            def down(s, w, src, inc):
                for k in range(KF):
                    for half in range(2):
                        for j in range(2):
                            a = j * ROWS
                            last = mm(ps[a:a + ROWS, 2 + 2 * s + half, :], src[:, k, a:a + ROWS],
                                      slots[w][:, j, 2, k * D + half * 512:k * D + (half + 1) * 512], start=k == 0, stop=k == KF - 1)
                last.then_inc(inc, 1)

            def expert_pair(pair, s, w, loaded, gathered, last=False):
                for j in range(2):
                    pe.wait_ge(w_in_s[w][j], loaded)
                pe.wait_ge(e_xT, pair + 1)
                gate_up(s, w, xT[:, s], e_gu)
                if not last:
                    pe.wait_ge(xg_in[1 - s], gathered)
                    rows_to_columns(xg[:, 1 - s, :], e_tr)
                pe.wait_ge(e_h, pair + 1)
                hidden_to_columns(s, he[:, s, :], e_ht)
                pe.wait_ge(e_hT, pair + 1)
                wait_from(pe, e_ys, pair)
                down(s, w, heT[:, s], e_y)
                n = pe.value_load(extra[0:1, bass.ds(pair, 1)], min_val=0, max_val=ROUNDS - 1)
                with pe.If(n > 0):
                    before = pe.value_load(extra[0:1, bass.ds(pair + PAIRS, 1)], min_val=0, max_val=PAIRS * (ROUNDS - 1))
                    with pe.Fori(1, n + 1) as r:
                        at = pe.snap(before + r)
                        pe.wait_ge(r_xg, at)
                        pe.wait_ge(e_xT, next_pair(pair) + 1)
                        rows_to_columns(xg[:, 1 - s, :], r_tr)
                        pe.wait_ge(r_xT, at)
                        gate_up(s, w, xT[:, s], r_gu)
                        pe.wait_ge(r_h, at)
                        hidden_to_columns(s, he[:, s, :], r_ht)
                        pe.wait_ge(r_hT, at)
                        pe.wait_ge(e_ys, pair + 1)
                        pe.wait_ge(r_ys, at)
                        down(s, w, heT[:, s], r_y)
                pe.drain().then_inc(w_used, 1)

            pe.wait_ge(xg_in[0], 16)
            rows_to_columns(xg[:, 0, :], e_tr)
            pe.wait_ge(cnt_ready, 1)
            expert_pair(0, 0, 0, 48, 16)
            expert_pair(1, 1, 1, 48, 32)
            expert_pair(2, 0, 2, 48, 32)
            with pe.Fori(0, LOOPED) as turn2:
                expert_pair(2 * turn2 + 3, 1, 1, 48 * turn2 + 96, 16 * turn2 + 48)
                expert_pair(2 * turn2 + 4, 0, 2, 48 * turn2 + 96, 16 * turn2 + 48)
            for pair, w, loads in ((PAIRS - 3, 0, 2), (PAIRS - 2, 1, LOOPED + 2), (PAIRS - 1, 2, LOOPED + 2)):
                expert_pair(pair, pair % 2, w, 48 * loads, 16 * ((pair + 1) // 2 + 1), last=pair == PAIRS - 1)


_INS = ["x_prompt", "x_sample", "cache_ckv", "cache_krope", "c", "c_ctx", "w_ada", "b_ada", "g_pre1", "g_post1",
        "g_pre2", "g_post2", "w_in", "w_dw", "b_dw", "conv_ln_g", "conv_ln_b", "q_norm_g", "kv_norm_g", "w_uq",
        "w_ukv", "w_out", "w_rg", "b_rg", "w_re", "b_re", "w_gate", "w_up", "w_down"]
_OUTS = [(1, TP, D), (1, TS, D), (1, 1, TP, KVL), (1, 1, TP, DR)]


def kernel(**inputs):
    import concourse.bacc as _bacc
    from concourse.bass_utils import run_bass_kernel_spmd as _run

    nc = _bacc.Bacc("TRN2", target_bir_lowering=False, num_devices=1)
    arrays, ins = {}, {}
    for name in _INS:
        arrays[f"in_{name}"] = np.ascontiguousarray(inputs[name])
    arrays["in_consts"] = constants()
    for name, a in arrays.items():
        ins[name[3:]] = nc.dram_tensor(name, a.shape, F32, kind="ExternalInput").ap()
    outs = [nc.dram_tensor(f"out_{n}", shape, F32, kind="ExternalOutput").ap() for n, shape in enumerate(_OUTS)]
    hybrid_layer(nc, ins, outs)
    r = _run(nc, [arrays], core_ids=[0])
    return tuple(r.results[0][f"out_{n}"] for n in range(len(_OUTS)))
```
